# Optimizing a Trainium2 kernel written in Bass

```python
import jax
import jax.numpy as jnp
from jax import lax
import numpy as np

D_MODEL = 1024
BATCH = 1
SEQ = 512
DEPTH = 1

CHUNK = 128
SGU_HEADS = 8
SGU_HEAD_DIM = D_MODEL // SGU_HEADS
SGU_WIDTH = SGU_HEADS * SGU_HEAD_DIM
POOL_WINDOWS = (2, 4, 8, 16)
POOL_GROUPS = len(POOL_WINDOWS)
POOL_WIDTH = D_MODEL
POOL_GROUP_DIM = POOL_WIDTH // POOL_GROUPS
N_BRANCHES = 2
SPLIT_SGU = 2 * SGU_WIDTH
SPLIT_POOL = SPLIT_SGU + POOL_WIDTH
IN_WIDTH = SPLIT_POOL + N_BRANCHES * D_MODEL
N_EXPERTS = 16
N_EXPERT_GROUPS = 4
EXPERTS_PER_GROUP = N_EXPERTS // N_EXPERT_GROUPS
TOP_K = 2
D_EXPERT = D_MODEL // 2
N_MOD = 6
EPS = 1e-6

kernel_name = 'hybrid_sgu_pool_grouped_moe_adaln'

def rmsnorm(x, g):
    xf = x.astype(jnp.float32)
    y = xf * lax.rsqrt(jnp.mean(xf * xf, axis=-1, keepdims=True) + EPS)
    return (y * g.astype(jnp.float32)).astype(x.dtype)

def layernorm(x, g):
    xf = x.astype(jnp.float32)
    xc = xf - jnp.mean(xf, axis=-1, keepdims=True)
    y = xc * lax.rsqrt(jnp.mean(xc * xc, axis=-1, keepdims=True) + EPS)
    return (y * g.astype(jnp.float32)).astype(x.dtype)

def modulate(h, shift, scale):
    return h * (1 + scale[:, None, :]) + shift[:, None, :]

def spatial_gating(z, v_g, w_s, b_s):
    u, v = jnp.split(z, 2, axis=-1)
    v = layernorm(v, v_g)
    B, S, _ = v.shape
    n_chunks = S // CHUNK
    v = v.reshape(B, n_chunks, CHUNK, SGU_HEADS, SGU_HEAD_DIM)
    causal = jnp.tril(jnp.ones((CHUNK, CHUNK), dtype=bool))
    w = jnp.where(causal[None], w_s, jnp.zeros((), w_s.dtype))
    s = jnp.einsum('hij,bnjhc->bnihc', w, v)
    s = s + jnp.swapaxes(b_s, 0, 1)[None, None, :, :, None]
    return u * s.reshape(B, S, SGU_WIDTH)

def multiscale_pool(p, w_pool, pool_scale):
    B, S, _ = p.shape
    pf = p.astype(jnp.float32)
    cs0 = jnp.pad(jnp.cumsum(pf, axis=1), ((0, 0), (1, 0), (0, 0)))
    pos = jnp.arange(1, S + 1)
    outs = []
    for gi, w in enumerate(POOL_WINDOWS):
        lo, hi = gi * POOL_GROUP_DIM, (gi + 1) * POOL_GROUP_DIM
        c_g = cs0[:, :, lo:hi]
        lagged = jnp.pad(c_g[:, :S - w + 1], ((0, 0), (w - 1, 0), (0, 0)))
        count = jnp.minimum(pos, w).astype(jnp.float32)[None, :, None]
        outs.append((c_g[:, 1:] - lagged) / count - pf[:, :, lo:hi])
    pooled = jnp.stack(outs, axis=2).astype(p.dtype)
    mixed = jnp.einsum('bsgc,gcd->bsgd', pooled, w_pool)
    return mixed.reshape(B, S, POOL_WIDTH) * pool_scale

def grouped_moe(h, router_w, router_bias, w_gate, w_up, w_down):
    B, S, D = h.shape
    t = h.reshape(-1, D)
    logits = jnp.dot(t.astype(jnp.float32), router_w.astype(jnp.float32))
    probs = jax.nn.softmax(logits, axis=-1)
    sel = (probs + router_bias.astype(jnp.float32)).reshape(-1, N_EXPERT_GROUPS, EXPERTS_PER_GROUP)
    group_score = jnp.sum(lax.top_k(sel, TOP_K)[0], axis=-1)
    g_idx = jnp.argmax(group_score, axis=-1)
    in_group = jnp.take_along_axis(sel, g_idx[:, None, None], axis=1)[:, 0]
    _, loc = lax.top_k(in_group, TOP_K)
    e_idx = g_idx[:, None] * EXPERTS_PER_GROUP + loc
    wts = jnp.take_along_axis(probs, e_idx, axis=1)
    wts = wts / jnp.sum(wts, axis=-1, keepdims=True)
    combine = jnp.einsum('tk,tke->te', wts,
                         jax.nn.one_hot(e_idx, N_EXPERTS, dtype=jnp.float32)).astype(h.dtype)
    g = jnp.einsum('td,edf->tef', t, w_gate)
    u = jnp.einsum('td,edf->tef', t, w_up)
    a = jax.nn.silu(g) * u * combine[:, :, None]
    y = jnp.einsum('tef,efd->td', a, w_down)
    return y.reshape(B, S, D)

def setup_inputs(seed: int = 0) -> dict:
    key = jax.random.key(seed)
    ks = jax.random.split(key, 24)
    f32 = jnp.float32
    nrm = lambda k, shape, s: jax.random.normal(k, shape, f32) * s
    L, D = DEPTH, D_MODEL
    return {
        'x': nrm(ks[0], (BATCH, SEQ, D), 1.0),
        'c': nrm(ks[1], (BATCH, D), 1.0),
        'w_ada': nrm(ks[2], (L, D, N_MOD * D), 0.5 * D ** -0.5),
        'b_ada': nrm(ks[3], (L, N_MOD * D), 0.02),
        'norm_mix_g': 1.0 + nrm(ks[4], (L, D), 0.02),
        'w_in': nrm(ks[5], (L, D, IN_WIDTH), D ** -0.5),
        'v_norm_g': 1.0 + nrm(ks[6], (L, SGU_WIDTH), 0.02),
        'sgu_w': nrm(ks[7], (L, SGU_HEADS, CHUNK, CHUNK), CHUNK ** -0.5),
        'sgu_b': 1.0 + nrm(ks[8], (L, SGU_HEADS, CHUNK), 0.1),
        'pool_w': nrm(ks[9], (L, POOL_GROUPS, POOL_GROUP_DIM, POOL_GROUP_DIM), POOL_GROUP_DIM ** -0.5),
        'pool_scale': 1.0 + nrm(ks[10], (L, POOL_WIDTH), 0.1),
        'w_branch_a': nrm(ks[11], (L, SGU_WIDTH, D), SGU_WIDTH ** -0.5),
        'w_branch_b': nrm(ks[12], (L, POOL_WIDTH, D), POOL_WIDTH ** -0.5),
        'w_out': nrm(ks[13], (L, D, D), D ** -0.5),
        'norm_ffn_g': 1.0 + nrm(ks[14], (L, D), 0.02),
        'router_w': nrm(ks[15], (D, N_EXPERTS), D ** -0.5),
        'router_bias': nrm(ks[16], (N_EXPERTS,), 0.01),
        'w_exp_gate': nrm(ks[17], (L, N_EXPERTS, D, D_EXPERT), D ** -0.5),
        'w_exp_up': nrm(ks[18], (L, N_EXPERTS, D, D_EXPERT), D ** -0.5),
        'w_exp_down': nrm(ks[19], (L, N_EXPERTS, D_EXPERT, D), D_EXPERT ** -0.5),
        'final_norm_g': 1.0 + nrm(ks[20], (D,), 0.02),
    }

def reference(x, c, w_ada, b_ada, norm_mix_g, w_in, v_norm_g, sgu_w, sgu_b, pool_w, pool_scale,
              w_branch_a, w_branch_b, w_out, norm_ffn_g, router_w, router_bias,
              w_exp_gate, w_exp_up, w_exp_down, final_norm_g):
    c_act = jax.nn.silu(c)
    for l in range(DEPTH):
        mod = jnp.dot(c_act, w_ada[l]) + b_ada[l]
        sh_m, sc_m, g_m, sh_f, sc_f, g_f = jnp.split(mod, N_MOD, axis=-1)
        h = modulate(rmsnorm(x, norm_mix_g[l]), sh_m, sc_m)
        z = jnp.einsum('bsd,de->bse', h, w_in[l])
        z_sgu, z_pool, z_gate = jnp.split(z, [SPLIT_SGU, SPLIT_POOL], axis=-1)
        y_a = spatial_gating(jax.nn.gelu(z_sgu), v_norm_g[l], sgu_w[l], sgu_b[l])
        y_b = multiscale_pool(z_pool, pool_w[l], pool_scale[l])
        gates = jax.nn.sigmoid(z_gate.astype(jnp.float32)).astype(x.dtype)
        gate_a, gate_b = jnp.split(gates, N_BRANCHES, axis=-1)
        merged = (gate_a * jnp.einsum('bsc,cd->bsd', y_a, w_branch_a[l])
                  + gate_b * jnp.einsum('bsc,cd->bsd', y_b, w_branch_b[l]))
        x = x + g_m[:, None, :] * jnp.einsum('bsd,de->bse', merged, w_out[l])
        hf = modulate(rmsnorm(x, norm_ffn_g[l]), sh_f, sc_f)
        x = x + g_f[:, None, :] * grouped_moe(hf, router_w, router_bias,
                                              w_exp_gate[l], w_exp_up[l], w_exp_down[l])
    return rmsnorm(x, final_norm_g)


_drawn_inputs = setup_inputs


def setup_inputs(seed=0):
    import zlib

    import numpy as np

    out = dict(_drawn_inputs(seed))
    spreads = {}
    factors = {'norm_mix_g': 6.159,
     'v_norm_g': 17.753,
     'final_norm_g': 8.116,
     'norm_ffn_g': 8.0,
     'router_bias': 4.248}
    for name, (base, spread) in spreads.items():
        noise = np.random.default_rng([zlib.crc32(name.encode()), seed]).standard_normal(out[name].shape)
        drawn = base * np.exp(spread * noise) if base else spread * noise
        out[name] = jnp.asarray(drawn.astype(out[name].dtype))
    for name, factor in factors.items():
        out[name] = (out[name] * factor).astype(out[name].dtype)
    return out
```

```python
from contextlib import ExitStack

import concourse.bass as bass
from concourse import mybir

F32 = mybir.dt.float32
F32R = mybir.dt.float32r
I32 = mybir.dt.int32
ALU = mybir.AluOpType
ACT = mybir.ActivationFunctionType
AX_X = mybir.AxisListType.X
ds = bass.ds

P = 128
SEQ = 512
NT = SEQ // P
D = 1024
ND = D // P
NH = 8
E = 16
EG = 4
FE = D // 2
NF = FE // P
WINDOWS = (2, 4, 8, 16)
EPS = 1e-6

CH = 2048
CC = CH // ND
RING_A = 4
RING = 6

V0, U0, P0, G0, O0 = 0, 4, 8, 12, 28
M0 = 32
RAW_ADA = 8
RAW_V = RAW_ADA
RAW_G = RAW_V + G0
RAW_O = RAW_G + 32
TILES_MAX = E + 8
SKIP = 5000


def tokens_moe_kernel(nc, A, out):
    w_ada = A["w_ada"][0].rearrange("(k p) n -> p k n", p=P)
    w_in = A["w_in"][0].rearrange("(k p) n -> p k n", p=P)
    w_a = A["w_branch_a"][0].rearrange("(k p) n -> p k n", p=P)
    w_b = A["w_branch_b"][0].rearrange("(k p) n -> p k n", p=P)
    w_out = A["w_out"][0].rearrange("(k p) n -> p k n", p=P)
    w_gate = A["w_exp_gate"][0].rearrange("e (k p) f -> e p k f", p=P)
    w_up = A["w_exp_up"][0].rearrange("e (k p) f -> e p k f", p=P)
    w_down = A["w_exp_down"][0].rearrange("e (k p) n -> e p k n", p=P)
    x_rows = A["x"][0].rearrange("(t p) d -> p t d", p=P)
    out_rows = out[0].rearrange("(t p) d -> p t d", p=P)

    hf_dram = nc.dram_tensor("hf_rows", (SEQ, D), F32, kind="Internal").ap()
    y_dram = nc.dram_tensor("expert_rows", (2 * SEQ + 1, D), F32, kind="Internal").ap()
    hf_out = hf_dram.rearrange("(t p) d -> p t d", p=P)
    y_pairs = y_dram[1:2 * SEQ + 1, :].rearrange("(t p two) d -> t p (two d)", p=P, two=2)

    ctx = ExitStack()
    with ctx:
        def sb(name, shape, dt=F32):
            return ctx.enter_context(nc.sbuf_tensor(name, shape, dt))

        def sem(name):
            return ctx.enter_context(nc.semaphore(name))

        ps = ctx.enter_context(nc.psum_tensor("ps", [P, 8, 512], F32))
        raw = sb("raw", [P, RING, CH])
        wsplit = sb("wsplit", [P, RING, 2, CH], F32R)
        mx = sb("mx", [P, NT * D])
        tmp = sb("tmp", [P, 2 * D])
        ident = sb("ident", [P, P])
        ones = sb("ones", [P, P])
        before = sb("before", [P, P])
        iota1 = sb("iota1", [P, P])
        router = sb("router", [P, ND, E])
        cols = sb("cols", [P, 32])
        c_silu = sb("c_silu", [P, ND])
        mod_cols = sb("mod_cols", [P, 16])
        gain = sb("gain", [P, ND])
        stats = sb("stats", [P, 32])
        nrm = sb("nrm", [P, 2 * NT])
        inv_count = sb("inv_count", [P, 16])
        bias_row = sb("bias_row", [P, E])
        order = sb("order", [P, 2, EG, EG])
        pos1 = sb("pos1", [P, NT, E])
        info = sb("info", [P, NT, E, 3])
        base = sb("base", [P, TILES_MAX])
        expert_of = sb("expert_of", [P, 32], I32)
        row_w = sb("row_w", [P, TILES_MAX])
        row_dest = sb("row_dest", [P, TILES_MAX], I32)
        tok_idx = sb("tok_idx", [P, 1], I32)
        dest_now = sb("dest_now", [P, 1], I32)
        iota_i = sb("iota_i", [P, P], I32)
        tok_i = sb("tok_i", [P, NT], I32)
        tok_f = sb("tok_f", [P, NT])
        with nc.sbuf_tensor("hT", [P, 2, ND, SEQ], F32R) as hT:
            pass
        hgT = sb("hgT", [P, 2, ND, P], F32R)
        aT = sb("aT", [P, 2, NF, P], F32R)
        work = sb("work", [P, 5 * D])

        v = raw[:, 4:6, :].rearrange("p s c -> p (s c)")
        macc_a = raw[:, 4, :]
        macc_b = raw[:, 4:6, :].rearrange("p s c -> p (s c)")
        hf = raw[:, 4:6, :].rearrange("p s (t d) -> p (s t) d", d=D)
        shf, gff = raw[:, 0, 0:D], raw[:, 0, D:2 * D]
        ya = wsplit[:, 2:4, :, :].rearrange("p s a (b n) -> p s (a b) n", n=SEQ)
        yb = wsplit[:, 4:6, :, :].rearrange("p s a (b n) -> p s (a b) n", n=SEQ)
        wnat = tmp[:, D:2 * D]
        wsT = tmp[:, 0:D]
        bsb = tmp[:, D:2 * D]
        rows32 = raw[0:32, 5, D:D + P]
        gm = tmp[:, 0:D]
        hg = work[:, 0:D]
        y = work[:, D:2 * D]
        act_g = work[:, 2 * D:2 * D + FE]
        a_t = work[:, 2 * D + FE:3 * D]
        gf = tmp[:, D:2 * D]
        hfT = work[:, 0:2 * D].rearrange("p (b k m) -> p b k m", b=2, m=P)
        sel = work[:, 3 * D:3 * D + NT * P].rearrange("p (t m) -> p t m", t=NT)
        rt = work[:, 3 * D + NT * P:5 * D]
        gfin = work[:, 4 * D:5 * D]

        rows_in = sem("rows_in")
        x_in = [sem(f"x_in{t}") for t in range(NT)]
        wnat_in, bsb_in, router_in, ba_in, bb_in = map(sem, ("wnat_in", "bsb_in", "router_in", "ba_in", "bb_in"))
        bias_in, wpool_in, gff_in, x_again = map(sem, ("bias_in", "wpool_in", "gff_in", "x_again"))
        landed = [sem(f"landed{s}") for s in range(RING)]
        hi_ready, lo_ready, chunk_used, ada_used, ada_step = map(
            sem, ("hi_ready", "lo_ready", "chunk_used", "ada_used", "ada_step"))
        consts, pool_step, causal, cols_t, cols_ready, c_ready = map(
            sem, ("consts", "pool_step", "causal", "cols_t", "cols_ready", "c_ready"))
        macc_zero, maccb_zero = map(sem, ("macc_zero", "maccb_zero"))
        ws_t, ws_ready, squares, xhat_ready, xT_t, mod_mm, mod_ready, gain_ready = map(
            sem, ("ws_t", "ws_ready", "squares", "xhat_ready", "xT_t", "mod_mm", "mod_ready", "gain_ready"))
        h_aff, h_hi, h_lo = map(sem, ("h_aff", "h_hi", "h_lo"))
        chain = sem("chain")
        v_gelu, v_centred, v_square, v_ready, u_ready = map(
            sem, ("v_gelu", "v_centred", "v_square", "v_ready", "u_ready"))
        s_mm, ya_f, ya_hi, ya_lo = map(sem, ("s_mm", "ya_f", "ya_hi", "ya_lo"))
        zp_read, pooled_ready, mix_mm, yb_hi, yb_lo = map(
            sem, ("zp_read", "pooled_ready", "mix_mm", "yb_hi", "yb_lo"))
        gate_ready, merge_a, merge_t, merge_b, m_hi, m_lo = map(
            sem, ("gate_ready", "merge_a", "merge_t", "merge_b", "m_hi", "m_lo"))
        row_mm, row_ready, o_tile, x2_half = map(sem, ("row_mm", "row_ready", "o_tile", "x2_half"))
        sq2, hf_ready, hf_saved, hf_t, hfT_ready, logits_mm, expd, mask_ready, pos_mm, tiles_ready = map(
            sem, ("sq2", "hf_ready", "hf_saved", "hf_t", "hfT_ready", "logits_mm", "expd", "mask_ready",
                  "pos_mm", "tiles_ready"))
        sel_ready, idx_mm, idx_ready, gathered, hg_t, hg_hi, hg_lo = map(
            sem, ("sel_ready", "idx_mm", "idx_ready", "gathered", "hg_t", "hg_hi", "hg_lo"))
        silu_ready, a_ready, a_trans, aT_hi, aT_lo, y_ready, dest_ready, scattered = map(
            sem, ("silu_ready", "a_ready", "a_trans", "aT_hi", "aT_lo", "y_ready", "dest_ready", "scattered"))
        gfin_in, fin_x, fin_sq, fin_n, fin_ready, out_done = map(
            sem, ("gfin_in", "fin_x", "fin_sq", "fin_n", "fin_ready", "out_done"))
        y_in = [sem(f"y_in{t}") for t in range(NT)]

        x_tiles = mx[:, :].rearrange("p (t d) -> p t d", t=NT)
        u = mx[:, :].rearrange("p (m n) -> p m n", n=SEQ)
        merged = u
        z, win_a, win_b = (mx[:, i * (16 + SEQ):(i + 1) * (16 + SEQ)] for i in range(3))
        pooled = mx[:, 2048:4096].rearrange("p (b k n) -> p b k n", b=2, k=2)
        sig_a = tmp[:, 0:D].rearrange("p (b n) -> p b n", b=2)
        sig_b = tmp[:, D:2 * D].rearrange("p (b n) -> p b n", b=2)

        at = [0]

        def small(n):
            at[0] += n
            return rt[:, at[0] - n:at[0]]

        te_view = lambda a: a.rearrange("p (t e) -> p t e", t=NT)
        r_d, r_p, r_sel, r_top, r_m = (small(NT * E) for _ in range(5))
        r_d3, r_p3, r_sel3, r_m3 = map(te_view, (r_d, r_p, r_sel, r_m))
        r_4, r_4b, r_4c = (small(NT) for _ in range(3))
        r_gs, r_gr = small(NT * EG), small(NT * EG)
        r_ge, r_gt = (small(NT * E * EG).rearrange("p (g a b) -> p g a b", a=EG, b=EG) for _ in range(2))
        r_cnt, r_x, r_x2, r_x3, r_cum = (small(E) for _ in range(5))
        r_le = small(8 * E).rearrange("p (k e) -> p k e", k=8)
        r_8, r_8b = small(8), small(8)
        sub_ready = sem("sub_ready")

        def mix_hi(act, activation, i):
            for j in range(2):
                m = 2 * (3 - i) + j
                act.wait_ge(mix_mm, 2 * i + j + 1)
                activation(yb[:, 0, m, :], ps[:, 2 * i + j, :], ACT.Copy,
                           scale=cols[:, 24 + m:25 + m]).then_inc(yb_hi, 1)

        def mix_lo(dve, V, i):
            for j in range(2):
                m = 2 * (3 - i) + j
                dve.wait_ge(yb_hi, 2 * i + j + 1)
                V.scalar_tensor_tensor(out=yb[:, 1, m, :], in0=ps[:, 2 * i + j, :], scalar=cols[:, 24 + m:25 + m],
                                       in1=yb[:, 0, m, :].bitcast(F32), op0=ALU.mult,
                                       op1=ALU.subtract).then_inc(yb_lo, 1)

        def turned(act, activation, t):
            act.wait_ge(hf_t, t + 1)
            if t >= 2:
                act.wait_ge(logits_mm, t - 1)
            activation(hfT[:, t % 2, :, :].rearrange("p k m -> p (k m)"), ps[:, 0:2, :].rearrange("p b n -> p (b n)"),
                       ACT.Copy).then_inc(hfT_ready, 1)

        def final(dve, V, step, inv_rms, t):
            dve.wait_ge(fin_sq, t + 1)
            inv_rms(28 + t, 1)
            dve.wait_ge(gfin_in, 16)
            V.scalar_tensor_tensor(out=x_tiles[:, t, :], in0=x_tiles[:, t, :], scalar=stats[:, 28 + t:29 + t],
                                   in1=gfin, op0=ALU.mult, op1=ALU.mult).then_inc(fin_ready, 1)

        block = ctx.enter_context(nc.Block())

        def split_slot(n):
            return n % 2 if n < M0 else (n - M0 + 2) % RING

        def raw_place(n):
            r = RAW_V + n if n < G0 else (RAW_O + n - O0 if n >= O0 else None)
            return r % RING_A, 16 * (r // RING_A + 1)

        def wait_reg(engine, semaphore, value, least=1):
            if not isinstance(value, int):
                value = engine.to_reg(value)
            engine.wait_ge(semaphore, least)
            engine.wait_ge(semaphore, value)

        @block.sync
        def _(sp):
            def load(slot, src, k):
                sp.dma_start(raw[:, slot, :].rearrange("p (k n) -> p k n", k=k), src).then_inc(landed[slot], 16)

            for r in range(RAW_ADA):
                if r >= RING_A:
                    sp.wait_ge(ada_used, r - RING_A + 1)
                load(r % RING_A, w_ada[:, :, r * CC:(r + 1) * CC], ND)
            for n in range(V0, G0):
                if n < RING_A:
                    sp.wait_ge(ada_used, RING_A + n + 1)
                else:
                    sp.wait_ge(lo_ready, n - RING_A + 1)
                if n < U0:
                    half, kh = n // 2, n % 2
                    load(n % RING_A, w_in[:, 4 * kh:4 * kh + 4, D + half * 512:D + half * 512 + 512], 4)
                elif n < P0:
                    load(n % RING_A, w_in[:, :, (n - U0) * CC:(n - U0 + 1) * CC], ND)
                else:
                    g = 3 - (n - P0)
                    load(n % RING_A, w_in[:, :, 2 * D + g * CC:2 * D + (g + 1) * CC], ND)
            sp.wait_ge(s_mm, NH)
            sp.dma_start(raw[:, 4, :].rearrange("p (a n) -> p a n", n=256),
                         A["pool_w"][0].rearrange("g (k p) n -> p (g k) n", p=P)).then_inc(wpool_in, 16)
            with sp.Fori(0, 4) as q:
                for j, (w, c0) in enumerate(((w_in, 3 * D), (w_a, 0), (w_in, 4 * D), (w_b, 0))):
                    wait_reg(sp, lo_ready, q * 4 + (P0 + 1 + j))
                    wait_reg(sp, ada_used, q * 4 + (5 + j))
                    load(j, w[:, :, ds(q * CC + c0, CC)], ND)
                for j in range(4):
                    wait_reg(sp, lo_ready, q * 4 + (G0 + 1 + j))
                    load(j, w_ada[:, :, ds(q * (4 * CC) + (2 * D + j * CC), CC)], ND)
            for j in range(4):
                sp.wait_ge(ada_used, RAW_ADA + 12 + j + 1)
                half, kh = j // 2, j % 2
                load(j, w_out[:, 4 * kh:4 * kh + 4, half * 512:half * 512 + 512], 4)
            sp.wait_ge(m_lo, ND)
            sp.dma_start(mx[:, :].rearrange("p (t d) -> p t d", t=NT), x_rows).then_inc(x_again, 16)
            sp.wait_ge(lo_ready, O0 + 1)
            sp.dma_start(gff, A["norm_ffn_g"][0].partition_broadcast(P)).then_inc(gff_in, 16)
            for c in range(2):
                sp.wait_ge(lo_ready, M0 - 1 + c)
                load(c + 2, w_gate[0, :, 4 * c:4 * c + 4, :], 4)
            for t in range(NT):
                sp.wait_ge(hf_ready, t + 1)
                sp.dma_start(hf_out[:, t, :], hf[:, t, :]).then_inc(hf_saved, 16)
            sp.wait_ge(hf_saved, 16 * NT)
            sp.wait_ge(hf_t, NT)
            for c in range(2):
                load(c + 4, w_up[0, :, 4 * c:4 * c + 4, :], 4)

            def weights(i, e, e_prev):
                for c in range(RING):
                    wait_reg(sp, lo_ready, i * 6 + (30 + c - 5))
                    if c < 4:
                        w, k0, k = (w_gate if c < 2 else w_up), 4 * (c % 2), 4
                        src = w[ds(e, 1), :, k0:k0 + k, :]
                    else:
                        k0, k = 2 * (c - 4), 2
                        src = w_down[ds(e_prev, 1), :, k0:k0 + k, :]
                    load(c, src.rearrange("a p k f -> (a p) k f"), k)

            with sp.Fori(1, 14) as i:
                weights(i, i, i - 1)
            sp.wait_ge(tiles_ready, 1)
            tiles = sp.value_load(expert_of[0:1, 31:32], min_val=0, max_val=7) + E
            with sp.Fori(14, tiles) as i:
                e = sp.value_load(expert_of[0:1, ds(i, 1)], min_val=0, max_val=E - 1)
                e_prev = sp.value_load(expert_of[0:1, ds(i - 1, 1)], min_val=0, max_val=E - 1)
                weights(i, e, e_prev)
            e = sp.value_load(expert_of[0:1, ds(tiles - 1, 1)], min_val=0, max_val=E - 1)
            for c in range(2):
                wait_reg(sp, lo_ready, tiles * 6 + (29 + c))
                load(4 + c, w_down[ds(e, 1), :, 2 * c:2 * c + 2, :].rearrange("a p k f -> (a p) k f"), 2)
            sp.dma_start(gfin, A["final_norm_g"].partition_broadcast(P)).then_inc(gfin_in, 16)
            wait_reg(sp, scattered, tiles * 16)
            for t in range(NT):
                sp.dma_start(raw[:, t, :], y_pairs[t]).then_inc(y_in[t], 16)
            for t in range(NT):
                sp.wait_ge(fin_ready, t + 1)
                sp.dma_start(out_rows[:, t, :], mx[:, t * D:(t + 1) * D]).then_inc(out_done, 16)
            sp.wait_ge(out_done, 16 * NT)

        @block.gpsimd
        def _(pool):
            g = nc.gpsimd
            g.memset(ident[:, :], 0.0)
            g.memset(ones[:, :], 1.0)
            g.memset(macc_a, 0.0).then_inc(macc_zero, 1)
            g.memset(before[:, :], 1.0)
            g.memset(base[:, :], 0.0)
            g.memset(order[:, :, :, :], 1.0)
            g.iota(iota_i[:, :], pattern=[[1, P]], base=1, channel_multiplier=0)
            g.iota(tok_i[:, :], pattern=[[P, NT]], base=0, channel_multiplier=1)
            g.iota(expert_of[:, 0:E], pattern=[[1, E]], base=0, channel_multiplier=0).then_inc(pool_step, 1)
            pool.wait_ge(pool_step, 1)
            g.affine_select(out=ident[:, :], in_=ident[:, :], compare_op=ALU.not_equal, fill=1.0, base=0,
                            pattern=[[-1, P]], channel_multiplier=1).then_inc(consts, 1)
            g.affine_select(out=before[:, :], in_=before[:, :], compare_op=ALU.is_gt, fill=0.0, base=0,
                            pattern=[[1, P]], channel_multiplier=-1)
            g.affine_select(out=order[:, 0, :, :], in_=order[:, 0, :, :], compare_op=ALU.is_gt, fill=0.0, base=0,
                            pattern=[[1, EG], [-1, EG]], channel_multiplier=0)
            g.affine_select(out=order[:, 1, :, :], in_=order[:, 1, :, :], compare_op=ALU.is_gt, fill=0.0, base=0,
                            pattern=[[-1, EG], [1, EG]], channel_multiplier=0)
            g.tensor_copy(iota1[:, :], iota_i[:, :])
            g.tensor_copy(tok_f[:, :], tok_i[:, :]).then_inc(consts, 1)
            pool.wait_ge(wnat_in, 16)
            w_ihj = wnat.rearrange("p (h j) -> p h j", h=NH)
            g.affine_select(out=w_ihj, in_=w_ihj, compare_op=ALU.is_ge, fill=0.0, base=0,
                            pattern=[[0, NH], [-1, P]], channel_multiplier=1).then_inc(causal, 1)
            pool.wait_ge(mix_mm, NH)
            g.memset(macc_b, 0.0).then_inc(maccb_zero, 1)
            pool.wait_ge(maccb_zero, 1)
            pool.dma_start(macc_b[0:1, :], A["b_ada"][:, 2 * D:6 * D]).then_inc(bb_in, 16)

            def gather(j):
                wait_reg(pool, idx_ready, j + 1)
                wait_reg(pool, hg_t, j, 0)
                g.indirect_dma_start(out=hg, out_offset=None, in_=hf_dram,
                                     in_offset=bass.IndirectOffsetOnAxis(ap=tok_idx[:, 0:1], axis=0),
                                     bounds_check=SEQ - 1, oob_is_err=False).then_inc(gathered, 16)

            def scatter(j):
                wait_reg(pool, y_ready, j + 1)
                wait_reg(pool, dest_ready, j + 1)
                g.indirect_dma_start(out=y_dram, out_offset=bass.IndirectOffsetOnAxis(ap=dest_now[:, 0:1], axis=0),
                                     in_=y, in_offset=None, bounds_check=2 * SEQ,
                                     oob_is_err=False).then_inc(scattered, 16)

            pool.wait_ge(hf_saved, 16 * NT)
            pool.wait_ge(logits_mm, NT)
            for j in range(3):
                gather(j)
            scatter(0)
            gather(3)
            with pool.Fori(2, 14) as i:
                scatter(i - 1)
                gather(i + 2)
            pool.wait_ge(tiles_ready, 1)
            tiles = pool.value_load(expert_of[0:1, 31:32], min_val=0, max_val=7) + E
            with pool.Fori(14, tiles - 1) as i:
                scatter(i - 1)
                gather(i + 2)
            scatter(tiles - 2)
            scatter(tiles - 1)
            wait_reg(pool, gathered, tiles * 16 + 16)
            wait_reg(pool, scattered, tiles * 16)

        @block.scalar
        def _(act):
            A_ = nc.scalar.activation
            for i, name in enumerate(("c", "norm_mix_g", "v_norm_g", "pool_scale")):
                act.dma_start(rows32[8 * i:8 * i + 8, :],
                              A[name].rearrange("a (k p) -> (a k) p", p=P)).then_inc(rows_in, 16)
            act.dma_start(x_tiles[:, 0, :], x_rows[:, 0, :]).then_inc(x_in[0], 16)
            act.wait_ge(macc_zero, 1)
            act.dma_start(macc_a[0:1, :], A["b_ada"][:, 0:2 * D]).then_inc(ba_in, 16)
            for t in range(1, NT):
                act.dma_start(x_tiles[:, t, :], x_rows[:, t, :]).then_inc(x_in[t], 16)
            act.dma_start(wnat.rearrange("p (h j) -> p h j", h=NH),
                          A["sgu_w"][0].rearrange("h i j -> i h j")).then_inc(wnat_in, 16)
            act.dma_start(router[:, :, :], A["router_w"].rearrange("(k p) e -> p k e", p=P)).then_inc(router_in, 16)
            act.dma_start(bias_row[:, :], A["router_bias"].partition_broadcast(P)).then_inc(bias_in, 16)

            def hi(n, slot, count, used=None):
                act.wait_ge(landed[slot], count)
                if used is not None:
                    act.wait_ge(chunk_used, used)
                A_(wsplit[:, n, 0, :], raw[:, slot, :], ACT.Copy).then_inc(hi_ready, 1)

            act.wait_ge(cols_ready, 1)
            A_(c_silu[:, :], cols[:, 0:ND], ACT.Silu).then_inc(c_ready, 1)
            for t in range(NT):
                act.wait_ge(x_in[t], 16)
                if t:
                    act.wait_ge(squares, t)
                A_(raw[:, 5, 0:D], x_tiles[:, t, :], ACT.Square, accum_out=stats[:, t:t + 1]).then_inc(squares, 1)
            act.wait_ge(ws_t, 1)
            A_(wsT, ps[:, 6:8, :].rearrange("p b n -> p (b n)"), ACT.Copy).then_inc(ws_ready, 1)
            act.wait_ge(ws_ready, 1)
            act.dma_start(bsb, A["sgu_b"][0].rearrange("h i -> (h i)").partition_broadcast(P)).then_inc(bsb_in, 16)
            for n in (0, 1):
                hi(n % 2, *raw_place(n))
            for k in range(ND):
                act.wait_ge(h_aff, k + 1)
                A_(hT[:, 0, k, :], ps[:, k, :], ACT.Copy).then_inc(h_hi, 1)
            for n in range(V0, G0):
                if n >= 1:
                    s, count = raw_place(n + 1) if n + 1 < G0 else (0, 16 * (RAW_G // RING_A + 1))
                    hi((n + 1) % 2, s, count, n)
                if n < U0 and n % 2:
                    act.wait_ge(chunk_used, n + 1)
                    for t in range(NT):
                        b = 4 * (n // 2) + t
                        A_(v[:, t * D + (n // 2) * 512:t * D + (n // 2) * 512 + 512], ps[:, b, :],
                           ACT.Gelu_apprx_tanh, accum_out=stats[:, 8 + b:9 + b]).then_inc(v_gelu, 1)
                if n == U0:
                    for t in range(NT):
                        act.wait_ge(v_centred, t + 1)
                        if t:
                            act.wait_ge(v_square, t)
                        A_(wsplit[:, 2, 0, 0:D], v[:, t * D:(t + 1) * D], ACT.Square,
                           accum_out=stats[:, 20 + t:21 + t]).then_inc(v_square, 1)
                if U0 <= n < P0:
                    act.wait_ge(chunk_used, n + 1)
                    for m in range(2 * (n - U0), 2 * (n - U0) + 2):
                        if m == 0:
                            act.wait_ge(xT_t, ND)
                        A_(u[:, m, :], ps[:, m, :], ACT.Gelu_apprx_tanh).then_inc(u_ready, 1)
                if n == P0:
                    for h in range(NH):
                        act.wait_ge(ya_f, h + 1)
                        if h == 0:
                            act.wait_ge(v_square, NT)
                        A_(ya[:, 0, h, :], u[:, h, :], ACT.Copy).then_inc(ya_hi, 1)
                if n > P0 + 1:
                    mix_hi(act, A_, n - P0 - 2)
            mix_hi(act, A_, 2)
            mix_hi(act, A_, 3)
            with act.Fori(0, 4) as q:
                def hi_next(j):
                    act.wait_ge(landed[(j + 1) % 4], (q * 2 + (RAW_G // 4 + 1 + (2 if j == 3 else 0))) * 16)
                    act.wait_ge(chunk_used, q * 4 + (G0 + j))
                    A_(wsplit[:, (j + 1) % 2, 0, :], raw[:, (j + 1) % 4, :], ACT.Copy).then_inc(hi_ready, 1)

                hi_next(0)
                act.wait_ge(chunk_used, q * 4 + (G0 + 1))
                for b in range(2):
                    A_(sig_a[:, b, :], ps[:, b, :], ACT.Sigmoid).then_inc(gate_ready, 1)
                hi_next(1)
                hi_next(2)
                act.wait_ge(chunk_used, q * 4 + (G0 + 3))
                for b in range(2):
                    A_(sig_b[:, b, :], ps[:, 4 + b, :], ACT.Sigmoid).then_inc(gate_ready, 1)
                hi_next(3)
            act.wait_ge(chunk_used, G0 + 15)
            act.wait_ge(merge_b, ND)
            for k in range(ND):
                A_(hT[:, 0, k, :], merged[:, k, :], ACT.Copy).then_inc(m_hi, 1)
            for n in range(O0 + 1, O0 + 4):
                hi(n % 2, *raw_place(n), n - 1)
            for c in range(2):
                hi(c + 2, c + 2, 16 * (RAW_O // 4 + 2), G0 + 16)
            for t in range(NT):
                act.wait_ge(x2_half, NT + t + 1)
                A_(hf[:, t, :], x_tiles[:, t, :], ACT.Square, accum_out=stats[:, 24 + t:25 + t]).then_inc(sq2, 1)
                if t:
                    turned(act, A_, t - 1)
            turned(act, A_, NT - 1)
            act.wait_ge(sub_ready, 1)
            A_(r_p, r_d, ACT.Exp).then_inc(expd, 1)
            for c in range(2):
                hi(c + 4, c + 4, 16, G0 + 16)

            def rows_hi(j):
                act.wait_ge(hg_t, j + 1)
                A_(hgT[:, 0, :, :].rearrange("p k m -> p (k m)"), ps[:, 2:4, :].rearrange("p b n -> p (b n)"),
                   ACT.Copy).then_inc(hg_hi, 1)

            def silu(i, gate_used):
                act.wait_ge(chunk_used, gate_used)
                act.wait_ge(a_ready, i)
                A_(act_g, ps[:, 0, :], ACT.Silu).then_inc(silu_ready, 1)

            def results(j, used):
                act.wait_ge(chunk_used, used)
                act.wait_ge(idx_ready, j + 1)
                act.wait_ge(scattered, j * 16)
                A_(y, ps[:, 5:7, :].rearrange("p b n -> p (b n)"), ACT.Copy,
                   scale=row_w[:, ds(j, 1)]).then_inc(y_ready, 1)

            def a_hi(i):
                act.wait_ge(a_trans, i + 1)
                A_(aT[:, 0, :, :].rearrange("p k m -> p (k m)"), ps[:, 4, :], ACT.Copy).then_inc(aT_hi, 1)

            def tile(i, gate_used):
                def hi_c(c):
                    act.wait_ge(landed[c], (i + (2, 2, 3, 3, 2, 2)[c] + (13 if c < 4 else 0)) * 16)
                    act.wait_ge(chunk_used, i * 6 + (31 + c))
                    A_(wsplit[:, c, 0, :], raw[:, c, :], ACT.Copy).then_inc(hi_ready, 1)

                hi_c(0)
                hi_c(1)
                silu(i, gate_used)
                hi_c(2)
                hi_c(3)
                rows_hi(i + 1)
                hi_c(4)
                hi_c(5)
                a_hi(i)

            rows_hi(0)
            tile(0, M0 + 2)
            tile(1, 6 + 32)
            results(0, 6 + 36)
            with act.Fori(2, 14) as i:
                tile(i, i * 6 + 32)
                results(i - 1, i * 6 + 36)
            act.wait_ge(tiles_ready, 1)
            tiles = act.value_load(expert_of[0:1, 31:32], min_val=0, max_val=7) + E
            with act.Fori(14, tiles - 1) as i:
                tile(i, i * 6 + 32)
                results(i - 1, i * 6 + 36)
            silu(tiles - 1, tiles * 6 + 26)
            for c in range(2):
                act.wait_ge(landed[4 + c], tiles * 16 + 16)
                act.wait_ge(chunk_used, tiles * 6 + (29 + c))
                A_(wsplit[:, 4 + c, 0, :], raw[:, 4 + c, :], ACT.Copy).then_inc(hi_ready, 1)
            a_hi(tiles - 1)
            results(tiles - 2, tiles * 6 + 30)
            results(tiles - 1, tiles * 6 + 32)
            for t in range(NT):
                act.wait_ge(fin_x, t + 1)
                A_(raw[:, t, 0:D], x_tiles[:, t, :], ACT.Square, accum_out=stats[:, 28 + t:29 + t]).then_inc(fin_sq, 1)

        @block.vector
        def _(dve):
            V = nc.vector
            steps = [0]

            def step(ins):
                steps[0] += 1
                ins.then_inc(chain, 1)

            def done():
                dve.wait_ge(chain, steps[0])

            def lo(n, slot):
                V.tensor_tensor(wsplit[:, n, 1, :], raw[:, slot, :], wsplit[:, n, 0, :].bitcast(F32),
                                ALU.subtract).then_inc(lo_ready, 1)

            def lo_n(n, slot):
                dve.wait_ge(hi_ready, n + 1)
                lo(split_slot(n), slot)

            def inv_rms(col, n):
                m, yv, sq = stats[:, col:col + n], nrm[:, 0:n], nrm[:, NT:NT + n]
                yi, mi = nrm[:, 0:n].bitcast(I32), m.bitcast(I32)
                step(V.tensor_scalar(m, m, 1.0 / D, EPS, ALU.mult, ALU.add))
                done()
                step(V.tensor_scalar(yi, mi, 1, None, ALU.logical_shift_right))
                done()
                step(V.tensor_scalar(yi, yi, -1.0, float(0x5F3759DF), ALU.mult, ALU.add))
                done()
                for last in (False, False, True):
                    step(V.tensor_tensor(sq, yv, yv, ALU.mult))
                    done()
                    step(V.scalar_tensor_tensor(out=sq, in0=sq, scalar=-0.5, in1=m, op0=ALU.mult, op1=ALU.mult))
                    done()
                    step(V.scalar_tensor_tensor(out=m if last else yv, in0=sq, scalar=1.5, in1=yv,
                                                op0=ALU.add, op1=ALU.mult))
                    done()

            def ada(acc, slot, a):
                for k in range(ND):
                    ins = V.scalar_tensor_tensor(out=acc, in0=raw[:, slot, k * CC:(k + 1) * CC],
                                                 scalar=c_silu[:, k:k + 1], in1=acc, op0=ALU.mult, op1=ALU.add)
                    if k < ND - 1:
                        ins.then_inc(ada_step, 1)
                        dve.wait_ge(ada_step, a * (ND - 1) + (k + 1))
                    else:
                        ins.then_inc(ada_used, 1)

            dve.wait_ge(cols_t, 1)
            V.tensor_copy(cols[:, :], ps[:, 5, 0:32]).then_inc(cols_ready, 1)
            dve.wait_ge(c_ready, 1)
            dve.wait_ge(ba_in, 16)
            for r in range(RAW_ADA):
                dve.wait_ge(landed[r % RING_A], 16 * (r // RING_A + 1))
                ada(macc_a[:, r * CC:(r + 1) * CC], r % RING_A, r)
                if r == 1:
                    dve.wait_ge(squares, NT)
                    inv_rms(0, NT)
                    for t in range(NT):
                        V.tensor_scalar(x_tiles[:, t, :], x_tiles[:, t, :], stats[:, t:t + 1], None,
                                        ALU.mult).then_inc(xhat_ready, 1)
            dve.wait_ge(consts, 2)
            step(V.reciprocal(inv_count[:, :], iota1[:, 0:16]))
            dve.wait_ge(mod_mm, 1)
            step(V.tensor_copy(mod_cols[:, :], ps[:, 7, 0:16]))
            done()
            V.scalar_tensor_tensor(out=gain[:, :], in0=mod_cols[:, 8:16], scalar=1.0, in1=cols[:, 8:16],
                                   op0=ALU.add, op1=ALU.mult).then_inc(gain_ready, 1)
            dve.wait_ge(gain_ready, 1)
            for k in range(ND + 1):
                if k < ND:
                    dve.wait_ge(xT_t, k + 1)
                    V.tensor_scalar(ps[:, k, :], ps[:, k, :], gain[:, k:k + 1], mod_cols[:, k:k + 1],
                                    ALU.mult, ALU.add).then_inc(h_aff, 1)
                if k:
                    dve.wait_ge(h_hi, k)
                    V.tensor_tensor(hT[:, 1, k - 1, :], ps[:, k - 1, :], hT[:, 0, k - 1, :].bitcast(F32),
                                    ALU.subtract).then_inc(h_lo, 1)
                if k == 0:
                    lo_n(0, 0)
                if k == 4:
                    lo_n(1, 1)

            for n in range(V0, G0):
                if n >= 1:
                    lo_n(n + 1, (RAW_V + n + 1) % RING_A)
                if n == U0:
                    dve.wait_ge(v_gelu, 2 * NT)
                    step(V.tensor_tensor(stats[:, 16:20], stats[:, 8:12], stats[:, 12:16], ALU.add))
                    done()
                    step(V.tensor_scalar(stats[:, 16:20], stats[:, 16:20], 1.0 / D, None, ALU.mult))
                    done()
                    for t in range(NT):
                        V.tensor_scalar(v[:, t * D:(t + 1) * D], v[:, t * D:(t + 1) * D], stats[:, 16 + t:17 + t],
                                        None, ALU.subtract).then_inc(v_centred, 1)
                    dve.wait_ge(v_square, NT)
                    inv_rms(20, NT)
                    for t in range(NT):
                        V.tensor_scalar(v[:, t * D:(t + 1) * D], v[:, t * D:(t + 1) * D], stats[:, 20 + t:21 + t],
                                        None, ALU.mult).then_inc(v_ready, 1)
                if n == P0:
                    dve.wait_ge(bsb_in, 16)
                    for h in range(NH):
                        dve.wait_ge(s_mm, h + 1)
                        dve.wait_ge(u_ready, h + 1)
                        s_h = ps[:, h, :].rearrange("p (c i) -> p c i", c=NT)
                        b_h = bsb[:, h * P:(h + 1) * P].unsqueeze(1).broadcast_to([P, NT, P])
                        step(V.scalar_tensor_tensor(out=s_h, in0=s_h, scalar=cols[:, 16 + h:17 + h], in1=b_h,
                                                    op0=ALU.mult, op1=ALU.add))
                        done()
                        V.tensor_tensor(u[:, h, :], ps[:, h, :], u[:, h, :], ALU.mult).then_inc(ya_f, 1)
                        if h:
                            dve.wait_ge(ya_hi, h)
                            V.tensor_tensor(ya[:, 1, h - 1, :], u[:, h - 1, :], ya[:, 0, h - 1, :].bitcast(F32),
                                            ALU.subtract).then_inc(ya_lo, 1)
                    dve.wait_ge(ya_hi, NH)
                    V.tensor_tensor(ya[:, 1, NH - 1, :], u[:, NH - 1, :], ya[:, 0, NH - 1, :].bitcast(F32),
                                    ALU.subtract).then_inc(ya_lo, 1)
                    dve.wait_ge(ya_lo, NH)
                    step(V.memset(z[:, 0:16], 0.0))
                    done()
                if n >= P0:
                    i = n - P0
                    w = WINDOWS[3 - i]
                    dve.wait_ge(chunk_used, n + 1)
                    if i >= 2:
                        dve.wait_ge(mix_mm, 2 * (i - 1))
                    for j in range(2):
                        step(V.tensor_copy(z[:, 16:], ps[:, 2 * i + j, :]))
                        done()
                        src, d, turn = z, 1, 0
                        while d < w:
                            dst = (win_a, win_b)[turn]
                            lo_col = 2 * d - 1
                            step(V.tensor_tensor(dst[:, lo_col:], src[:, lo_col:], src[:, lo_col - d:16 + SEQ - d],
                                                 ALU.add))
                            done()
                            src, d, turn = dst, 2 * d, 1 - turn
                        out_j = pooled[:, i % 2, j, :]
                        step(V.scalar_tensor_tensor(out=out_j, in0=src[:, 16:], scalar=1.0 / w, in1=z[:, 16:],
                                                    op0=ALU.mult, op1=ALU.subtract))
                        done()
                        step(V.tensor_tensor(src[:, 16:16 + w - 1], src[:, 16:16 + w - 1], inv_count[:, 0:w - 1],
                                             ALU.mult))
                        done()
                        V.tensor_tensor(out_j[:, 0:w - 1], src[:, 16:16 + w - 1], z[:, 16:16 + w - 1],
                                        ALU.subtract).then_inc(pooled_ready, 1)
                        dve.wait_ge(pooled_ready, 2 * i + j + 1)
                if n > P0 + 1:
                    mix_lo(dve, V, n - P0 - 2)
            mix_lo(dve, V, 2)
            mix_lo(dve, V, 3)
            dve.wait_ge(mix_mm, NH)
            dve.wait_ge(bb_in, 16)
            with dve.Fori(0, 4) as q:
                def lo_next(j):
                    dve.wait_ge(hi_ready, q * 4 + (G0 + j + 2))
                    lo((j + 1) % 2, (j + 1) % 4)

                def ada_next(j):
                    dve.wait_ge(landed[j], (q * 2 + (RAW_G // 4 + 2)) * 16)
                    ada(macc_b[:, ds(q * (4 * CC) + j * CC, CC)], j, q * 4 + (RAW_ADA + j))

                lo_next(0)
                ada_next(0)
                lo_next(1)
                dve.wait_ge(chunk_used, q * 4 + (G0 + 2))
                dve.wait_ge(gate_ready, q * 4 + 2)
                for b in range(2):
                    V.tensor_tensor(merged[:, ds(q * 2 + b, 1), :].rearrange("p a n -> p (a n)"), ps[:, 2 + b, :],
                                    sig_a[:, b, :], ALU.mult).then_inc(merge_a, 1)
                ada_next(1)
                lo_next(2)
                ada_next(2)
                ada_next(3)
                lo_next(3)
                dve.wait_ge(chunk_used, q * 4 + (G0 + 4))
                dve.wait_ge(gate_ready, q * 4 + 4)
                for b in range(2):
                    V.tensor_tensor(ps[:, 6 + b, :], ps[:, 6 + b, :], sig_b[:, b, :], ALU.mult).then_inc(merge_t, 1)
                for b in range(2):
                    dve.wait_ge(merge_t, q * 2 + (b + 1))
                    dve.wait_ge(merge_a, q * 2 + 2)
                    m_t = merged[:, ds(q * 2 + b, 1), :].rearrange("p a n -> p (a n)")
                    V.tensor_tensor(m_t, ps[:, 6 + b, :], m_t, ALU.add).then_inc(merge_b, 1)
            for k in range(ND):
                dve.wait_ge(m_hi, k + 1)
                V.tensor_tensor(hT[:, 1, k, :], merged[:, k, :], hT[:, 0, k, :].bitcast(F32),
                                ALU.subtract).then_inc(m_lo, 1)
            dve.wait_ge(lo_ready, O0 + 1)
            for b in range(4):
                dve.wait_ge(row_mm, b + 1)
                dst = gm if b < 2 else shf
                V.tensor_copy(dst[:, (b % 2) * 512:(b % 2) * 512 + 512], ps[:, 4 + b, :]).then_inc(row_ready, 1)
            lo_n(O0 + 1, 1)
            dve.wait_ge(gff_in, 16)
            for b in range(4):
                dve.wait_ge(row_mm, b + 5)
                c = slice((b % 2) * 512, (b % 2) * 512 + 512)
                if b < 2:
                    ins = V.scalar_tensor_tensor(out=gff[:, c], in0=ps[:, 4 + b, :], scalar=1.0, in1=gff[:, c],
                                                 op0=ALU.add, op1=ALU.mult)
                else:
                    ins = V.tensor_copy(gf[:, c], ps[:, 4 + b, :])
                ins.then_inc(row_ready, 1)
            lo_n(O0 + 2, 2)
            dve.wait_ge(x_again, 16)
            dve.wait_ge(row_ready, 8)

            def residual(t, half):
                b = 4 * half + t
                step(V.tensor_tensor(ps[:, b, :], ps[:, b, :], gm[:, half * 512:half * 512 + 512], ALU.mult))
                done()
                x_h = x_tiles[:, t, half * 512:half * 512 + 512]
                V.tensor_tensor(x_h, ps[:, b, :], x_h, ALU.add).then_inc(x2_half, 1)

            dve.wait_ge(chunk_used, O0 + 2)
            for t in range(NT):
                residual(t, 0)
                if t == 0:
                    lo_n(O0 + 3, 3)

            def normed(t):
                dve.wait_ge(sq2, t + 1)
                inv_rms(24 + t, 1)
                step(V.scalar_tensor_tensor(out=hf[:, t, :], in0=x_tiles[:, t, :], scalar=stats[:, 24 + t:25 + t],
                                            in1=gff, op0=ALU.mult, op1=ALU.mult))
                done()
                V.tensor_tensor(hf[:, t, :], hf[:, t, :], shf, ALU.add).then_inc(hf_ready, 1)

            for c in range(2):
                lo_n(M0 + c, c + 2)
            for t in range(NT):
                if t < NT - 1:
                    dve.wait_ge(o_tile, t + 1)
                else:
                    dve.wait_ge(chunk_used, M0)
                residual(t, 1)
                if t:
                    normed(t - 1)
            normed(NT - 1)

            lg = ps[:, 3, 0:NT * E].rearrange("p (t e) -> p t e", t=NT)
            te = [P, NT, E]
            dve.wait_ge(logits_mm, NT)
            step(V.tensor_reduce(r_4, lg, AX_X, ALU.max))
            done()
            V.tensor_tensor(r_d3, lg, r_4.unsqueeze(2).broadcast_to(te), ALU.subtract).then_inc(sub_ready, 1)
            dve.wait_ge(expd, 1)
            step(V.tensor_reduce(r_4, r_p3, AX_X, ALU.add))
            done()
            step(V.reciprocal(r_4, r_4))
            done()
            step(V.tensor_tensor(r_p3, r_p3, r_4.unsqueeze(2).broadcast_to(te), ALU.mult))
            done()
            dve.wait_ge(bias_in, 16)
            step(V.tensor_tensor(r_sel3, r_p3, bias_row[:, :].unsqueeze(1).broadcast_to(te), ALU.add))
            done()

            def rank(values, n, result):
                pair = [P, n, EG, EG]
                mine = values.unsqueeze(3).broadcast_to(pair)
                other = values.unsqueeze(2).broadcast_to(pair)
                step(V.tensor_tensor(r_ge[:, 0:n], other, mine, ALU.is_ge))
                step(V.tensor_tensor(r_gt[:, 0:n], other, mine, ALU.is_gt))
                done()
                step(V.tensor_tensor(r_ge[:, 0:n], r_ge[:, 0:n],
                                     order[:, 0, :, :].unsqueeze(1).broadcast_to(pair), ALU.mult))
                step(V.tensor_tensor(r_gt[:, 0:n], r_gt[:, 0:n],
                                     order[:, 1, :, :].unsqueeze(1).broadcast_to(pair), ALU.mult))
                done()
                step(V.tensor_tensor(r_ge[:, 0:n], r_ge[:, 0:n], r_gt[:, 0:n], ALU.add))
                done()
                step(V.tensor_reduce(result, r_ge[:, 0:n], AX_X, ALU.add))
                done()

            ge3 = [P, NT * EG, EG]
            sel_g = r_sel.rearrange("p (g e) -> p g e", e=EG)
            top_g = r_top.rearrange("p (g e) -> p g e", e=EG)
            rank(sel_g, NT * EG, top_g)
            step(V.tensor_scalar(r_top, r_top, 2.0, None, ALU.is_lt))
            done()
            step(V.tensor_tensor(r_m, r_sel, r_top, ALU.mult))
            done()
            step(V.tensor_reduce(r_gs, r_m.rearrange("p (g e) -> p g e", e=EG), AX_X, ALU.add))
            done()
            rank(r_gs.rearrange("p (t g) -> p t g", t=NT), NT, r_gr.rearrange("p (t g) -> p t g", t=NT))
            step(V.tensor_scalar(r_gr, r_gr, 1.0, None, ALU.is_lt))
            done()
            V.tensor_tensor(r_m.rearrange("p (g e) -> p g e", e=EG), top_g,
                            r_gr.unsqueeze(2).broadcast_to(ge3), ALU.mult).then_inc(mask_ready, 1)
            dve.wait_ge(mask_ready, 1)
            step(V.tensor_tensor(r_p, r_p, r_m, ALU.mult))
            step(V.tensor_tensor(r_d3, r_m3, iota1[:, 0:E].unsqueeze(1).broadcast_to(te), ALU.mult))
            done()
            step(V.tensor_reduce(r_4, r_p3, AX_X, ALU.add))
            step(V.tensor_reduce(r_4b, r_d3, AX_X, ALU.max))
            done()
            step(V.reciprocal(r_4, r_4))
            step(V.tensor_tensor(r_d3, r_d3, r_4b.unsqueeze(2).broadcast_to(te), ALU.is_equal))
            step(V.tensor_scalar(r_4c, tok_f[:, :], 2.0, 1.0 - SKIP, ALU.mult, ALU.add))
            step(V.tensor_copy(info[:, :, :, 0], tok_f[:, :].unsqueeze(2).broadcast_to(te)))
            done()
            step(V.tensor_tensor(info[:, :, :, 1], r_p3, r_4.unsqueeze(2).broadcast_to(te), ALU.mult))
            step(V.tensor_tensor(info[:, :, :, 2], r_d3, r_4c.unsqueeze(2).broadcast_to(te), ALU.add))
            dve.wait_ge(pos_mm, 1)
            step(V.scalar_tensor_tensor(out=pos1[:, :, :], in0=ps[:, 2, 0:NT * E].rearrange("p (t e) -> p t e", t=NT),
                                        scalar=1.0, in1=r_m3, op0=ALU.add, op1=ALU.mult))
            step(V.tensor_copy(r_cnt, ps[:, 2, NT * E:NT * E + E]))
            done()

            def select(j, e):
                dve.wait_ge(idx_mm, j)
                for t in range(NT):
                    ins = V.tensor_scalar(sel[:, t, :], iota1[:, :], base[:, ds(j, 1)], pos1[:, t, ds(e, 1)],
                                          ALU.add, ALU.is_equal)
                ins.then_inc(sel_ready, 1)

            def indices(j):
                dve.wait_ge(idx_mm, j + 1)
                dve.wait_ge(gathered, j * 16)
                V.tensor_copy(tok_idx[:, :], ps[:, 7, 0:1])
                V.tensor_copy(row_w[:, ds(j, 1)], ps[:, 7, 1:2])
                V.tensor_scalar(row_dest[:, ds(j, 1)], ps[:, 7, 2:3], float(SKIP), None,
                                ALU.add).then_inc(idx_ready, 1)

            def rows_lo(j):
                dve.wait_ge(hg_hi, j + 1)
                V.tensor_tensor(hgT[:, 1, :, :].rearrange("p k m -> p (k m)"),
                                ps[:, 2:4, :].rearrange("p b n -> p (b n)"),
                                hgT[:, 0, :, :].rearrange("p k m -> p (k m)").bitcast(F32),
                                ALU.subtract).then_inc(hg_lo, 1)

            select(0, 0)
            step(V.tensor_scalar(r_x, r_cnt, float(P), None, ALU.is_gt))
            step(V.tensor_scalar(r_x2, r_cnt, float(2 * P), None, ALU.is_gt))
            step(V.tensor_scalar(r_x3, r_cnt, float(3 * P), None, ALU.is_gt))
            done()
            indices(0)
            select(1, 1)
            step(V.tensor_tensor(r_x, r_x, r_x2, ALU.add))
            done()
            step(V.tensor_tensor(r_x, r_x, r_x3, ALU.add))
            done()
            step(V.tensor_tensor_scan(r_cum, ones[:, 0:E], r_x, 0.0, ALU.mult, ALU.add))
            done()
            ke = [P, 8, E]
            indices(1)
            lo_n(M0 + 2, 4)
            rows_lo(0)
            lo_n(M0 + 3, 5)
            step(V.tensor_tensor(r_le, iota1[:, 0:8].unsqueeze(2).broadcast_to(ke),
                                 r_cum.unsqueeze(1).broadcast_to(ke), ALU.is_gt))
            done()
            step(V.tensor_reduce(r_8, r_le, AX_X, ALU.add))
            done()
            step(V.tensor_tensor(r_le, r_le, r_cum.unsqueeze(1).broadcast_to(ke), ALU.mult))
            done()
            step(V.tensor_scalar(expert_of[:, E:E + 8], r_8, float(E - 1), None, ALU.min))
            step(V.tensor_reduce(r_8b, r_le, AX_X, ALU.max))
            done()
            step(V.tensor_tensor(r_8b, iota1[:, 0:8], r_8b, ALU.subtract))
            done()
            step(V.tensor_scalar(base[:, E:E + 8], r_8b, float(P), None, ALU.mult))
            V.tensor_copy(expert_of[:, 31:32], r_cum[:, E - 1:E]).then_inc(tiles_ready, 1)
            dve.wait_ge(tiles_ready, 1)

            def hidden(i, up_used):
                dve.wait_ge(silu_ready, i + 1)
                dve.wait_ge(chunk_used, up_used)
                dve.wait_ge(a_trans, i)
                V.tensor_tensor(a_t, ps[:, 1, :], act_g, ALU.mult).then_inc(a_ready, 1)

            def a_lo(i):
                dve.wait_ge(aT_hi, i + 1)
                V.tensor_tensor(aT[:, 1, :, :].rearrange("p k m -> p (k m)"), ps[:, 4, :],
                                aT[:, 0, :, :].rearrange("p k m -> p (k m)").bitcast(F32),
                                ALU.subtract).then_inc(aT_lo, 1)

            def destination(j):
                dve.wait_ge(idx_ready, j + 1)
                dve.wait_ge(scattered, j * 16)
                V.tensor_copy(dest_now[:, :], row_dest[:, ds(j, 1)]).then_inc(dest_ready, 1)

            def tile(i, e2, up_used, prev):
                def lo_c(c):
                    dve.wait_ge(hi_ready, i * 6 + (37 + c))
                    lo(c, c)

                lo_c(0)
                lo_c(1)
                select(i + 2, e2)
                lo_c(2)
                hidden(i, up_used)
                lo_c(3)
                rows_lo(i + 1)
                lo_c(4)
                lo_c(5)
                if prev:
                    destination(i - 1)
                a_lo(i)
                indices(i + 2)

            tile(0, 2, M0 + 4, False)
            tile(1, 3, 6 + 34, True)
            with dve.Fori(2, 14) as i:
                tile(i, i + 2, i * 6 + 34, True)
            tiles = dve.value_load(expert_of[0:1, 31:32], min_val=0, max_val=7) + E
            with dve.Fori(14, tiles - 1) as i:
                e2 = dve.value_load(expert_of[0:1, ds(i + 2, 1)], min_val=0, max_val=E - 1)
                tile(i, e2, i * 6 + 34, True)
            hidden(tiles - 1, tiles * 6 + 28)
            for c in range(2):
                dve.wait_ge(hi_ready, tiles * 6 + (31 + c))
                lo(4 + c, 4 + c)
            destination(tiles - 2)
            a_lo(tiles - 1)
            destination(tiles - 1)
            for t in range(NT):
                dve.wait_ge(y_in[t], 16)
                step(V.tensor_tensor(raw[:, t, 0:D], raw[:, t, 0:D], raw[:, t, D:2 * D], ALU.add))
                done()
                step(V.tensor_tensor(raw[:, t, 0:D], raw[:, t, 0:D], gf, ALU.mult))
                done()
                V.tensor_tensor(x_tiles[:, t, :], x_tiles[:, t, :], raw[:, t, 0:D], ALU.add).then_inc(fin_x, 1)
                if t:
                    final(dve, V, step, inv_rms, t - 1)
            final(dve, V, step, inv_rms, NT - 1)

        @block.tensor
        def _(pe):
            def three(out, w_hi, w_lo, m_hi_, m_lo_, first, last):
                nc.tensor.matmul(out, w_hi, m_hi_, start=first, stop=False)
                nc.tensor.matmul(out, w_hi, m_lo_, start=False, stop=False)
                return nc.tensor.matmul(out, w_lo, m_hi_, start=False, stop=last)

            pe.wait_ge(consts, 1)
            pe.wait_ge(rows_in, 64)
            nc.tensor.transpose(ps[:, 5, 0:32], rows32, ident[0:32, 0:32]).then_inc(cols_t, 1)
            pe.wait_ge(causal, 1)
            for h in range(NH):
                mm = nc.tensor.transpose(ps[:, 6 + h // 4, (h % 4) * P:(h % 4 + 1) * P], wnat[:, h * P:(h + 1) * P],
                                         ident[:, :])
            mm.then_inc(ws_t, 1)
            pe.wait_ge(xhat_ready, NT)
            for k in range(ND):
                if k == 5:
                    pe.wait_ge(cols_ready, 1)
                if k == 6:
                    pe.wait_ge(ws_ready, 1)
                if k == 7:
                    pe.wait_ge(ada_used, RAW_ADA)
                    for j in range(2 * ND):
                        mm = nc.tensor.matmul(ps[:, 7, j:j + 1], macc_a[:, j * P:(j + 1) * P], ones[:, 0:1],
                                              start=True, stop=True)
                    mm.then_inc(mod_mm, 1)
                    pe.wait_ge(gain_ready, 1)
                for t in range(NT):
                    mm = nc.tensor.transpose(ps[:, k, t * P:(t + 1) * P], x_tiles[:, t, k * P:(k + 1) * P], ident[:, :])
                mm.then_inc(xT_t, 1)

            def wblock(s, part, k, width):
                return wsplit[:, s, part, k * width:(k + 1) * width]

            def by_token(n, stationary, bank):
                s, kh = split_slot(n), n % 2
                for t in range(NT):
                    for k in range(4):
                        kk = 4 * kh + k
                        mm = three(ps[:, bank + t, :],
                                   stationary[:, 0, kk, t * P:(t + 1) * P], stationary[:, 1, kk, t * P:(t + 1) * P],
                                   wblock(s, 0, k, 512), wblock(s, 1, k, 512), kk == 0, kk == ND - 1)
                    if n == O0 + 3 and t < NT - 1:
                        mm.then_inc(o_tile, 1)
                mm.then_inc(chunk_used, 1)

            def by_feature(s, moving, bank):
                for m in range(2):
                    for k in range(ND):
                        col = k * CC + m * P
                        w_hi, w_lo = wsplit[:, s, 0, col:col + P], wsplit[:, s, 1, col:col + P]
                        mm = three(ps[:, bank + m, :], w_hi, w_lo, moving[:, 0, k, :], moving[:, 1, k, :],
                                   k == 0, k == ND - 1)
                mm.then_inc(chunk_used, 1)

            for n in range(V0, U0):
                pe.wait_ge(lo_ready, n + 1)
                pe.wait_ge(h_lo, 4 if n == 0 else ND)
                by_token(n, hT, 4 * (n // 2))
            for n in range(U0, P0):
                pe.wait_ge(lo_ready, n + 1)
                if n < U0 + 2:
                    pe.wait_ge(v_gelu, NT)
                else:
                    pe.wait_ge(v_gelu, 2 * NT)
                by_feature(n % 2, hT, 2 * (n - U0))
            pe.wait_ge(v_ready, NT)
            pe.wait_ge(ws_ready, 1)
            for h in range(NH):
                pe.wait_ge(u_ready, h + 1)
                for c in range(NT):
                    mm = nc.tensor.matmul(ps[:, h, c * P:(c + 1) * P], v[:, c * D + h * P:c * D + (h + 1) * P],
                                          wsT[:, h * P:(h + 1) * P], start=True, stop=True)
                mm.then_inc(s_mm, 1)

            def mix(i):
                g = 3 - i
                pe.wait_ge(pooled_ready, 2 * i + 2)
                pe.wait_ge(wpool_in, 16)
                for dj in range(2):
                    for k in range(2):
                        col = (2 * g + k) * 256 + dj * P
                        mm = nc.tensor.matmul(ps[:, 2 * i + dj, :], raw[:, 4, col:col + P], pooled[:, i % 2, k, :],
                                              start=(k == 0), stop=(k == 1))
                    mm.then_inc(mix_mm, 1)

            for n in range(P0, G0):
                pe.wait_ge(lo_ready, n + 1)
                pe.wait_ge(ya_f, 2 * (n - P0) + 2)
                s = n % 2
                by_feature(s, hT, 2 * (n - P0))
                if n > P0:
                    mix(n - P0 - 1)
            mix(3)
            pe.wait_ge(ya_lo, NH)
            with pe.Fori(0, 4) as q:
                for j in range(4):
                    pe.wait_ge(lo_ready, q * 4 + (G0 + j + 1))
                    pe.wait_ge(yb_lo, 2 * j + 2)
                    by_feature(j % 2, (hT, ya, hT, yb)[j], 2 * j)

            def row(b, bank):
                nc.tensor.matmul(ps[:, bank, :], ones[:, :], macc_b[:, b * 512:(b + 1) * 512],
                                 start=True, stop=True).then_inc(row_mm, 1)

            pe.wait_ge(ada_used, RAW_ADA + 16)
            pe.wait_ge(merge_b, ND)
            for b in range(4):
                row(b, 4 + b)
            for n in range(O0, M0):
                pe.wait_ge(lo_ready, n + 1)
                if n == O0 + 1:
                    pe.wait_ge(row_ready, 4)
                    for b in range(4):
                        row(4 + b, 4 + b)
                if n == O0:
                    pe.wait_ge(m_lo, 4)
                if n == O0 + 1:
                    pe.wait_ge(m_lo, ND)
                if n == O0 + 2:
                    pe.wait_ge(row_ready, 8)
                by_token(n, hT, 4 * ((n - O0) // 2))
            pe.wait_ge(router_in, 16)
            for t in range(NT):
                pe.wait_ge(hf_ready, t + 1)
                if t:
                    pe.wait_ge(hfT_ready, t)
                for k in range(ND):
                    mm = nc.tensor.transpose(ps[:, k // 4, (k % 4) * P:(k % 4 + 1) * P], hf[:, t, k * P:(k + 1) * P],
                                             ident[:, :])
                mm.then_inc(hf_t, 1)
                pe.wait_ge(hfT_ready, t + 1)
                for k in range(ND):
                    mm = nc.tensor.matmul(ps[:, 3, t * E:(t + 1) * E], hfT[:, t % 2, k, :], router[:, k, :],
                                          start=(k == 0), stop=(k == ND - 1))
                mm.then_inc(logits_mm, 1)
            pe.wait_ge(mask_ready, 1)
            for t in range(NT + 1):
                o = ps[:, 2, t * E:(t + 1) * E]
                for b in range(t):
                    mm = nc.tensor.matmul(o, ones[:, :], r_m[:, b * E:(b + 1) * E], start=(b == 0), stop=(b == NT - 1))
                if t < NT:
                    nc.tensor.matmul(o, before[:, :], r_m[:, t * E:(t + 1) * E], start=(t == 0), stop=True)
            mm.then_inc(pos_mm, 1)

            def index(j, e):
                pe.wait_ge(sel_ready, j + 1)
                pe.wait_ge(idx_ready, j)
                for t in range(NT):
                    mm = nc.tensor.matmul(ps[:, 7, 0:3], sel[:, t, :],
                                          info[:, t, ds(e, 1), :].rearrange("p a n -> p (a n)"),
                                          start=(t == 0), stop=(t == NT - 1))
                mm.then_inc(idx_mm, 1)

            def turn(j):
                pe.wait_ge(gathered, j * 16 + 16)
                pe.wait_ge(hg_lo, j)
                for k in range(ND):
                    mm = nc.tensor.transpose(ps[:, 2 + k // 4, (k % 4) * P:(k % 4 + 1) * P],
                                             hg[:, k * P:(k + 1) * P], ident[:, :])
                mm.then_inc(hg_t, 1)

            def gate_up(i, first_chunk, slot0):
                pe.wait_ge(hg_lo, i + 1)
                for c in range(4):
                    pe.wait_ge(lo_ready, first_chunk + (c + 1))
                    for k in range(4):
                        kk = 4 * (c % 2) + k
                        mm = three(ps[:, c // 2, :], hgT[:, 0, kk, :], hgT[:, 1, kk, :],
                                   wblock(slot0 + c, 0, k, 512), wblock(slot0 + c, 1, k, 512), kk == 0, kk == ND - 1)
                    mm.then_inc(chunk_used, 1)

            def down(i, first_chunk):
                pe.wait_ge(aT_lo, i + 1)
                pe.wait_ge(y_ready, i)
                for c in range(2):
                    pe.wait_ge(lo_ready, first_chunk + (c + 1))
                    for k in range(2):
                        for half in range(2):
                            w = 2 * k + half
                            mm = three(ps[:, 5 + half, :], aT[:, 0, 2 * c + k, :], aT[:, 1, 2 * c + k, :],
                                       wblock(4 + c, 0, w, 512), wblock(4 + c, 1, w, 512),
                                       c == 0 and k == 0, c == 1 and k == 1)
                    mm.then_inc(chunk_used, 1)

            def turn_hidden(i):
                pe.wait_ge(a_ready, i + 1)
                pe.wait_ge(aT_lo, i)
                for k in range(NF):
                    mm = nc.tensor.transpose(ps[:, 4, k * P:(k + 1) * P], a_t[:, k * P:(k + 1) * P], ident[:, :])
                mm.then_inc(a_trans, 1)

            index(0, 0)
            index(1, 1)
            turn(0)
            gate_up(0, M0, 2)
            turn(1)
            turn_hidden(0)
            index(2, 2)

            def tile(i, e2):
                gate_up(i, i * 6 + 30, 0)
                turn(i + 1)
                down(i - 1, i * 6 + 34)
                turn_hidden(i)
                index(i + 2, e2)

            tile(1, 3)
            with pe.Fori(2, 14) as i:
                tile(i, i + 2)
            pe.wait_ge(tiles_ready, 1)
            tiles = pe.value_load(expert_of[0:1, 31:32], min_val=0, max_val=7) + E
            with pe.Fori(14, tiles - 1) as i:
                e2 = pe.value_load(expert_of[0:1, ds(i + 2, 1)], min_val=0, max_val=E - 1)
                tile(i, e2)
            gate_up(tiles - 1, tiles * 6 + 24, 0)
            down(tiles - 2, tiles * 6 + 28)
            turn_hidden(tiles - 1)
            down(tiles - 1, tiles * 6 + 30)


_INS = ["x", "c", "w_ada", "b_ada", "norm_mix_g", "w_in", "v_norm_g", "sgu_w", "sgu_b", "pool_w", "pool_scale",
        "w_branch_a", "w_branch_b", "w_out", "norm_ffn_g", "router_w", "router_bias",
        "w_exp_gate", "w_exp_up", "w_exp_down", "final_norm_g"]


def kernel(**inputs):
    import numpy as _np
    import concourse.bacc as _bacc
    from concourse import mybir as _mybir
    from concourse.bass_utils import run_bass_kernel_spmd as _run

    nc = _bacc.Bacc("TRN2", target_bir_lowering=False, num_devices=1)
    arrays, aps = {}, {}
    for name in _INS:
        a = _np.ascontiguousarray(inputs[name])
        arrays[f"in_{name}"] = a
        aps[name] = nc.dram_tensor(f"in_{name}", a.shape, _mybir.dt.from_np(a.dtype), kind="ExternalInput").ap()
    out = nc.dram_tensor("out_0", (1, SEQ, D), F32, kind="ExternalOutput").ap()
    tokens_moe_kernel(nc, aps, out)
    r = _run(nc, [arrays], core_ids=[0])
    return r.results[0]["out_0"]
```

```python
from contextlib import ExitStack

import concourse.bass as bass
from concourse import mybir

F32 = mybir.dt.float32
F32R = mybir.dt.float32r
I32 = mybir.dt.int32
ALU = mybir.AluOpType
ACT = mybir.ActivationFunctionType
AX_X = mybir.AxisListType.X
ds = bass.ds

P = 128
SEQ = 512
NT = SEQ // P
D = 1024
ND = D // P
NH = 8
E = 16
EG = 4
FE = D // 2
NF = FE // P
WINDOWS = (2, 4, 8, 16)
EPS = 1e-6

CH = 2048
CC = CH // ND
RING_A = 4
RING = 6

V0, U0, P0, G0, O0 = 0, 4, 8, 12, 28
M0 = 32
RAW_ADA = 8
RAW_V = RAW_ADA
RAW_G = RAW_V + G0
RAW_O = RAW_G + 32
TILES_MAX = E + 8
SKIP = 5000


def tokens_moe_kernel(nc, A, out):
    w_ada = A["w_ada"][0].rearrange("(k p) n -> p k n", p=P)
    w_in = A["w_in"][0].rearrange("(k p) n -> p k n", p=P)
    w_a = A["w_branch_a"][0].rearrange("(k p) n -> p k n", p=P)
    w_b = A["w_branch_b"][0].rearrange("(k p) n -> p k n", p=P)
    w_out = A["w_out"][0].rearrange("(k p) n -> p k n", p=P)
    w_gate = A["w_exp_gate"][0].rearrange("e (k p) f -> e p k f", p=P)
    w_up = A["w_exp_up"][0].rearrange("e (k p) f -> e p k f", p=P)
    w_down = A["w_exp_down"][0].rearrange("e (k p) n -> e p k n", p=P)
    x_rows = A["x"][0].rearrange("(t p) d -> p t d", p=P)
    out_rows = out[0].rearrange("(t p) d -> p t d", p=P)

    hf_dram = nc.dram_tensor("hf_rows", (SEQ, D), F32, kind="Internal").ap()
    y_dram = nc.dram_tensor("expert_rows", (2 * SEQ + 1, D), F32, kind="Internal").ap()
    hf_out = hf_dram.rearrange("(t p) d -> p t d", p=P)
    y_pairs = y_dram[1:2 * SEQ + 1, :].rearrange("(t p two) d -> t p (two d)", p=P, two=2)

    ctx = ExitStack()
    with ctx:
        def sb(name, shape, dt=F32):
            return ctx.enter_context(nc.sbuf_tensor(name, shape, dt))

        def sem(name):
            return ctx.enter_context(nc.semaphore(name))

        ps = ctx.enter_context(nc.psum_tensor("ps", [P, 8, 512], F32))
        raw = sb("raw", [P, RING, CH])
        wsplit = sb("wsplit", [P, RING, 2, CH], F32R)
        mx = sb("mx", [P, NT * D])
        tmp = sb("tmp", [P, 2 * D])
        ident = sb("ident", [P, P])
        ones = sb("ones", [P, P])
        before = sb("before", [P, P])
        iota1 = sb("iota1", [P, P])
        router = sb("router", [P, ND, E])
        cols = sb("cols", [P, 48])
        c_silu = sb("c_silu", [P, ND])
        mod_cols = sb("mod_cols", [P, 16])
        gain = sb("gain", [P, ND])
        stats = sb("stats", [P, 32])
        nrm = sb("nrm", [P, 2 * NT + 1])
        inv_count = sb("inv_count", [P, 16])
        bias_row = sb("bias_row", [P, E])
        order = sb("order", [P, 2, EG, EG])
        pos1 = sb("pos1", [P, NT, E])
        info = sb("info", [P, NT, E, 3])
        base = sb("base", [P, TILES_MAX])
        expert_of = sb("expert_of", [P, 32], I32)
        row_w = sb("row_w", [P, TILES_MAX])
        row_dest = sb("row_dest", [P, TILES_MAX], I32)
        tok_idx = sb("tok_idx", [P, 1], I32)
        dest_now = sb("dest_now", [P, 1], I32)
        iota_i = sb("iota_i", [P, P], I32)
        tok_i = sb("tok_i", [P, NT], I32)
        tok_f = sb("tok_f", [P, NT])
        with nc.sbuf_tensor("hT", [P, 2, ND, SEQ], F32R) as hT:
            pass
        hgT = sb("hgT", [P, 2, ND, P], F32R)
        aT = sb("aT", [P, 2, NF, P], F32R)
        work = sb("work", [P, 5 * D])

        v = raw[:, 4:6, :].rearrange("p s c -> p (s c)")
        ada_prod = raw[:, 4, :].rearrange("p (k n) -> p k n", k=ND)
        macc_a = work[:, 0:RAW_ADA // 2 * CC]
        mod_row = work[0:1, 2 * D:2 * D + CC]
        macc_b = raw[:, 4:6, :].rearrange("p s c -> p (s c)")
        hf = raw[:, 4:6, :].rearrange("p s (t d) -> p (s t) d", d=D)
        shf, gff = raw[:, 0, 0:D], raw[:, 0, D:2 * D]
        ya = wsplit[:, 2:4, :, :].rearrange("p s a (b n) -> p s (a b) n", n=SEQ)
        yb = wsplit[:, 4:6, :, :].rearrange("p s a (b n) -> p s (a b) n", n=SEQ)
        wnat = tmp[:, D:2 * D]
        wsT = tmp[:, 0:D]
        bsb = tmp[:, D:2 * D]
        rows_c = raw[0:48, 5, D:D + P]
        gm = tmp[:, 0:D]
        hg = work[:, 0:D]
        y = work[:, D:2 * D]
        act_g = work[:, 2 * D:2 * D + FE]
        a_t = work[:, 2 * D + FE:3 * D]
        gf = tmp[:, D:2 * D]
        hfT = work[:, 0:2 * D].rearrange("p (b k m) -> p b k m", b=2, m=P)
        sel = work[:, 3 * D:3 * D + NT * P].rearrange("p (t m) -> p t m", t=NT)
        rt = work[:, 3 * D + NT * P:5 * D]
        gfin = work[:, 4 * D:5 * D]

        rows_in = sem("rows_in")
        x_in = [sem(f"x_in{t}") for t in range(NT)]
        wnat_in, bsb_in, router_in, bb_in = map(sem, ("wnat_in", "bsb_in", "router_in", "bb_in"))
        bias_in, wpool_in, gff_in, x_again = map(sem, ("bias_in", "wpool_in", "gff_in", "x_again"))
        landed = [sem(f"landed{s}") for s in range(RING)]
        hi_ready, lo_ready, chunk_used, ada_used, ada_step = map(
            sem, ("hi_ready", "lo_ready", "chunk_used", "ada_used", "ada_step"))
        consts, pool_step, causal, cols_t, cols_ready, c_ready = map(
            sem, ("consts", "pool_step", "causal", "cols_t", "cols_ready", "c_ready"))
        maccb_zero, mod_used, mod_row_ready = map(sem, ("maccb_zero", "mod_used", "mod_row_ready"))
        ws_t, ws_ready, squares, xhat_ready, xT_t, mod_mm, mod_ready, gain_ready = map(
            sem, ("ws_t", "ws_ready", "squares", "xhat_ready", "xT_t", "mod_mm", "mod_ready", "gain_ready"))
        h_aff, h_hi, h_lo = map(sem, ("h_aff", "h_hi", "h_lo"))
        chain = sem("chain")
        v_gelu, v_centred, v_square, v_ready, u_ready = map(
            sem, ("v_gelu", "v_centred", "v_square", "v_ready", "u_ready"))
        s_mm, ya_f, ya_hi, ya_lo = map(sem, ("s_mm", "ya_f", "ya_hi", "ya_lo"))
        zp_read, pooled_ready, mix_mm, yb_hi, yb_lo = map(
            sem, ("zp_read", "pooled_ready", "mix_mm", "yb_hi", "yb_lo"))
        gate_ready, merge_a, merge_t, merge_b, m_hi, m_lo = map(
            sem, ("gate_ready", "merge_a", "merge_t", "merge_b", "m_hi", "m_lo"))
        row_mm, row_ready, o_tile, x2_half = map(sem, ("row_mm", "row_ready", "o_tile", "x2_half"))
        sq2, hf_scaled, hf_ready, hf_saved, hf_t, hfT_ready, logits_mm, expd, mask_ready, pos_mm, tiles_ready = map(
            sem, ("sq2", "hf_scaled", "hf_ready", "hf_saved", "hf_t", "hfT_ready", "logits_mm", "expd", "mask_ready",
                  "pos_mm", "tiles_ready"))
        sel_ready, idx_mm, idx_ready, gathered, hg_t, hg_hi, hg_lo = map(
            sem, ("sel_ready", "idx_mm", "idx_ready", "gathered", "hg_t", "hg_hi", "hg_lo"))
        silu_ready, a_ready, a_trans, aT_hi, aT_lo, y_ready, dest_ready, scattered = map(
            sem, ("silu_ready", "a_ready", "a_trans", "aT_hi", "aT_lo", "y_ready", "dest_ready", "scattered"))
        gfin_in, fin_x, fin_sq, fin_n, fin_ready, out_done = map(
            sem, ("gfin_in", "fin_x", "fin_sq", "fin_n", "fin_ready", "out_done"))
        y_sum, hg_zero = sem("y_sum"), sem("hg_zero")
        y_in = [sem(f"y_in{t}") for t in range(NT)]

        x_tiles = mx[:, :].rearrange("p (t d) -> p t d", t=NT)
        u = mx[:, :].rearrange("p (m n) -> p m n", n=SEQ)
        merged = u
        z, win_a, win_b = (mx[:, i * (16 + SEQ):(i + 1) * (16 + SEQ)] for i in range(3))
        pooled = mx[:, 2048:4096].rearrange("p (b k n) -> p b k n", b=2, k=2)
        sig_a = tmp[:, 0:D].rearrange("p (b n) -> p b n", b=2)
        sig_b = tmp[:, D:2 * D].rearrange("p (b n) -> p b n", b=2)

        at = [0]

        def small(n):
            at[0] += n
            return rt[:, at[0] - n:at[0]]

        te_view = lambda a: a.rearrange("p (t e) -> p t e", t=NT)
        r_d, r_p, r_sel, r_top = (small(NT * E) for _ in range(4))
        r_m_all = small((NT + 1) * E)
        r_m = r_m_all[:, 0:NT * E]
        r_d3, r_p3, r_sel3, r_m3 = map(te_view, (r_d, r_p, r_sel, r_m))
        r_4, r_4b, r_4c = (small(NT) for _ in range(3))
        r_gs, r_gr = small(NT * EG), small(NT * EG)
        r_ge, r_gt = (small(NT * E * EG).rearrange("p (g a b) -> p g a b", a=EG, b=EG) for _ in range(2))
        r_cnt, r_x, r_x2, r_x3, r_cum = (small(E) for _ in range(5))
        r_le = small(8 * E).rearrange("p (k e) -> p k e", k=8)
        r_8, r_8b = small(8), small(8)
        sub_ready = sem("sub_ready")

        def mix_hi(act, activation, i):
            for j in range(2):
                m = 2 * (3 - i) + j
                act.wait_ge(mix_mm, 2 * i + j + 1)
                activation(yb[:, 0, m, :], ps[:, 2 * i + j, :], ACT.Copy,
                           scale=cols[:, 24 + m:25 + m]).then_inc(yb_hi, 1)

        def mix_lo(dve, V, i):
            for j in range(2):
                m = 2 * (3 - i) + j
                dve.wait_ge(yb_hi, 2 * i + j + 1)
                V.scalar_tensor_tensor(out=yb[:, 1, m, :], in0=ps[:, 2 * i + j, :], scalar=cols[:, 24 + m:25 + m],
                                       in1=yb[:, 0, m, :].bitcast(F32), op0=ALU.mult,
                                       op1=ALU.subtract).then_inc(yb_lo, 1)

        def turned(act, activation, t):
            b = 5 * (t % 2)
            act.wait_ge(hf_t, t + 1)
            if t >= 2:
                act.wait_ge(logits_mm, t - 1)
            activation(hfT[:, t % 2, :, :].rearrange("p k m -> p (k m)"), ps[:, b:b + 2, :].rearrange("p b n -> p (b n)"),
                       ACT.Copy).then_inc(hfT_ready, 1)

        def final(dve, V, inv_rms_1, t):
            dve.wait_ge(fin_sq, t + 1)
            inv_rms_1(28 + t)
            dve.wait_ge(gfin_in, 16)
            V.scalar_tensor_tensor(out=x_tiles[:, t, :], in0=x_tiles[:, t, :], scalar=stats[:, 28 + t:29 + t],
                                   in1=gfin, op0=ALU.mult, op1=ALU.mult).then_inc(fin_ready, 1)

        block = ctx.enter_context(nc.Block())

        def split_slot(n):
            if n == M0 - 1:
                return 4
            return n % 2 if n < M0 else (n - M0 + 2) % RING

        def raw_place(n):
            r = RAW_V + n if n < G0 else (RAW_O + n - O0 if n >= O0 else None)
            return r % RING_A, 16 * (r // RING_A + 1)

        def wait_reg(engine, semaphore, value, least=1):
            if not isinstance(value, int):
                value = engine.to_reg(value)
            engine.wait_ge(semaphore, least)
            engine.wait_ge(semaphore, value)

        @block.sync
        def _(sp):
            def load(slot, src, k):
                sp.dma_start(raw[:, slot, :].rearrange("p (k n) -> p k n", k=k), src).then_inc(landed[slot], 16)

            for i, name in enumerate(("c", "norm_mix_g", "v_norm_g", "pool_scale")):
                sp.dma_start(rows_c[8 * i:8 * i + 8, :],
                            A[name].rearrange("a (k p) -> (a k) p", p=P)).then_inc(rows_in, 16)
            sp.dma_start(rows_c[32:48, :],
                         A["b_ada"][:, 0:2 * D].rearrange("a (k p) -> (a k) p", p=P)).then_inc(rows_in, 16)
            def first_used(r):
                sp.wait_ge(mod_used if r % 2 else ada_used, r // 2 + 1)

            for r in range(RAW_ADA):
                if r >= RING_A:
                    first_used(r - RING_A)
                load(r % RING_A, w_ada[:, :, r * CC:(r + 1) * CC], ND)
                if r == 1:
                    for t in range(NT):
                        sp.dma_start(x_tiles[:, t, :], x_rows[:, t, :]).then_inc(x_in[t], 16)
                if r == 3:
                    sp.dma_start(wnat.rearrange("p (h j) -> p h j", h=NH),
                                 A["sgu_w"][0].rearrange("h i j -> i h j")).then_inc(wnat_in, 16)
            for n in range(V0, G0):
                if n < RING_A:
                    first_used(RING_A + n)
                else:
                    sp.wait_ge(lo_ready, n - RING_A + 1)
                if n < U0:
                    half, kh = n // 2, n % 2
                    load(n % RING_A, w_in[:, 4 * kh:4 * kh + 4, D + half * 512:D + half * 512 + 512], 4)
                elif n < P0:
                    load(n % RING_A, w_in[:, :, (n - U0) * CC:(n - U0 + 1) * CC], ND)
                else:
                    g = 3 - (n - P0)
                    load(n % RING_A, w_in[:, :, 2 * D + g * CC:2 * D + (g + 1) * CC], ND)
            sp.wait_ge(s_mm, NH)
            sp.dma_start(raw[:, 4, :].rearrange("p (a n) -> p a n", n=256),
                         A["pool_w"][0].rearrange("g (k p) n -> p (g k) n", p=P)).then_inc(wpool_in, 16)
            with sp.Fori(0, 4) as q:
                for j, (w, c0) in enumerate(((w_in, 3 * D), (w_a, 0), (w_in, 4 * D), (w_b, 0))):
                    wait_reg(sp, lo_ready, q * 4 + (P0 + 1 + j))
                    wait_reg(sp, ada_used, q * 4 + (1 + j))
                    load(j, w[:, :, ds(q * CC + c0, CC)], ND)
                for j in range(4):
                    wait_reg(sp, lo_ready, q * 4 + (G0 + 1 + j))
                    load(j, w_ada[:, :, ds(q * (4 * CC) + (2 * D + j * CC), CC)], ND)
            for j in range(4):
                sp.wait_ge(ada_used, RAW_ADA // 2 + 12 + j + 1)
                half, kh = j % 2, j // 2
                load(j, w_out[:, 4 * kh:4 * kh + 4, half * 512:half * 512 + 512], 4)
            sp.wait_ge(m_lo, ND)
            sp.dma_start(mx[:, :].rearrange("p (t d) -> p t d", t=NT), x_rows).then_inc(x_again, 16)
            sp.wait_ge(lo_ready, O0 + 1)
            sp.dma_start(gff, A["norm_ffn_g"][0].partition_broadcast(P)).then_inc(gff_in, 16)
            for c in range(2):
                sp.wait_ge(lo_ready, M0 - 1 + c)
                load(c + 2, w_gate[0, :, 4 * c:4 * c + 4, :], 4)
            for t in range(NT):
                sp.wait_ge(hf_ready, t + 1)
                sp.dma_start(hf_out[:, t, :], hf[:, t, :]).then_inc(hf_saved, 16)
            sp.wait_ge(hf_saved, 16 * NT)
            sp.wait_ge(hf_t, NT)
            for c in range(2):
                load(c + 4, w_up[0, :, 4 * c:4 * c + 4, :], 4)

            def weights(i, e, e_prev):
                for c in range(RING):
                    wait_reg(sp, lo_ready, i * 6 + (30 + c - 5))
                    if c < 4:
                        w, k0, k = (w_gate if c < 2 else w_up), 4 * (c % 2), 4
                        src = w[ds(e, 1), :, k0:k0 + k, :]
                    else:
                        k0, k = 2 * (c - 4), 2
                        src = w_down[ds(e_prev, 1), :, k0:k0 + k, :]
                    load(c, src.rearrange("a p k f -> (a p) k f"), k)

            with sp.Fori(1, 14) as i:
                weights(i, i, i - 1)
            sp.wait_ge(tiles_ready, 1)
            tiles = sp.value_load(expert_of[0:1, 31:32], min_val=0, max_val=7) + E
            with sp.Fori(14, tiles) as i:
                e = sp.value_load(expert_of[0:1, ds(i, 1)], min_val=0, max_val=E - 1)
                e_prev = sp.value_load(expert_of[0:1, ds(i - 1, 1)], min_val=0, max_val=E - 1)
                weights(i, e, e_prev)
            e = sp.value_load(expert_of[0:1, ds(tiles - 1, 1)], min_val=0, max_val=E - 1)
            for c in range(2):
                wait_reg(sp, lo_ready, tiles * 6 + (25 + c))
                load(c, w_down[ds(e, 1), :, 2 * c:2 * c + 2, :].rearrange("a p k f -> (a p) k f"), 2)
            sp.dma_start(gfin, A["final_norm_g"].partition_broadcast(P)).then_inc(gfin_in, 16)
            wait_reg(sp, scattered, tiles * 16)
            for t in range(NT):
                sp.dma_start(raw[:, t, :], y_pairs[t]).then_inc(y_in[t], 16)
            for t in range(NT):
                sp.wait_ge(fin_ready, t + 1)
                sp.dma_start(out_rows[:, t, :], mx[:, t * D:(t + 1) * D]).then_inc(out_done, 16)
            sp.wait_ge(out_done, 16 * NT)

        @block.gpsimd
        def _(pool):
            g = nc.gpsimd
            g.memset(ident[:, :], 0.0)
            g.memset(ones[:, :], 1.0)
            g.memset(before[:, :], 1.0)
            g.memset(base[:, :], 0.0)
            g.memset(order[:, :, :, :], 1.0)
            g.iota(iota_i[:, :], pattern=[[1, P]], base=1, channel_multiplier=0)
            g.iota(tok_i[:, :], pattern=[[P, NT]], base=0, channel_multiplier=1)
            g.iota(expert_of[:, 0:E], pattern=[[1, E]], base=0, channel_multiplier=0).then_inc(pool_step, 1)
            pool.wait_ge(pool_step, 1)
            g.affine_select(out=ident[:, :], in_=ident[:, :], compare_op=ALU.not_equal, fill=1.0, base=0,
                            pattern=[[-1, P]], channel_multiplier=1).then_inc(consts, 1)
            g.affine_select(out=before[:, :], in_=before[:, :], compare_op=ALU.is_gt, fill=0.0, base=0,
                            pattern=[[1, P]], channel_multiplier=-1)
            g.affine_select(out=order[:, 0, :, :], in_=order[:, 0, :, :], compare_op=ALU.is_gt, fill=0.0, base=0,
                            pattern=[[1, EG], [-1, EG]], channel_multiplier=0)
            g.affine_select(out=order[:, 1, :, :], in_=order[:, 1, :, :], compare_op=ALU.is_gt, fill=0.0, base=0,
                            pattern=[[-1, EG], [1, EG]], channel_multiplier=0)
            g.tensor_copy(iota1[:, :], iota_i[:, :])
            g.tensor_copy(tok_f[:, :], tok_i[:, :]).then_inc(consts, 1)
            pool.wait_ge(wnat_in, 16)
            w_ihj = wnat.rearrange("p (h j) -> p h j", h=NH)
            g.affine_select(out=w_ihj, in_=w_ihj, compare_op=ALU.is_ge, fill=0.0, base=0,
                            pattern=[[0, NH], [-1, P]], channel_multiplier=1).then_inc(causal, 1)
            pool.wait_ge(mix_mm, NH)
            g.memset(macc_b, 0.0).then_inc(maccb_zero, 1)
            pool.wait_ge(maccb_zero, 1)
            pool.dma_start(macc_b[0:1, :], A["b_ada"][:, 2 * D:6 * D]).then_inc(bb_in, 16)

            def gather(j):
                wait_reg(pool, idx_ready, j + 1)
                wait_reg(pool, hg_t, j, 0)
                g.indirect_dma_start(out=hg, out_offset=None, in_=hf_dram,
                                     in_offset=bass.IndirectOffsetOnAxis(ap=tok_idx[:, 0:1], axis=0),
                                     bounds_check=SEQ - 1, oob_is_err=False).then_inc(gathered, 16)

            def scatter(j):
                wait_reg(pool, y_ready, j + 1)
                wait_reg(pool, dest_ready, j + 1)
                g.indirect_dma_start(out=y_dram, out_offset=bass.IndirectOffsetOnAxis(ap=dest_now[:, 0:1], axis=0),
                                     in_=y, in_offset=None, bounds_check=2 * SEQ,
                                     oob_is_err=False).then_inc(scattered, 16)

            pool.wait_ge(row_ready, 4)
            for t in range(NT):
                pool.wait_ge(hf_scaled, t + 1)
                g.tensor_tensor(hf[:, t, :], hf[:, t, :], shf, ALU.add).then_inc(hf_ready, 1)
            pool.wait_ge(hf_saved, 16 * NT)
            pool.wait_ge(logits_mm, NT)
            g.memset(hg, 0.0).then_inc(hg_zero, 1)
            pool.wait_ge(hg_zero, 1)
            for j in range(3):
                gather(j)
            scatter(0)
            gather(3)
            with pool.Fori(2, 14) as i:
                scatter(i - 1)
                gather(i + 2)
            pool.wait_ge(tiles_ready, 1)
            tiles = pool.value_load(expert_of[0:1, 31:32], min_val=0, max_val=7) + E
            with pool.Fori(14, tiles - 1) as i:
                scatter(i - 1)
                gather(i + 2)
            scatter(tiles - 2)
            scatter(tiles - 1)
            wait_reg(pool, gathered, tiles * 16 + 16)
            wait_reg(pool, scattered, tiles * 16)
            for t in range(NT):
                pool.wait_ge(y_in[t], 16)
                g.tensor_tensor(raw[:, t, 0:D], raw[:, t, 0:D], raw[:, t, D:2 * D], ALU.add).then_inc(y_sum, 1)

        @block.scalar
        def _(act):
            A_ = nc.scalar.activation
            def hi(n, slot, count, used=None):
                act.wait_ge(landed[slot], count)
                if used is not None:
                    act.wait_ge(chunk_used, used)
                A_(wsplit[:, n, 0, :], raw[:, slot, :], ACT.Copy).then_inc(hi_ready, 1)

            act.wait_ge(cols_ready, 1)
            A_(c_silu[:, :], cols[:, 0:ND], ACT.Silu).then_inc(c_ready, 1)
            for t in range(NT):
                act.wait_ge(x_in[t], 16)
                if t:
                    act.wait_ge(squares, t)
                A_(raw[:, 5, 0:D], x_tiles[:, t, :], ACT.Square, accum_out=stats[:, t:t + 1]).then_inc(squares, 1)
            for i in range(RAW_ADA // 2):
                act.wait_ge(mod_used, i + 1)
                if i:
                    act.wait_ge(mod_mm, i)
                A_(mod_row, ps[0:1, 7, CC:2 * CC], ACT.Copy).then_inc(mod_row_ready, 1)
                if i == 1:
                    act.wait_ge(ws_t, 1)
                    A_(wsT, ps[:, 5:7, :].rearrange("p b n -> p (b n)"), ACT.Copy).then_inc(ws_ready, 1)
            hi(0, *raw_place(0))
            for k in range(ND):
                act.wait_ge(h_aff, k + 1)
                A_(hT[:, 0, k, :], ps[:, k, :], ACT.Copy).then_inc(h_hi, 1)
                if k == 3:
                    hi(1, *raw_place(1))
            act.wait_ge(ws_ready, 1)
            act.dma_start(bsb, A["sgu_b"][0].rearrange("h i -> (h i)").partition_broadcast(P)).then_inc(bsb_in, 16)
            act.dma_start(router[:, :, :], A["router_w"].rearrange("(k p) e -> p k e", p=P)).then_inc(router_in, 16)
            act.dma_start(bias_row[:, :], A["router_bias"].partition_broadcast(P)).then_inc(bias_in, 16)
            for n in range(V0, G0):
                if n >= 1:
                    s, count = raw_place(n + 1) if n + 1 < G0 else (0, 16 * (RAW_G // RING_A + 1))
                    hi((n + 1) % 2, s, count, n)
                if n < U0 and n % 2:
                    act.wait_ge(chunk_used, n + 1)
                    for t in range(NT):
                        b = 4 * (n // 2) + t
                        A_(v[:, t * D + (n // 2) * 512:t * D + (n // 2) * 512 + 512], ps[:, b, :],
                           ACT.Gelu_apprx_tanh, accum_out=stats[:, 8 + b:9 + b]).then_inc(v_gelu, 1)
                if n == U0:
                    for t in range(NT):
                        act.wait_ge(v_centred, t + 1)
                        if t:
                            act.wait_ge(v_square, t)
                        A_(wsplit[:, 2, 0, 0:D], v[:, t * D:(t + 1) * D], ACT.Square,
                           accum_out=stats[:, 20 + t:21 + t]).then_inc(v_square, 1)
                if U0 <= n < P0:
                    act.wait_ge(chunk_used, n + 1)
                    for m in range(2 * (n - U0), 2 * (n - U0) + 2):
                        if m == 0:
                            act.wait_ge(xT_t, ND)
                        A_(u[:, m, :], ps[:, m, :], ACT.Gelu_apprx_tanh).then_inc(u_ready, 1)
                if n == P0:
                    for h in range(NH):
                        act.wait_ge(ya_f, h + 1)
                        if h == 0:
                            act.wait_ge(v_square, NT)
                        A_(ya[:, 0, h, :], u[:, h, :], ACT.Copy).then_inc(ya_hi, 1)
                if n > P0 + 1:
                    mix_hi(act, A_, n - P0 - 2)
            mix_hi(act, A_, 2)
            mix_hi(act, A_, 3)
            with act.Fori(0, 4) as q:
                def hi_next(j):
                    act.wait_ge(landed[(j + 1) % 4], (q * 2 + (RAW_G // 4 + 1 + (2 if j == 3 else 0))) * 16)
                    act.wait_ge(chunk_used, q * 4 + (G0 + j))
                    A_(wsplit[:, (j + 1) % 2, 0, :], raw[:, (j + 1) % 4, :], ACT.Copy).then_inc(hi_ready, 1)

                hi_next(0)
                act.wait_ge(chunk_used, q * 4 + (G0 + 1))
                for b in range(2):
                    A_(sig_a[:, b, :], ps[:, b, :], ACT.Sigmoid).then_inc(gate_ready, 1)
                hi_next(1)
                hi_next(2)
                act.wait_ge(chunk_used, q * 4 + (G0 + 3))
                for b in range(2):
                    A_(sig_b[:, b, :], ps[:, 4 + b, :], ACT.Sigmoid).then_inc(gate_ready, 1)
                hi_next(3)
            act.wait_ge(chunk_used, G0 + 15)
            act.wait_ge(merge_b, ND)
            for k in range(ND):
                A_(hT[:, 0, k, :], merged[:, k, :], ACT.Copy).then_inc(m_hi, 1)
            for n in range(O0 + 1, O0 + 4):
                hi(split_slot(n), *raw_place(n), min(n - 1, O0 + 1))
            for c in range(2):
                hi(c + 2, c + 2, 16 * (RAW_O // 4 + 2), G0 + 16)
            for t in range(NT):
                act.wait_ge(x2_half, 2 * t + 2)
                A_(hf[:, t, :], x_tiles[:, t, :], ACT.Square, accum_out=stats[:, 24 + t:25 + t]).then_inc(sq2, 1)
                if t:
                    turned(act, A_, t - 1)
            turned(act, A_, NT - 1)
            act.wait_ge(sub_ready, 1)
            A_(r_p, r_d, ACT.Exp).then_inc(expd, 1)
            for c in range(2):
                hi(c + 4, c + 4, 16, M0)

            def rows_hi(j):
                act.wait_ge(hg_t, j + 1)
                A_(hgT[:, 0, :, :].rearrange("p k m -> p (k m)"), ps[:, 2:4, :].rearrange("p b n -> p (b n)"),
                   ACT.Copy).then_inc(hg_hi, 1)

            def silu(i, gate_used):
                act.wait_ge(chunk_used, gate_used)
                act.wait_ge(a_ready, i)
                A_(act_g, ps[:, 0, :], ACT.Silu).then_inc(silu_ready, 1)

            def a_hi(i):
                act.wait_ge(a_trans, i + 1)
                A_(aT[:, 0, :, :].rearrange("p k m -> p (k m)"), ps[:, 4, :], ACT.Copy).then_inc(aT_hi, 1)

            def tile(i, gate_used):
                def hi_c(c):
                    act.wait_ge(landed[c], (i + (2, 2, 3, 3, 2, 2)[c] + (13 if c < 4 else 0)) * 16)
                    act.wait_ge(chunk_used, i * 6 + (31 + c))
                    A_(wsplit[:, c, 0, :], raw[:, c, :], ACT.Copy).then_inc(hi_ready, 1)

                hi_c(0)
                hi_c(1)
                silu(i, gate_used)
                hi_c(2)
                hi_c(3)
                rows_hi(i + 1)
                hi_c(4)
                hi_c(5)
                a_hi(i)

            rows_hi(0)
            tile(0, M0 + 2)
            tile(1, 6 + 32)
            with act.Fori(2, 14) as i:
                tile(i, i * 6 + 32)
            act.wait_ge(tiles_ready, 1)
            tiles = act.value_load(expert_of[0:1, 31:32], min_val=0, max_val=7) + E
            with act.Fori(14, tiles - 1) as i:
                tile(i, i * 6 + 32)
            silu(tiles - 1, tiles * 6 + 26)
            for c in range(2):
                act.wait_ge(landed[c], tiles * 16 + 14 * 16)
                act.wait_ge(chunk_used, tiles * 6 + (25 + c))
                A_(wsplit[:, c, 0, :], raw[:, c, :], ACT.Copy).then_inc(hi_ready, 1)
            a_hi(tiles - 1)
            for t in range(NT):
                act.wait_ge(fin_x, t + 1)
                A_(raw[:, t, 0:D], x_tiles[:, t, :], ACT.Square, accum_out=stats[:, 28 + t:29 + t]).then_inc(fin_sq, 1)

        @block.vector
        def _(dve):
            V = nc.vector
            steps = [0]

            def step(ins):
                steps[0] += 1
                ins.then_inc(chain, 1)

            def done():
                dve.wait_ge(chain, steps[0])

            def lo(n, slot):
                V.tensor_tensor(wsplit[:, n, 1, :], raw[:, slot, :], wsplit[:, n, 0, :].bitcast(F32),
                                ALU.subtract).then_inc(lo_ready, 1)

            def lo_n(n, slot):
                dve.wait_ge(hi_ready, n + 1)
                lo(split_slot(n), slot)

            def inv_rms(col, n):
                m, yv, sq = stats[:, col:col + n], nrm[:, 0:n], nrm[:, NT:NT + n]
                yi, mi = nrm[:, 0:n].bitcast(I32), m.bitcast(I32)
                step(V.tensor_scalar(m, m, 1.0 / D, EPS, ALU.mult, ALU.add))
                done()
                step(V.tensor_scalar(yi, mi, 1, None, ALU.logical_shift_right))
                done()
                step(V.tensor_scalar(yi, yi, -1.0, float(0x5F3759DF), ALU.mult, ALU.add))
                done()
                for last in (False, False, True):
                    step(V.tensor_tensor(sq, yv, yv, ALU.mult))
                    done()
                    step(V.scalar_tensor_tensor(out=sq, in0=sq, scalar=-0.5, in1=m, op0=ALU.mult, op1=ALU.mult))
                    done()
                    step(V.scalar_tensor_tensor(out=m if last else yv, in0=sq, scalar=1.5, in1=yv,
                                                op0=ALU.add, op1=ALU.mult))
                    done()

            def inv_rms_1(col):
                m, z = stats[:, col:col + 1], nrm[:, 0:1]
                zi = z.bitcast(I32)
                powers = [nrm[:, NT + j:NT + j + 1] for j in range(3)]
                for j in range(3):
                    f = 4.0 ** (3 - j)
                    step(V.tensor_scalar(powers[j], m, f / D, f * EPS, ALU.mult, ALU.add))
                done()
                step(V.tensor_scalar(zi, powers[2].bitcast(I32), -0.5,
                                     float(0x5F3759DF - (2 << 23) - (1 << 31)), ALU.mult, ALU.add))
                done()
                for j in range(3):
                    step(V.scalar_tensor_tensor(out=nrm[:, 2 * NT:2 * NT + 1], in0=z, scalar=powers[j], in1=z,
                                                op0=ALU.mult, op1=ALU.mult))
                    done()
                    step(V.scalar_tensor_tensor(out=m if j == 2 else z, in0=nrm[:, 2 * NT:2 * NT + 1],
                                                scalar=-3.0, in1=z, op0=ALU.add, op1=ALU.mult))
                    done()

            def ada(acc, slot, a):
                for k in range(ND):
                    ins = V.scalar_tensor_tensor(out=acc, in0=raw[:, slot, k * CC:(k + 1) * CC],
                                                 scalar=c_silu[:, k:k + 1], in1=acc, op0=ALU.mult, op1=ALU.add)
                    if k < ND - 1:
                        ins.then_inc(ada_step, 1)
                        dve.wait_ge(ada_step, a * (ND - 1) + (k + 1))
                    else:
                        ins.then_inc(ada_used, 1)

            dve.wait_ge(cols_t, 1)
            V.tensor_copy(cols[:, :], ps[:, 7, 32:80]).then_inc(cols_ready, 1)
            dve.wait_ge(c_ready, 1)
            for i in range(RAW_ADA // 2):
                r = 2 * i
                dve.wait_ge(landed[r % RING_A], 16 * (r // RING_A + 1))
                step(V.tensor_tensor(ada_prod, raw[:, r % RING_A, :].rearrange("p (k n) -> p k n", k=ND),
                                     c_silu[:, :].unsqueeze(2).broadcast_to([P, ND, CC]), ALU.mult))
                done()
                V.tensor_reduce(macc_a[:, i * CC:(i + 1) * CC], ada_prod.rearrange("p k n -> p n k"), AX_X,
                                ALU.add).then_inc(ada_used, 1)
                dve.wait_ge(ada_used, i + 1)
                if i == 0:
                    dve.wait_ge(squares, NT)
                    inv_rms(0, NT)
                    for t in range(NT):
                        V.tensor_scalar(x_tiles[:, t, :], x_tiles[:, t, :], stats[:, t:t + 1], None,
                                        ALU.mult).then_inc(xhat_ready, 1)
            dve.wait_ge(consts, 2)
            step(V.reciprocal(inv_count[:, :], iota1[:, 0:16]))
            dve.wait_ge(mod_mm, RAW_ADA // 2)
            step(V.tensor_tensor(mod_cols[:, :], ps[:, 7, 0:16], cols[:, 32:48], ALU.add))
            done()
            V.scalar_tensor_tensor(out=gain[:, :], in0=mod_cols[:, 8:16], scalar=1.0, in1=cols[:, 8:16],
                                   op0=ALU.add, op1=ALU.mult).then_inc(gain_ready, 1)
            dve.wait_ge(gain_ready, 1)
            for k in range(ND + 1):
                if k < ND:
                    dve.wait_ge(xT_t, k + 1)
                    V.tensor_scalar(ps[:, k, :], ps[:, k, :], gain[:, k:k + 1], mod_cols[:, k:k + 1],
                                    ALU.mult, ALU.add).then_inc(h_aff, 1)
                if k:
                    dve.wait_ge(h_hi, k)
                    V.tensor_tensor(hT[:, 1, k - 1, :], ps[:, k - 1, :], hT[:, 0, k - 1, :].bitcast(F32),
                                    ALU.subtract).then_inc(h_lo, 1)
                if k == 0:
                    lo_n(0, 0)
                if k == 5:
                    lo_n(1, 1)

            for n in range(V0, G0):
                if n >= 1:
                    lo_n(n + 1, (RAW_V + n + 1) % RING_A)
                if n == U0:
                    dve.wait_ge(v_gelu, 2 * NT)
                    step(V.tensor_tensor(stats[:, 16:20], stats[:, 8:12], stats[:, 12:16], ALU.add))
                    done()
                    step(V.tensor_scalar(stats[:, 16:20], stats[:, 16:20], 1.0 / D, None, ALU.mult))
                    done()
                    for t in range(NT):
                        V.tensor_scalar(v[:, t * D:(t + 1) * D], v[:, t * D:(t + 1) * D], stats[:, 16 + t:17 + t],
                                        None, ALU.subtract).then_inc(v_centred, 1)
                    dve.wait_ge(v_square, NT)
                    inv_rms(20, NT)
                    for t in range(NT):
                        V.tensor_scalar(v[:, t * D:(t + 1) * D], v[:, t * D:(t + 1) * D], stats[:, 20 + t:21 + t],
                                        None, ALU.mult).then_inc(v_ready, 1)
                if n == P0:
                    dve.wait_ge(bsb_in, 16)
                    for h in range(NH):
                        dve.wait_ge(s_mm, h + 1)
                        dve.wait_ge(u_ready, h + 1)
                        s_h = ps[:, h, :].rearrange("p (c i) -> p c i", c=NT)
                        b_h = bsb[:, h * P:(h + 1) * P].unsqueeze(1).broadcast_to([P, NT, P])
                        step(V.scalar_tensor_tensor(out=s_h, in0=s_h, scalar=cols[:, 16 + h:17 + h], in1=b_h,
                                                    op0=ALU.mult, op1=ALU.add))
                        done()
                        V.tensor_tensor(u[:, h, :], ps[:, h, :], u[:, h, :], ALU.mult).then_inc(ya_f, 1)
                        if h:
                            dve.wait_ge(ya_hi, h)
                            V.tensor_tensor(ya[:, 1, h - 1, :], u[:, h - 1, :], ya[:, 0, h - 1, :].bitcast(F32),
                                            ALU.subtract).then_inc(ya_lo, 1)
                    dve.wait_ge(ya_hi, NH)
                    V.tensor_tensor(ya[:, 1, NH - 1, :], u[:, NH - 1, :], ya[:, 0, NH - 1, :].bitcast(F32),
                                    ALU.subtract).then_inc(ya_lo, 1)
                    dve.wait_ge(ya_lo, NH)
                    step(V.memset(z[:, 0:16], 0.0))
                    done()
                if n >= P0:
                    i = n - P0
                    w = WINDOWS[3 - i]
                    dve.wait_ge(chunk_used, n + 1)
                    if i >= 2:
                        dve.wait_ge(mix_mm, 2 * (i - 1))
                    for j in range(2):
                        step(V.tensor_copy(z[:, 16:], ps[:, 2 * i + j, :]))
                        done()
                        src, d, turn = z, 1, 0
                        while d < w:
                            dst = (win_a, win_b)[turn]
                            lo_col = 2 * d - 1
                            step(V.tensor_tensor(dst[:, lo_col:], src[:, lo_col:], src[:, lo_col - d:16 + SEQ - d],
                                                 ALU.add))
                            done()
                            src, d, turn = dst, 2 * d, 1 - turn
                        out_j = pooled[:, i % 2, j, :]
                        step(V.scalar_tensor_tensor(out=out_j, in0=src[:, 16:], scalar=1.0 / w, in1=z[:, 16:],
                                                    op0=ALU.mult, op1=ALU.subtract))
                        done()
                        step(V.tensor_tensor(src[:, 16:16 + w - 1], src[:, 16:16 + w - 1], inv_count[:, 0:w - 1],
                                             ALU.mult))
                        done()
                        V.tensor_tensor(out_j[:, 0:w - 1], src[:, 16:16 + w - 1], z[:, 16:16 + w - 1],
                                        ALU.subtract).then_inc(pooled_ready, 1)
                        dve.wait_ge(pooled_ready, 2 * i + j + 1)
                if n > P0 + 1:
                    mix_lo(dve, V, n - P0 - 2)
            mix_lo(dve, V, 2)
            mix_lo(dve, V, 3)
            dve.wait_ge(mix_mm, NH)
            dve.wait_ge(bb_in, 16)
            with dve.Fori(0, 4) as q:
                def lo_next(j):
                    dve.wait_ge(hi_ready, q * 4 + (G0 + j + 2))
                    lo((j + 1) % 2, (j + 1) % 4)

                def ada_next(j):
                    dve.wait_ge(landed[j], (q * 2 + (RAW_G // 4 + 2)) * 16)
                    ada(macc_b[:, ds(q * (4 * CC) + j * CC, CC)], j, q * 4 + j)

                lo_next(0)
                ada_next(0)
                lo_next(1)
                dve.wait_ge(chunk_used, q * 4 + (G0 + 2))
                dve.wait_ge(gate_ready, q * 4 + 2)
                for b in range(2):
                    V.tensor_tensor(merged[:, ds(q * 2 + b, 1), :].rearrange("p a n -> p (a n)"), ps[:, 2 + b, :],
                                    sig_a[:, b, :], ALU.mult).then_inc(merge_a, 1)
                ada_next(1)
                lo_next(2)
                ada_next(2)
                ada_next(3)
                lo_next(3)
                dve.wait_ge(chunk_used, q * 4 + (G0 + 4))
                dve.wait_ge(gate_ready, q * 4 + 4)
                for b in range(2):
                    V.tensor_tensor(ps[:, 6 + b, :], ps[:, 6 + b, :], sig_b[:, b, :], ALU.mult).then_inc(merge_t, 1)
                for b in range(2):
                    dve.wait_ge(merge_t, q * 2 + (b + 1))
                    dve.wait_ge(merge_a, q * 2 + 2)
                    m_t = merged[:, ds(q * 2 + b, 1), :].rearrange("p a n -> p (a n)")
                    V.tensor_tensor(m_t, ps[:, 6 + b, :], m_t, ALU.add).then_inc(merge_b, 1)
            for k in range(ND):
                dve.wait_ge(m_hi, k + 1)
                V.tensor_tensor(hT[:, 1, k, :], merged[:, k, :], hT[:, 0, k, :].bitcast(F32),
                                ALU.subtract).then_inc(m_lo, 1)
            dve.wait_ge(lo_ready, O0 + 1)
            for b in range(4):
                dve.wait_ge(row_mm, b + 1)
                dst = gm if b < 2 else shf
                V.tensor_copy(dst[:, (b % 2) * 512:(b % 2) * 512 + 512], ps[:, 4 + b, :]).then_inc(row_ready, 1)
            lo_n(O0 + 1, 1)
            dve.wait_ge(gff_in, 16)
            for b in range(4):
                dve.wait_ge(row_mm, b + 5)
                c = slice((b % 2) * 512, (b % 2) * 512 + 512)
                if b < 2:
                    ins = V.scalar_tensor_tensor(out=gff[:, c], in0=ps[:, 4 + b, :], scalar=1.0, in1=gff[:, c],
                                                 op0=ALU.add, op1=ALU.mult)
                else:
                    ins = V.tensor_copy(gf[:, c], ps[:, 4 + b, :])
                ins.then_inc(row_ready, 1)
            lo_n(O0 + 2, 2)
            dve.wait_ge(x_again, 16)
            dve.wait_ge(row_ready, 8)

            def residual(t, half):
                b = 4 * half + t
                step(V.tensor_tensor(ps[:, b, :], ps[:, b, :], gm[:, half * 512:half * 512 + 512], ALU.mult))
                done()
                x_h = x_tiles[:, t, half * 512:half * 512 + 512]
                V.tensor_tensor(x_h, ps[:, b, :], x_h, ALU.add).then_inc(x2_half, 1)

            def normed(t):
                dve.wait_ge(sq2, t + 1)
                inv_rms_1(24 + t)
                V.scalar_tensor_tensor(out=hf[:, t, :], in0=x_tiles[:, t, :], scalar=stats[:, 24 + t:25 + t],
                                       in1=gff, op0=ALU.mult, op1=ALU.mult).then_inc(hf_scaled, 1)

            lo_n(O0 + 3, 3)
            for c in range(2):
                lo_n(M0 + c, c + 2)
            for t in range(NT):
                for half in range(2):
                    if t < NT - 1:
                        dve.wait_ge(o_tile, 2 * t + half + 1)
                    else:
                        dve.wait_ge(chunk_used, M0 - 1 + half)
                    residual(t, half)
                if t:
                    normed(t - 1)
            normed(NT - 1)
            dve.wait_ge(consts, 2)
            step(V.tensor_scalar(r_4c, tok_f[:, :], 2.0, 1.0 - SKIP, ALU.mult, ALU.add))
            step(V.tensor_scalar(info[:, :, :, 0], tok_f[:, :].unsqueeze(2).broadcast_to([P, NT, E]), float(-SKIP), None,
                                 ALU.add))
            step(V.memset(r_m_all[:, NT * E:], 0.0))

            lg = ps[:, 4, 0:NT * E].rearrange("p (t e) -> p t e", t=NT)
            te = [P, NT, E]
            dve.wait_ge(logits_mm, NT)
            step(V.tensor_reduce(r_4, lg, AX_X, ALU.max))
            done()
            V.tensor_tensor(r_d3, lg, r_4.unsqueeze(2).broadcast_to(te), ALU.subtract).then_inc(sub_ready, 1)
            dve.wait_ge(expd, 1)
            step(V.tensor_reduce(r_4, r_p3, AX_X, ALU.add))
            done()
            step(V.reciprocal(r_4, r_4))
            done()
            step(V.tensor_tensor(r_p3, r_p3, r_4.unsqueeze(2).broadcast_to(te), ALU.mult))
            done()
            dve.wait_ge(bias_in, 16)
            step(V.tensor_tensor(r_sel3, r_p3, bias_row[:, :].unsqueeze(1).broadcast_to(te), ALU.add))
            done()

            def rank(values, n, result):
                pair = [P, n, EG, EG]
                mine = values.unsqueeze(3).broadcast_to(pair)
                other = values.unsqueeze(2).broadcast_to(pair)
                step(V.tensor_tensor(r_ge[:, 0:n], other, mine, ALU.is_ge))
                step(V.tensor_tensor(r_gt[:, 0:n], other, mine, ALU.is_gt))
                done()
                step(V.tensor_tensor(r_ge[:, 0:n], r_ge[:, 0:n],
                                     order[:, 0, :, :].unsqueeze(1).broadcast_to(pair), ALU.mult))
                step(V.tensor_tensor(r_gt[:, 0:n], r_gt[:, 0:n],
                                     order[:, 1, :, :].unsqueeze(1).broadcast_to(pair), ALU.mult))
                done()
                step(V.tensor_tensor(r_ge[:, 0:n], r_ge[:, 0:n], r_gt[:, 0:n], ALU.add))
                done()
                step(V.tensor_reduce(result, r_ge[:, 0:n], AX_X, ALU.add))
                done()

            ge3 = [P, NT * EG, EG]
            sel_g = r_sel.rearrange("p (g e) -> p g e", e=EG)
            top_g = r_top.rearrange("p (g e) -> p g e", e=EG)
            rank(sel_g, NT * EG, top_g)
            step(V.tensor_scalar(r_top, r_top, 2.0, None, ALU.is_lt))
            done()
            step(V.tensor_tensor(r_m, r_sel, r_top, ALU.mult))
            done()
            step(V.tensor_reduce(r_gs, r_m.rearrange("p (g e) -> p g e", e=EG), AX_X, ALU.add))
            done()
            rank(r_gs.rearrange("p (t g) -> p t g", t=NT), NT, r_gr.rearrange("p (t g) -> p t g", t=NT))
            step(V.tensor_scalar(r_gr, r_gr, 1.0, None, ALU.is_lt))
            done()
            V.tensor_tensor(r_m.rearrange("p (g e) -> p g e", e=EG), top_g,
                            r_gr.unsqueeze(2).broadcast_to(ge3), ALU.mult).then_inc(mask_ready, 1)
            dve.wait_ge(mask_ready, 1)
            step(V.tensor_tensor(r_p, r_p, r_m, ALU.mult))
            step(V.tensor_tensor(r_d3, r_m3, iota1[:, 0:E].unsqueeze(1).broadcast_to(te), ALU.mult))
            done()
            step(V.tensor_reduce(r_4, r_p3, AX_X, ALU.add))
            step(V.tensor_reduce(r_4b, r_d3, AX_X, ALU.max))
            done()
            step(V.reciprocal(r_4, r_4))
            step(V.tensor_tensor(r_d3, r_d3, r_4b.unsqueeze(2).broadcast_to(te), ALU.is_equal))
            done()
            step(V.tensor_tensor(info[:, :, :, 1], r_p3, r_4.unsqueeze(2).broadcast_to(te), ALU.mult))
            step(V.tensor_tensor(info[:, :, :, 2], r_d3, r_4c.unsqueeze(2).broadcast_to(te), ALU.add))
            dve.wait_ge(pos_mm, 1)
            step(V.scalar_tensor_tensor(out=pos1[:, :, :], in0=ps[:, 2, 0:NT * E].rearrange("p (t e) -> p t e", t=NT),
                                        scalar=1.0, in1=r_m3, op0=ALU.add, op1=ALU.mult))
            step(V.tensor_copy(r_cnt, ps[:, 2, NT * E:NT * E + E]))
            done()

            def select(j, e):
                dve.wait_ge(idx_mm, j)
                for t in range(NT):
                    ins = V.tensor_scalar(sel[:, t, :], iota1[:, :], base[:, ds(j, 1)], pos1[:, t, ds(e, 1)],
                                          ALU.add, ALU.is_equal)
                ins.then_inc(sel_ready, 1)

            def indices(j):
                dve.wait_ge(idx_mm, j + 1)
                dve.wait_ge(gathered, j * 16)
                V.tensor_scalar(tok_idx[:, :], ps[:, 7, 0:1], float(SKIP), None, ALU.add)
                V.tensor_copy(row_w[:, ds(j, 1)], ps[:, 7, 1:2])
                V.tensor_scalar(row_dest[:, ds(j, 1)], ps[:, 7, 2:3], float(SKIP), None,
                                ALU.add).then_inc(idx_ready, 1)

            def rows_lo(j):
                dve.wait_ge(hg_hi, j + 1)
                V.tensor_tensor(hgT[:, 1, :, :].rearrange("p k m -> p (k m)"),
                                ps[:, 2:4, :].rearrange("p b n -> p (b n)"),
                                hgT[:, 0, :, :].rearrange("p k m -> p (k m)").bitcast(F32),
                                ALU.subtract).then_inc(hg_lo, 1)

            select(0, 0)
            step(V.tensor_scalar(r_x, r_cnt, float(P), None, ALU.is_gt))
            step(V.tensor_scalar(r_x2, r_cnt, float(2 * P), None, ALU.is_gt))
            step(V.tensor_scalar(r_x3, r_cnt, float(3 * P), None, ALU.is_gt))
            done()
            indices(0)
            select(1, 1)
            step(V.tensor_tensor(r_x, r_x, r_x2, ALU.add))
            done()
            step(V.tensor_tensor(r_x, r_x, r_x3, ALU.add))
            done()
            step(V.tensor_tensor_scan(r_cum, ones[:, 0:E], r_x, 0.0, ALU.mult, ALU.add))
            done()
            ke = [P, 8, E]
            indices(1)
            lo_n(M0 + 2, 4)
            rows_lo(0)
            lo_n(M0 + 3, 5)
            step(V.tensor_tensor(r_le, iota1[:, 0:8].unsqueeze(2).broadcast_to(ke),
                                 r_cum.unsqueeze(1).broadcast_to(ke), ALU.is_gt))
            done()
            step(V.tensor_reduce(r_8, r_le, AX_X, ALU.add))
            done()
            step(V.tensor_tensor(r_le, r_le, r_cum.unsqueeze(1).broadcast_to(ke), ALU.mult))
            done()
            step(V.tensor_scalar(expert_of[:, E:E + 8], r_8, float(E - 1), None, ALU.min))
            step(V.tensor_reduce(r_8b, r_le, AX_X, ALU.max))
            done()
            step(V.tensor_tensor(r_8b, iota1[:, 0:8], r_8b, ALU.subtract))
            done()
            step(V.tensor_scalar(base[:, E:E + 8], r_8b, float(P), None, ALU.mult))
            V.tensor_copy(expert_of[:, 31:32], r_cum[:, E - 1:E]).then_inc(tiles_ready, 1)
            dve.wait_ge(tiles_ready, 1)

            def hidden(i, up_used):
                dve.wait_ge(silu_ready, i + 1)
                dve.wait_ge(chunk_used, up_used)
                dve.wait_ge(a_trans, i)
                V.tensor_tensor(a_t, ps[:, 1, :], act_g, ALU.mult).then_inc(a_ready, 1)

            def a_lo(i):
                dve.wait_ge(aT_hi, i + 1)
                V.tensor_tensor(aT[:, 1, :, :].rearrange("p k m -> p (k m)"), ps[:, 4, :],
                                aT[:, 0, :, :].rearrange("p k m -> p (k m)").bitcast(F32),
                                ALU.subtract).then_inc(aT_lo, 1)

            def destination(j):
                dve.wait_ge(idx_ready, j + 1)
                dve.wait_ge(scattered, j * 16)
                V.tensor_copy(dest_now[:, :], row_dest[:, ds(j, 1)]).then_inc(dest_ready, 1)

            def results(j, used):
                dve.wait_ge(chunk_used, used)
                dve.wait_ge(idx_ready, j + 1)
                dve.wait_ge(scattered, j * 16)
                V.scalar_tensor_tensor(out=y, in0=ps[:, 5:7, :].rearrange("p b n -> p (b n)"),
                                       scalar=row_w[:, ds(j, 1)], in1=gf, op0=ALU.mult,
                                       op1=ALU.mult).then_inc(y_ready, 1)

            def tile(i, e2, up_used, prev, down_used=None):
                def lo_c(c):
                    dve.wait_ge(hi_ready, i * 6 + (37 + c))
                    lo(c, c)

                lo_c(0)
                lo_c(1)
                select(i + 2, e2)
                lo_c(2)
                hidden(i, up_used)
                lo_c(3)
                rows_lo(i + 1)
                lo_c(4)
                lo_c(5)
                if prev:
                    destination(i - 1)
                a_lo(i)
                indices(i + 2)
                if prev:
                    results(i - 1, down_used)

            tile(0, 2, M0 + 4, False)
            tile(1, 3, 6 + 34, True, 6 + 36)
            with dve.Fori(2, 14) as i:
                tile(i, i + 2, i * 6 + 34, True, i * 6 + 36)
            tiles = dve.value_load(expert_of[0:1, 31:32], min_val=0, max_val=7) + E
            with dve.Fori(14, tiles - 1) as i:
                e2 = dve.value_load(expert_of[0:1, ds(i + 2, 1)], min_val=0, max_val=E - 1)
                tile(i, e2, i * 6 + 34, True, i * 6 + 36)
            hidden(tiles - 1, tiles * 6 + 28)
            for c in range(2):
                dve.wait_ge(hi_ready, tiles * 6 + (31 + c))
                lo(c, c)
            destination(tiles - 2)
            a_lo(tiles - 1)
            results(tiles - 2, tiles * 6 + 30)
            destination(tiles - 1)
            results(tiles - 1, tiles * 6 + 32)
            for t in range(NT):
                dve.wait_ge(y_sum, t + 1)
                V.tensor_tensor(x_tiles[:, t, :], x_tiles[:, t, :], raw[:, t, 0:D], ALU.add).then_inc(fin_x, 1)
                if t:
                    final(dve, V, inv_rms_1, t - 1)
            final(dve, V, inv_rms_1, NT - 1)

        @block.tensor
        def _(pe):
            def three(out, w_hi, w_lo, m_hi_, m_lo_, first, last):
                nc.tensor.matmul(out, w_hi, m_hi_, start=first, stop=False)
                nc.tensor.matmul(out, w_hi, m_lo_, start=False, stop=False)
                return nc.tensor.matmul(out, w_lo, m_hi_, start=False, stop=last)

            pe.wait_ge(consts, 1)
            pe.wait_ge(rows_in, 80)
            nc.tensor.transpose(ps[:, 7, 32:80], rows_c, ident[0:48, 0:48]).then_inc(cols_t, 1)

            def mod_row_products(i):
                r = 2 * i + 1
                pe.wait_ge(landed[r % RING_A], 16 * (r // RING_A + 1))
                if i == 0:
                    pe.wait_ge(c_ready, 1)
                    pe.wait_ge(cols_ready, 1)
                else:
                    pe.wait_ge(mod_row_ready, i)
                for k in range(ND):
                    mm = nc.tensor.matmul(ps[0:1, 7, CC:2 * CC], c_silu[:, k:k + 1],
                                          raw[:, r % RING_A, k * CC:(k + 1) * CC], start=(k == 0), stop=(k == ND - 1))
                mm.then_inc(mod_used, 1)

            def mod_columns(i):
                pe.wait_ge(ada_used, i + 1)
                pe.wait_ge(mod_row_ready, i + 1)
                for m in range(2):
                    nc.tensor.matmul(ps[:, 7, 4 * i + m:4 * i + m + 1],
                                     macc_a[:, i * CC + m * P:i * CC + (m + 1) * P], ones[:, 0:1],
                                     start=True, stop=True)
                for m in range(2):
                    mm = nc.tensor.matmul(ps[:, 7, 4 * i + 2 + m:4 * i + 3 + m], mod_row[:, m * P:(m + 1) * P],
                                          ones[0:1, 0:1], start=True, stop=True)
                mm.then_inc(mod_mm, 1)

            def x_turn(k):
                for t in range(NT):
                    mm = nc.tensor.transpose(ps[:, k, t * P:(t + 1) * P], x_tiles[:, t, k * P:(k + 1) * P],
                                             ident[:, :])
                mm.then_inc(xT_t, 1)

            mod_row_products(0)
            mod_columns(0)
            mod_row_products(1)
            pe.wait_ge(causal, 1)
            for h in range(NH):
                mm = nc.tensor.transpose(ps[:, 5 + h // 4, (h % 4) * P:(h % 4 + 1) * P], wnat[:, h * P:(h + 1) * P],
                                         ident[:, :])
            mm.then_inc(ws_t, 1)
            pe.wait_ge(xhat_ready, NT)
            for k in range(5):
                x_turn(k)
            mod_columns(1)
            mod_row_products(2)
            pe.wait_ge(ws_ready, 1)
            x_turn(5)
            x_turn(6)
            mod_columns(2)
            mod_row_products(3)
            mod_columns(3)
            pe.wait_ge(gain_ready, 1)
            x_turn(7)

            def wblock(s, part, k, width):
                return wsplit[:, s, part, k * width:(k + 1) * width]

            def by_token(n, stationary, bank):
                s, kh = split_slot(n), n % 2
                for t in range(NT):
                    for k in range(4):
                        kk = 4 * kh + k
                        if n == V0 and t == 0:
                            pe.wait_ge(h_lo, k + 1)
                        mm = three(ps[:, bank + t, :],
                                   stationary[:, 0, kk, t * P:(t + 1) * P], stationary[:, 1, kk, t * P:(t + 1) * P],
                                   wblock(s, 0, k, 512), wblock(s, 1, k, 512), kk == 0, kk == ND - 1)
                mm.then_inc(chunk_used, 1)

            def by_feature(s, moving, bank):
                for m in range(2):
                    for k in range(ND):
                        col = k * CC + m * P
                        w_hi, w_lo = wsplit[:, s, 0, col:col + P], wsplit[:, s, 1, col:col + P]
                        mm = three(ps[:, bank + m, :], w_hi, w_lo, moving[:, 0, k, :], moving[:, 1, k, :],
                                   k == 0, k == ND - 1)
                mm.then_inc(chunk_used, 1)

            for n in range(V0, U0):
                pe.wait_ge(lo_ready, n + 1)
                if n:
                    pe.wait_ge(h_lo, ND)
                by_token(n, hT, 4 * (n // 2))
            for n in range(U0, P0):
                pe.wait_ge(lo_ready, n + 1)
                if n < U0 + 2:
                    pe.wait_ge(v_gelu, NT)
                else:
                    pe.wait_ge(v_gelu, 2 * NT)
                by_feature(n % 2, hT, 2 * (n - U0))
            pe.wait_ge(v_ready, NT)
            pe.wait_ge(ws_ready, 1)
            for h in range(NH):
                pe.wait_ge(u_ready, h + 1)
                for c in range(NT):
                    mm = nc.tensor.matmul(ps[:, h, c * P:(c + 1) * P], v[:, c * D + h * P:c * D + (h + 1) * P],
                                          wsT[:, h * P:(h + 1) * P], start=True, stop=True)
                mm.then_inc(s_mm, 1)

            def mix(i):
                g = 3 - i
                pe.wait_ge(pooled_ready, 2 * i + 2)
                pe.wait_ge(wpool_in, 16)
                for dj in range(2):
                    for k in range(2):
                        col = (2 * g + k) * 256 + dj * P
                        mm = nc.tensor.matmul(ps[:, 2 * i + dj, :], raw[:, 4, col:col + P], pooled[:, i % 2, k, :],
                                              start=(k == 0), stop=(k == 1))
                    mm.then_inc(mix_mm, 1)

            for n in range(P0, G0):
                pe.wait_ge(lo_ready, n + 1)
                pe.wait_ge(ya_f, 2 * (n - P0) + 2)
                s = n % 2
                by_feature(s, hT, 2 * (n - P0))
                if n > P0:
                    mix(n - P0 - 1)
            mix(3)
            pe.wait_ge(ya_lo, NH)
            with pe.Fori(0, 4) as q:
                for j in range(4):
                    pe.wait_ge(lo_ready, q * 4 + (G0 + j + 1))
                    pe.wait_ge(yb_lo, 2 * j + 2)
                    by_feature(j % 2, (hT, ya, hT, yb)[j], 2 * j)

            def row(b, bank):
                nc.tensor.matmul(ps[:, bank, :], ones[:, :], macc_b[:, b * 512:(b + 1) * 512],
                                 start=True, stop=True).then_inc(row_mm, 1)

            def out_tile(n, t):
                s, half, kh = split_slot(n), (n - O0) % 2, (n - O0) // 2
                for k in range(4):
                    kk = 4 * kh + k
                    mm = three(ps[:, 4 * half + t, :], hT[:, 0, kk, t * P:(t + 1) * P], hT[:, 1, kk, t * P:(t + 1) * P],
                               wblock(s, 0, k, 512), wblock(s, 1, k, 512), kk == 0, kk == ND - 1)
                return mm

            pe.wait_ge(ada_used, RAW_ADA // 2 + 16)
            pe.wait_ge(merge_b, ND)
            for b in range(4):
                row(b, 4 + b)
            pe.wait_ge(lo_ready, O0 + 1)
            pe.wait_ge(m_lo, 4)
            for t in range(NT):
                if t == 2:
                    pe.wait_ge(row_ready, 4)
                    for b in range(4):
                        row(4 + b, 4 + b)
                mm = out_tile(O0, t)
            mm.then_inc(chunk_used, 1)
            pe.wait_ge(lo_ready, O0 + 2)
            pe.wait_ge(row_ready, 8)
            for t in range(NT):
                mm = out_tile(O0 + 1, t)
            mm.then_inc(chunk_used, 1)
            pe.wait_ge(lo_ready, O0 + 3)
            pe.wait_ge(m_lo, ND)
            for t in range(NT):
                mm = out_tile(O0 + 2, t)
                mm.then_inc(o_tile if t < NT - 1 else chunk_used, 1)
                if t == 0:
                    pe.wait_ge(lo_ready, O0 + 4)
                mm = out_tile(O0 + 3, t)
                mm.then_inc(o_tile if t < NT - 1 else chunk_used, 1)
            pe.wait_ge(router_in, 16)

            def logits(t):
                pe.wait_ge(hfT_ready, t + 1)
                for k in range(ND):
                    mm = nc.tensor.matmul(ps[:, 4, t * E:(t + 1) * E], hfT[:, t % 2, k, :], router[:, k, :],
                                          start=(k == 0), stop=(k == ND - 1))
                mm.then_inc(logits_mm, 1)

            for t in range(NT):
                pe.wait_ge(hf_ready, t + 1)
                if t >= 2:
                    pe.wait_ge(hfT_ready, t - 1)
                for k in range(ND):
                    mm = nc.tensor.transpose(ps[:, 5 * (t % 2) + k // 4, (k % 4) * P:(k % 4 + 1) * P],
                                             hf[:, t, k * P:(k + 1) * P], ident[:, :])
                mm.then_inc(hf_t, 1)
                if t:
                    logits(t - 1)
            logits(NT - 1)
            pe.wait_ge(mask_ready, 1)
            nc.tensor.matmul(ps[:, 2, 0:(NT + 1) * E], before[:, :], r_m_all, start=True, stop=False)
            for t in range(1, NT + 1):
                mm = nc.tensor.matmul(ps[:, 2, t * E:(NT + 1) * E], ones[:, :], r_m_all[:, 0:(NT + 1 - t) * E],
                                      start=False, stop=(t == NT))
            mm.then_inc(pos_mm, 1)

            def index(j, e):
                pe.wait_ge(sel_ready, j + 1)
                pe.wait_ge(idx_ready, j)
                for t in range(NT):
                    mm = nc.tensor.matmul(ps[:, 7, 0:3], sel[:, t, :],
                                          info[:, t, ds(e, 1), :].rearrange("p a n -> p (a n)"),
                                          start=(t == 0), stop=(t == NT - 1))
                mm.then_inc(idx_mm, 1)

            def turn(j):
                pe.wait_ge(gathered, j * 16 + 16)
                pe.wait_ge(hg_lo, j)
                for k in range(ND):
                    mm = nc.tensor.transpose(ps[:, 2 + k // 4, (k % 4) * P:(k % 4 + 1) * P],
                                             hg[:, k * P:(k + 1) * P], ident[:, :])
                mm.then_inc(hg_t, 1)

            def gate_up(i, first_chunk, slot0):
                pe.wait_ge(hg_lo, i + 1)
                for c in range(4):
                    pe.wait_ge(lo_ready, first_chunk + (c + 1))
                    for k in range(4):
                        kk = 4 * (c % 2) + k
                        mm = three(ps[:, c // 2, :], hgT[:, 0, kk, :], hgT[:, 1, kk, :],
                                   wblock(slot0 + c, 0, k, 512), wblock(slot0 + c, 1, k, 512), kk == 0, kk == ND - 1)
                    mm.then_inc(chunk_used, 1)

            def down(i, first_chunk, slot0=4):
                pe.wait_ge(aT_lo, i + 1)
                pe.wait_ge(y_ready, i)
                for c in range(2):
                    pe.wait_ge(lo_ready, first_chunk + (c + 1))
                    for k in range(2):
                        for half in range(2):
                            w = 2 * k + half
                            mm = three(ps[:, 5 + half, :], aT[:, 0, 2 * c + k, :], aT[:, 1, 2 * c + k, :],
                                       wblock(slot0 + c, 0, w, 512), wblock(slot0 + c, 1, w, 512),
                                       c == 0 and k == 0, c == 1 and k == 1)
                    mm.then_inc(chunk_used, 1)

            def turn_hidden(i):
                pe.wait_ge(a_ready, i + 1)
                pe.wait_ge(aT_lo, i)
                for k in range(NF):
                    mm = nc.tensor.transpose(ps[:, 4, k * P:(k + 1) * P], a_t[:, k * P:(k + 1) * P], ident[:, :])
                mm.then_inc(a_trans, 1)

            index(0, 0)
            index(1, 1)
            turn(0)
            gate_up(0, M0, 2)
            turn(1)
            turn_hidden(0)
            index(2, 2)

            def tile(i, e2):
                gate_up(i, i * 6 + 30, 0)
                turn(i + 1)
                down(i - 1, i * 6 + 34)
                turn_hidden(i)
                index(i + 2, e2)

            tile(1, 3)
            with pe.Fori(2, 14) as i:
                tile(i, i + 2)
            pe.wait_ge(tiles_ready, 1)
            tiles = pe.value_load(expert_of[0:1, 31:32], min_val=0, max_val=7) + E
            with pe.Fori(14, tiles - 1) as i:
                e2 = pe.value_load(expert_of[0:1, ds(i + 2, 1)], min_val=0, max_val=E - 1)
                tile(i, e2)
            gate_up(tiles - 1, tiles * 6 + 24, 0)
            down(tiles - 2, tiles * 6 + 28)
            turn_hidden(tiles - 1)
            down(tiles - 1, tiles * 6 + 30, 0)


_INS = ["x", "c", "w_ada", "b_ada", "norm_mix_g", "w_in", "v_norm_g", "sgu_w", "sgu_b", "pool_w", "pool_scale",
        "w_branch_a", "w_branch_b", "w_out", "norm_ffn_g", "router_w", "router_bias",
        "w_exp_gate", "w_exp_up", "w_exp_down", "final_norm_g"]


def kernel(**inputs):
    import numpy as _np
    import concourse.bacc as _bacc
    from concourse import mybir as _mybir
    from concourse.bass_utils import run_bass_kernel_spmd as _run

    nc = _bacc.Bacc("TRN2", target_bir_lowering=False, num_devices=1)
    arrays, aps = {}, {}
    for name in _INS:
        a = _np.ascontiguousarray(inputs[name])
        arrays[f"in_{name}"] = a
        aps[name] = nc.dram_tensor(f"in_{name}", a.shape, _mybir.dt.from_np(a.dtype), kind="ExternalInput").ap()
    out = nc.dram_tensor("out_0", (1, SEQ, D), F32, kind="ExternalOutput").ap()
    tokens_moe_kernel(nc, aps, out)
    r = _run(nc, [arrays], core_ids=[0])
    return r.results[0]["out_0"]
```

```python
from contextlib import ExitStack

import concourse.bass as bass
from concourse import mybir

F32 = mybir.dt.float32
F32R = mybir.dt.float32r
I32 = mybir.dt.int32
ALU = mybir.AluOpType
ACT = mybir.ActivationFunctionType
AX_X = mybir.AxisListType.X
ds = bass.ds

P = 128
SEQ = 512
NT = SEQ // P
D = 1024
ND = D // P
NH = 8
E = 16
EG = 4
FE = D // 2
NF = FE // P
WINDOWS = (2, 4, 8, 16)
EPS = 1e-6

CH = 2048
CC = CH // ND
RING_A = 4
RING = 6

V0, U0, P0, G0, O0 = 0, 4, 8, 12, 28
M0 = 32
RAW_ADA = 8
RAW_V = RAW_ADA
RAW_G = RAW_V + G0
RAW_O = RAW_G + 32
TILES_MAX = E + 8
LAST_BANK = 2
SKIP = 5000


def tokens_moe_kernel(nc, A, out):
    w_ada = A["w_ada"][0].rearrange("(k p) n -> p k n", p=P)
    w_in = A["w_in"][0].rearrange("(k p) n -> p k n", p=P)
    w_a = A["w_branch_a"][0].rearrange("(k p) n -> p k n", p=P)
    w_b = A["w_branch_b"][0].rearrange("(k p) n -> p k n", p=P)
    w_out = A["w_out"][0].rearrange("(k p) n -> p k n", p=P)
    w_gate = A["w_exp_gate"][0].rearrange("e (k p) f -> e p k f", p=P)
    w_up = A["w_exp_up"][0].rearrange("e (k p) f -> e p k f", p=P)
    w_down = A["w_exp_down"][0].rearrange("e (k p) n -> e p k n", p=P)
    x_rows = A["x"][0].rearrange("(t p) d -> p t d", p=P)
    out_rows = out[0].rearrange("(t p) d -> p t d", p=P)

    hf_dram = nc.dram_tensor("hf_rows", (SEQ, D), F32, kind="Internal").ap()
    y_dram = nc.dram_tensor("expert_rows", (2 * SEQ + 1, D), F32, kind="Internal").ap()
    hf_out = hf_dram.rearrange("(t p) d -> p t d", p=P)
    y_pairs = y_dram[1:2 * SEQ + 1, :].rearrange("(t p two) d -> t p (two d)", p=P, two=2)

    ctx = ExitStack()
    with ctx:
        def sb(name, shape, dt=F32):
            return ctx.enter_context(nc.sbuf_tensor(name, shape, dt))

        def sem(name):
            return ctx.enter_context(nc.semaphore(name))

        ps = ctx.enter_context(nc.psum_tensor("ps", [P, 8, 512], F32))
        raw = sb("raw", [P, RING, CH])
        wsplit = sb("wsplit", [P, RING, 2, CH], F32R)
        mx = sb("mx", [P, NT * D])
        tmp = sb("tmp", [P, 2 * D])
        ident = sb("ident", [P, P])
        ones = sb("ones", [P, P])
        before = sb("before", [P, P])
        iota1 = sb("iota1", [P, P])
        router = sb("router", [P, ND, E])
        cols = sb("cols", [P, 48])
        c_silu = sb("c_silu", [P, ND])
        mod_cols = sb("mod_cols", [P, 16])
        gain = sb("gain", [P, ND])
        stats = sb("stats", [P, 32])
        nrm = sb("nrm", [P, 2 * NT + 1])
        fin_rms = sb("fin_rms", [P, 1])
        inv_count = sb("inv_count", [P, 16])
        bias_row = sb("bias_row", [P, E])
        order = sb("order", [P, 2, EG, EG])
        pos1 = sb("pos1", [P, NT, E])
        info = sb("info", [P, NT, E, 3])
        base = sb("base", [P, TILES_MAX])
        expert_of = sb("expert_of", [P, 32], I32)
        weights_of = sb("weights_of", [P, 2, TILES_MAX], I32)
        row_w = sb("row_w", [P, TILES_MAX])
        row_dest = sb("row_dest", [P, TILES_MAX], I32)
        tok_idx = sb("tok_idx", [P, 1], I32)
        dest_now = sb("dest_now", [P, 1], I32)
        signal = sb("signal", [1, RING, E])
        iota_i = sb("iota_i", [P, P], I32)
        tok_i = sb("tok_i", [P, NT], I32)
        tok_f = sb("tok_f", [P, NT])
        with nc.sbuf_tensor("hT", [P, 2, ND, SEQ], F32R) as hT:
            pass
        hgT = sb("hgT", [P, 2, ND, P], F32R)
        aT = sb("aT", [P, 2, NF, P], F32R)
        work = sb("work", [P, 5 * D])

        v = raw[:, 4:6, :].rearrange("p s c -> p (s c)")
        ada_prod = raw[:, 4, :].rearrange("p (k n) -> p k n", k=ND)
        macc_a = work[:, 0:RAW_ADA // 2 * CC]
        mod_row = work[0:1, 2 * D:2 * D + CC]
        macc_b = raw[:, 4:6, :].rearrange("p s c -> p (s c)")
        hf = raw[:, 4:6, :].rearrange("p s (t d) -> p (s t) d", d=D)
        shf, gff = raw[:, 0, 0:D], raw[:, 0, D:2 * D]
        ya = wsplit[:, 2:4, :, :].rearrange("p s a (b n) -> p s (a b) n", n=SEQ)
        yb = wsplit[:, 4:6, :, :].rearrange("p s a (b n) -> p s (a b) n", n=SEQ)
        wnat = tmp[:, D:2 * D]
        wsT = tmp[:, 0:D]
        bsb = tmp[:, D:2 * D]
        rows_c = raw[0:48, 5, D:D + P]
        gm = tmp[:, 0:D]
        hg = work[:, 0:D]
        y = work[:, D:2 * D]
        act_g = work[:, 2 * D:2 * D + FE]
        a_t = work[:, 2 * D + FE:3 * D]
        gf = tmp[:, D:2 * D]
        hfT = work[:, 0:2 * D].rearrange("p (b k m) -> p b k m", b=2, m=P)
        sel = work[:, 3 * D:3 * D + NT * P].rearrange("p (t m) -> p t m", t=NT)
        rt = work[:, 3 * D + NT * P:5 * D]
        gfin = work[:, 4 * D:5 * D]

        rows_in = sem("rows_in")
        x_in = [sem(f"x_in{t}") for t in range(NT)]
        wnat_in, bsb_in, router_in, bb_in = map(sem, ("wnat_in", "bsb_in", "router_in", "bb_in"))
        bias_in, wpool_in, gff_in, x_again = map(sem, ("bias_in", "wpool_in", "gff_in", "x_again"))
        landed = [sem(f"landed{s}") for s in range(RING)]
        hi_ready, lo_ready, chunk_used, ada_used, ada_step = map(
            sem, ("hi_ready", "lo_ready", "chunk_used", "ada_used", "ada_step"))
        consts, pool_step, causal, cols_t, cols_ready, c_ready = map(
            sem, ("consts", "pool_step", "causal", "cols_t", "cols_ready", "c_ready"))
        maccb_zero, mod_used, mod_row_ready = map(sem, ("maccb_zero", "mod_used", "mod_row_ready"))
        ws_t, ws_ready, squares, xhat_ready, xT_t, mod_mm, mod_ready, gain_ready = map(
            sem, ("ws_t", "ws_ready", "squares", "xhat_ready", "xT_t", "mod_mm", "mod_ready", "gain_ready"))
        h_aff, h_hi, h_lo = map(sem, ("h_aff", "h_hi", "h_lo"))
        chain = sem("chain")
        v_gelu, v_centred, v_square, v_ready, u_ready = map(
            sem, ("v_gelu", "v_centred", "v_square", "v_ready", "u_ready"))
        s_mm, ya_f, ya_hi, ya_lo = map(sem, ("s_mm", "ya_f", "ya_hi", "ya_lo"))
        z_ready, pooled_ready, mix_mm, yb_hi, yb_lo = map(
            sem, ("z_ready", "pooled_ready", "mix_mm", "yb_hi", "yb_lo"))
        gate_ready, merge_a, merge_t, merge_b, m_hi, m_lo = map(
            sem, ("gate_ready", "merge_a", "merge_t", "merge_b", "m_hi", "m_lo"))
        row_mm, row_ready, o_tile, x2_half = map(sem, ("row_mm", "row_ready", "o_tile", "x2_half"))
        sq2, hf_scaled, hf_ready, hf_saved, hf_t, hfT_ready, logits_mm, expd, mask_ready, pos_mm, tiles_ready = map(
            sem, ("sq2", "hf_scaled", "hf_ready", "hf_saved", "hf_t", "hfT_ready", "logits_mm", "expd", "mask_ready",
                  "pos_mm", "tiles_ready"))
        sel_ready, idx_mm, idx_ready, gathered, hg_t, hg_hi, hg_lo = map(
            sem, ("sel_ready", "idx_mm", "idx_ready", "gathered", "hg_t", "hg_hi", "hg_lo"))
        silu_ready, a_ready, a_trans, aT_hi, aT_lo, y_ready, dest_ready, scattered = map(
            sem, ("silu_ready", "a_ready", "a_trans", "aT_hi", "aT_lo", "y_ready", "dest_ready", "scattered"))
        gfin_in, fin_x, fin_sq, fin_n, fin_ready, out_done = map(
            sem, ("gfin_in", "fin_x", "fin_sq", "fin_n", "fin_ready", "out_done"))
        fin_rms_ready, fin_scaled, fin_second = map(sem, ("fin_rms_ready", "fin_scaled", "fin_second"))
        y_sum, hg_zero = sem("y_sum"), sem("hg_zero")
        y_in = [sem(f"y_in{t}") for t in range(NT)]

        x_tiles = mx[:, :].rearrange("p (t d) -> p t d", t=NT)
        u = mx[:, :].rearrange("p (m n) -> p m n", n=SEQ)
        merged = u
        z0, win_a, win_b = (mx[:, i * (16 + SEQ):(i + 1) * (16 + SEQ)] for i in range(3))
        z = (z0, tmp[:, 0:16 + SEQ])
        pooled = mx[:, 2048:4096].rearrange("p (b k n) -> p b k n", b=2, k=2)
        sig_a = tmp[:, 0:D].rearrange("p (b n) -> p b n", b=2)
        sig_b = tmp[:, D:2 * D].rearrange("p (b n) -> p b n", b=2)

        at = [0]

        def small(n):
            at[0] += n
            return rt[:, at[0] - n:at[0]]

        te_view = lambda a: a.rearrange("p (t e) -> p t e", t=NT)
        r_d, r_p, r_sel, r_top = (small(NT * E) for _ in range(4))
        r_m_all = small((NT + 1) * E)
        r_m = r_m_all[:, 0:NT * E]
        r_d3, r_p3, r_sel3, r_m3 = map(te_view, (r_d, r_p, r_sel, r_m))
        r_4, r_4b, r_4c = (small(NT) for _ in range(3))
        r_gs, r_gr = small(NT * EG), small(NT * EG)
        r_ge, r_gt = (small(NT * E * EG).rearrange("p (g a b) -> p g a b", a=EG, b=EG) for _ in range(2))
        r_cnt, r_x, r_x2, r_x3, r_cum = (small(E) for _ in range(5))
        r_le = small(TILES_MAX * E).rearrange("p (i e) -> p i e", i=TILES_MAX)
        r_n, r_first, r_wrap, r_i = (small(TILES_MAX) for _ in range(4))
        r_extra = small(1)
        sub_ready = sem("sub_ready")

        def mix_hi(act, activation, i):
            for j in range(2):
                m = 2 * (3 - i) + j
                act.wait_ge(mix_mm, 2 * i + j + 1)
                activation(yb[:, 0, m, :], ps[:, 2 * i + j, :], ACT.Copy,
                           scale=cols[:, 24 + m:25 + m]).then_inc(yb_hi, 1)

        def mix_lo(dve, V, i):
            for j in range(2):
                m = 2 * (3 - i) + j
                dve.wait_ge(yb_hi, 2 * i + j + 1)
                V.scalar_tensor_tensor(out=yb[:, 1, m, :], in0=ps[:, 2 * i + j, :], scalar=cols[:, 24 + m:25 + m],
                                       in1=yb[:, 0, m, :].bitcast(F32), op0=ALU.mult,
                                       op1=ALU.subtract).then_inc(yb_lo, 1)

        def turned(act, activation, t):
            for half in range(2):
                act.wait_ge(hf_t, 2 * t + half + 1)
                if t >= 2:
                    act.wait_ge(logits_mm, t - 1)
                activation(hfT[:, t % 2, 4 * half:4 * half + 4, :].rearrange("p k m -> p (k m)"),
                           ps[:, 5 * (t % 2) + half, :], ACT.Copy).then_inc(hfT_ready, 1)

        def final(dve, V, inv_rms_1, t):
            dve.wait_ge(fin_sq, t + 1)
            inv_rms_1(28 + t)
            dve.wait_ge(gfin_in, 16)
            V.scalar_tensor_tensor(out=x_tiles[:, t, :], in0=x_tiles[:, t, :], scalar=stats[:, 28 + t:29 + t],
                                   in1=gfin, op0=ALU.mult, op1=ALU.mult).then_inc(fin_ready, 1)

        block = ctx.enter_context(nc.Block())

        def split_slot(n):
            if n == M0 - 1:
                return 4
            return n % 2 if n < M0 else (n - M0 + 2) % RING

        def raw_place(n):
            r = RAW_V + n if n < G0 else (RAW_O + n - O0 if n >= O0 else None)
            return r % RING_A, 16 * (r // RING_A + 1)

        def wait_reg(engine, semaphore, value, least=1):
            if not isinstance(value, int):
                value = engine.to_reg(value)
            engine.wait_ge(semaphore, least)
            engine.wait_ge(semaphore, value)

        @block.sync
        def _(sp):
            def load(slot, src, k):
                sp.dma_start(raw[:, slot, :].rearrange("p (k n) -> p k n", k=k), src).then_inc(landed[slot], 16)

            for i, name in enumerate(("c", "norm_mix_g", "v_norm_g", "pool_scale")):
                sp.dma_start(rows_c[8 * i:8 * i + 8, :],
                            A[name].rearrange("a (k p) -> (a k) p", p=P)).then_inc(rows_in, 16)
            sp.dma_start(rows_c[32:48, :],
                         A["b_ada"][:, 0:2 * D].rearrange("a (k p) -> (a k) p", p=P)).then_inc(rows_in, 16)
            def first_used(r):
                sp.wait_ge(mod_used if r % 2 else ada_used, r // 2 + 1)

            for r in range(RAW_ADA):
                if r >= RING_A:
                    first_used(r - RING_A)
                load(r % RING_A, w_ada[:, :, r * CC:(r + 1) * CC], ND)
                if r == 1:
                    for t in range(NT):
                        sp.dma_start(x_tiles[:, t, :], x_rows[:, t, :]).then_inc(x_in[t], 16)
                if r == 3:
                    sp.dma_start(wnat.rearrange("p (h j) -> p h j", h=NH),
                                 A["sgu_w"][0].rearrange("h i j -> i h j")).then_inc(wnat_in, 16)
            for n in range(V0, G0):
                if n < RING_A:
                    first_used(RING_A + n)
                else:
                    sp.wait_ge(lo_ready, n - RING_A + 1)
                if n < U0:
                    half, kh = n // 2, n % 2
                    load(n % RING_A, w_in[:, 4 * kh:4 * kh + 4, D + half * 512:D + half * 512 + 512], 4)
                elif n < P0:
                    load(n % RING_A, w_in[:, :, (n - U0) * CC:(n - U0 + 1) * CC], ND)
                else:
                    g = 3 - (n - P0)
                    load(n % RING_A, w_in[:, :, 2 * D + g * CC:2 * D + (g + 1) * CC], ND)
            sp.wait_ge(s_mm, NH)
            sp.dma_start(raw[:, 4, :].rearrange("p (a n) -> p a n", n=256),
                         A["pool_w"][0].rearrange("g (k p) n -> p (g k) n", p=P)).then_inc(wpool_in, 16)
            with sp.Fori(0, 4) as q:
                for j, (w, c0) in enumerate(((w_in, 3 * D), (w_a, 0), (w_in, 4 * D), (w_b, 0))):
                    wait_reg(sp, lo_ready, q * 4 + (P0 + 1 + j))
                    wait_reg(sp, ada_used, q * 4 + (1 + j))
                    load(j, w[:, :, ds(q * CC + c0, CC)], ND)
                for j in range(4):
                    wait_reg(sp, lo_ready, q * 4 + (G0 + 1 + j))
                    load(j, w_ada[:, :, ds(q * (4 * CC) + (2 * D + j * CC), CC)], ND)
            for j in range(4):
                sp.wait_ge(ada_used, RAW_ADA // 2 + 12 + j + 1)
                half, kh = j % 2, j // 2
                load(j, w_out[:, 4 * kh:4 * kh + 4, half * 512:half * 512 + 512], 4)
            sp.wait_ge(m_lo, ND)
            sp.dma_start(mx[:, :].rearrange("p (t d) -> p t d", t=NT), x_rows).then_inc(x_again, 16)
            sp.wait_ge(lo_ready, O0 + 1)
            sp.dma_start(gff, A["norm_ffn_g"][0].partition_broadcast(P)).then_inc(gff_in, 16)
            for c in range(2):
                sp.wait_ge(lo_ready, M0 - 1 + c)
                load(c + 2, w_gate[0, :, 4 * c:4 * c + 4, :], 4)
            load(1, w_gate[1, :, 4:8, :], 4)
            for c in range(2):
                sp.wait_ge(lo_ready, M0 + 1 + c)
                load(c + 2, w_up[1, :, 4 * c:4 * c + 4, :], 4)
            for t in range(NT):
                sp.wait_ge(hf_ready, t + 1)
                sp.dma_start(hf_out[:, t, :], hf[:, t, :]).then_inc(hf_saved, 16)
            sp.wait_ge(hf_saved, 16 * NT)
            sp.wait_ge(hf_t, 2 * NT)
            for c in range(2):
                load(c + 4, w_up[0, :, 4 * c:4 * c + 4, :], 4)
            load(0, w_gate[1, :, 0:4, :], 4)
            for c in range(2):
                sp.wait_ge(lo_ready, M0 + 3 + c)
                load(c + 4, w_down[0, :, 2 * c:2 * c + 2, :], 2)

            def part(i, table, chunks, source):
                new = sp.value_load(weights_of[0:1, 0, ds(table, 1)], min_val=0, max_val=1)
                again = sp.value_load(weights_of[0:1, 1, ds(table, 1)], min_val=0, max_val=1)
                with sp.If(new > 0):
                    for c in chunks:
                        wait_reg(sp, lo_ready, i * 6 + (25 + c))
                        src, k = source(c)
                        load(c, src.rearrange("a p k f -> (a p) k f"), k)
                with sp.If(again > 0):
                    for c in chunks:
                        wait_reg(sp, lo_ready, i * 6 + (25 + c))
                        sp.dma_start(signal[:, c, :], A["router_bias"]).then_inc(landed[c], 16)

            sp.wait_ge(tiles_ready, 1)
            tiles = sp.value_load(expert_of[0:1, 31:32], min_val=0, max_val=7) + E
            with sp.Fori(2, tiles) as i:
                e = sp.value_load(expert_of[0:1, ds(i, 1)], min_val=0, max_val=E - 1)
                e_prev = sp.value_load(expert_of[0:1, ds(i - 1, 1)], min_val=0, max_val=E - 1)
                part(i, i, range(4), lambda c: ((w_gate if c < 2 else w_up)[ds(e, 1), :, 4 * (c % 2):4 * (c % 2) + 4, :],
                                                4))
                part(i, i - 1, range(4, RING), lambda c: (w_down[ds(e_prev, 1), :, 2 * (c - 4):2 * (c - 4) + 2, :], 2))
            e = sp.value_load(expert_of[0:1, ds(tiles - 1, 1)], min_val=0, max_val=E - 1)
            for c in range(2):
                wait_reg(sp, lo_ready, tiles * 6 + (25 + c))
                load(c, w_down[ds(e, 1), :, 2 * c:2 * c + 2, :].rearrange("a p k f -> (a p) k f"), 2)
            sp.dma_start(gfin, A["final_norm_g"].partition_broadcast(P)).then_inc(gfin_in, 16)
            wait_reg(sp, scattered, tiles * 16)
            for t in range(NT):
                sp.dma_start(raw[:, t, :], y_pairs[t]).then_inc(y_in[t], 16)
            for t in range(NT):
                if t == 1:
                    sp.wait_ge(fin_second, 1)
                else:
                    sp.wait_ge(fin_ready, max(t, 1))
                sp.dma_start(out_rows[:, t, :], mx[:, t * D:(t + 1) * D]).then_inc(out_done, 16)
            sp.wait_ge(out_done, 16 * NT)

        @block.gpsimd
        def _(pool):
            g = nc.gpsimd
            g.memset(ident[:, :], 0.0)
            g.memset(ones[:, :], 1.0)
            g.memset(before[:, :], 1.0)
            g.memset(base[:, :], 0.0)
            g.memset(order[:, :, :, :], 1.0)
            g.iota(iota_i[:, :], pattern=[[1, P]], base=1, channel_multiplier=0)
            g.iota(tok_i[:, :], pattern=[[P, NT]], base=0, channel_multiplier=1).then_inc(pool_step, 1)
            pool.wait_ge(pool_step, 1)
            g.affine_select(out=ident[:, :], in_=ident[:, :], compare_op=ALU.not_equal, fill=1.0, base=0,
                            pattern=[[-1, P]], channel_multiplier=1).then_inc(consts, 1)
            g.affine_select(out=before[:, :], in_=before[:, :], compare_op=ALU.is_gt, fill=0.0, base=0,
                            pattern=[[1, P]], channel_multiplier=-1)
            g.affine_select(out=order[:, 0, :, :], in_=order[:, 0, :, :], compare_op=ALU.is_gt, fill=0.0, base=0,
                            pattern=[[1, EG], [-1, EG]], channel_multiplier=0)
            g.affine_select(out=order[:, 1, :, :], in_=order[:, 1, :, :], compare_op=ALU.is_gt, fill=0.0, base=0,
                            pattern=[[-1, EG], [1, EG]], channel_multiplier=0)
            g.tensor_copy(iota1[:, :], iota_i[:, :])
            g.tensor_copy(tok_f[:, :], tok_i[:, :]).then_inc(consts, 1)
            pool.wait_ge(wnat_in, 16)
            w_ihj = wnat.rearrange("p (h j) -> p h j", h=NH)
            g.affine_select(out=w_ihj, in_=w_ihj, compare_op=ALU.is_ge, fill=0.0, base=0,
                            pattern=[[0, NH], [-1, P]], channel_multiplier=1).then_inc(causal, 1)
            for h in range(NH):
                pool.wait_ge(ya_hi, h + 1)
                g.tensor_tensor(ya[:, 1, h, :], u[:, h, :], ya[:, 0, h, :].bitcast(F32),
                                ALU.subtract).then_inc(ya_lo, 1)
            pool.wait_ge(mix_mm, NH)
            g.memset(macc_b, 0.0).then_inc(maccb_zero, 1)
            pool.wait_ge(maccb_zero, 1)
            pool.dma_start(macc_b[0:1, :], A["b_ada"][:, 2 * D:6 * D]).then_inc(bb_in, 16)

            def gather(j):
                wait_reg(pool, idx_ready, j + 1)
                wait_reg(pool, hg_t, j, 0)
                g.indirect_dma_start(out=hg, out_offset=None, in_=hf_dram,
                                     in_offset=bass.IndirectOffsetOnAxis(ap=tok_idx[:, 0:1], axis=0),
                                     bounds_check=SEQ - 1, oob_is_err=False).then_inc(gathered, 16)

            def scatter(j):
                wait_reg(pool, y_ready, j + 1)
                wait_reg(pool, dest_ready, j + 1)
                g.indirect_dma_start(out=y_dram, out_offset=bass.IndirectOffsetOnAxis(ap=dest_now[:, 0:1], axis=0),
                                     in_=y, in_offset=None, bounds_check=2 * SEQ,
                                     oob_is_err=False).then_inc(scattered, 16)

            for c in range(2):
                pool.wait_ge(hi_ready, M0 + c + 1)
                pool.wait_ge(lo_ready, M0 + c)
                g.tensor_tensor(wsplit[:, c + 2, 1, :], raw[:, c + 2, :], wsplit[:, c + 2, 0, :].bitcast(F32),
                                ALU.subtract).then_inc(lo_ready, 1)
            pool.wait_ge(row_ready, 4)
            for t in range(NT - 1):
                pool.wait_ge(hf_scaled, t + 1)
                g.tensor_tensor(hf[:, t, :], hf[:, t, :], shf, ALU.add).then_inc(hf_ready, 1)
            pool.wait_ge(hf_saved, 16 * NT)
            pool.wait_ge(logits_mm, NT)
            g.memset(hg, 0.0).then_inc(hg_zero, 1)
            pool.wait_ge(hg_zero, 1)
            for j in range(4):
                gather(j)
            scatter(0)
            pool.wait_ge(tiles_ready, 1)
            tiles = pool.value_load(expert_of[0:1, 31:32], min_val=0, max_val=7) + E
            with pool.Fori(2, tiles - 1) as i:
                gather(i + 2)
                scatter(i - 1)
            scatter(tiles - 2)
            scatter(tiles - 1)
            wait_reg(pool, gathered, tiles * 16 + 16)
            wait_reg(pool, scattered, tiles * 16)
            for t in range(1, NT):
                pool.wait_ge(y_in[t], 16)
                g.tensor_tensor(raw[:, t, 0:D], raw[:, t, 0:D], raw[:, t, D:2 * D], ALU.add).then_inc(y_sum, 1)
            pool.wait_ge(fin_scaled, 1)
            pool.wait_ge(gfin_in, 16)
            g.tensor_tensor(x_tiles[:, 1, :], x_tiles[:, 1, :], gfin, ALU.mult).then_inc(fin_second, 1)

        @block.scalar
        def _(act):
            A_ = nc.scalar.activation
            def hi(n, slot, count, used=None):
                act.wait_ge(landed[slot], count)
                if used is not None:
                    act.wait_ge(chunk_used, used)
                A_(wsplit[:, n, 0, :], raw[:, slot, :], ACT.Copy).then_inc(hi_ready, 1)

            act.wait_ge(cols_ready, 1)
            A_(c_silu[:, :], cols[:, 0:ND], ACT.Silu).then_inc(c_ready, 1)
            for t in range(NT):
                act.wait_ge(x_in[t], 16)
                if t:
                    act.wait_ge(squares, t)
                A_(raw[:, 5, 0:D], x_tiles[:, t, :], ACT.Square, accum_out=stats[:, t:t + 1]).then_inc(squares, 1)
            for i in range(RAW_ADA // 2):
                if i == RAW_ADA // 2 - 1:
                    hi(0, *raw_place(0))
                act.wait_ge(mod_used, i + 1)
                if i:
                    act.wait_ge(mod_mm, i)
                A_(mod_row, ps[0:1, 7, CC:2 * CC], ACT.Copy).then_inc(mod_row_ready, 1)
                if i == 1:
                    act.wait_ge(ws_t, 1)
                    A_(wsT, ps[:, 5:7, :].rearrange("p b n -> p (b n)"), ACT.Copy).then_inc(ws_ready, 1)
            for k in range(ND):
                act.wait_ge(h_aff, k + 1)
                A_(hT[:, 0, k, :], ps[:, k, :], ACT.Copy).then_inc(h_hi, 1)
                if k == 3:
                    hi(1, *raw_place(1))
            act.wait_ge(ws_ready, 1)
            act.dma_start(bsb, A["sgu_b"][0].rearrange("h i -> (h i)").partition_broadcast(P)).then_inc(bsb_in, 16)
            act.dma_start(router[:, :, :], A["router_w"].rearrange("(k p) e -> p k e", p=P)).then_inc(router_in, 16)
            act.dma_start(bias_row[:, :], A["router_bias"].partition_broadcast(P)).then_inc(bias_in, 16)
            for n in range(V0, G0):
                if n >= 1:
                    s, count = raw_place(n + 1) if n + 1 < G0 else (0, 16 * (RAW_G // RING_A + 1))
                    hi((n + 1) % 2, s, count, n)
                if n < U0 and n % 2:
                    act.wait_ge(chunk_used, n + 1)
                    for t in range(NT):
                        b = 4 * (n // 2) + t
                        A_(v[:, t * D + (n // 2) * 512:t * D + (n // 2) * 512 + 512], ps[:, b, :],
                           ACT.Gelu_apprx_tanh, accum_out=stats[:, 8 + b:9 + b]).then_inc(v_gelu, 1)
                if n == U0:
                    for t in range(NT):
                        act.wait_ge(v_centred, t + 1)
                        if t:
                            act.wait_ge(v_square, t)
                        A_(wsplit[:, 2, 0, 0:D], v[:, t * D:(t + 1) * D], ACT.Square,
                           accum_out=stats[:, 20 + t:21 + t]).then_inc(v_square, 1)
                if U0 <= n < P0:
                    act.wait_ge(chunk_used, n + 1)
                    for m in range(2 * (n - U0), 2 * (n - U0) + 2):
                        if m == 0:
                            act.wait_ge(xT_t, ND)
                        A_(u[:, m, :], ps[:, m, :], ACT.Gelu_apprx_tanh).then_inc(u_ready, 1)
                if n == P0:
                    for h in range(NH):
                        act.wait_ge(ya_f, h + 1)
                        if h == 0:
                            act.wait_ge(v_square, NT)
                        A_(ya[:, 0, h, :], u[:, h, :], ACT.Copy).then_inc(ya_hi, 1)
                if n > P0 + 1:
                    mix_hi(act, A_, n - P0 - 2)
                if n >= P0:
                    i = n - P0
                    act.wait_ge(chunk_used, n + 1)
                    act.wait_ge(ya_lo, NH)
                    act.wait_ge(s_mm, NH)
                    for j in range(2):
                        if i:
                            act.wait_ge(pooled_ready, 2 * i + j - 1)
                        A_(z[j][:, 16:], ps[:, 2 * i + j, :], ACT.Copy).then_inc(z_ready, 1)
            mix_hi(act, A_, 2)
            mix_hi(act, A_, 3)
            with act.Fori(0, 4) as q:
                def hi_next(j):
                    act.wait_ge(landed[(j + 1) % 4], (q * 2 + (RAW_G // 4 + 1 + (2 if j == 3 else 0))) * 16)
                    act.wait_ge(chunk_used, q * 4 + (G0 + j))
                    A_(wsplit[:, (j + 1) % 2, 0, :], raw[:, (j + 1) % 4, :], ACT.Copy).then_inc(hi_ready, 1)

                hi_next(0)
                act.wait_ge(chunk_used, q * 4 + (G0 + 1))
                for b in range(2):
                    A_(sig_a[:, b, :], ps[:, b, :], ACT.Sigmoid).then_inc(gate_ready, 1)
                hi_next(1)
                hi_next(2)
                act.wait_ge(chunk_used, q * 4 + (G0 + 3))
                for b in range(2):
                    A_(sig_b[:, b, :], ps[:, 4 + b, :], ACT.Sigmoid).then_inc(gate_ready, 1)
                hi_next(3)
            act.wait_ge(chunk_used, G0 + 15)
            for k in range(ND):
                act.wait_ge(merge_b, k + 1)
                A_(hT[:, 0, k, :], merged[:, k, :], ACT.Copy).then_inc(m_hi, 1)
            for n in range(O0 + 1, O0 + 4):
                hi(split_slot(n), *raw_place(n), min(n - 1, O0 + 1))
            for c in range(2):
                hi(c + 2, c + 2, 16 * (RAW_O // 4 + 2), G0 + 16)
            for t in range(NT):
                if t == NT - 1:
                    turned(act, A_, 0)
                    turned(act, A_, 1)
                act.wait_ge(x2_half, 2 * t + 2)
                A_(hf[:, t, :], x_tiles[:, t, :], ACT.Square, accum_out=stats[:, 24 + t:25 + t]).then_inc(sq2, 1)
            for t in range(2, NT):
                turned(act, A_, t)
            act.wait_ge(sub_ready, 1)
            A_(r_p, r_d, ACT.Exp).then_inc(expd, 1)
            for c in range(2):
                hi(c + 4, c + 4, 16, M0)

            def rows_hi(j):
                act.wait_ge(hg_t, j + 1)
                A_(hgT[:, 0, :, :].rearrange("p k m -> p (k m)"), ps[:, 2:4, :].rearrange("p b n -> p (b n)"),
                   ACT.Copy).then_inc(hg_hi, 1)

            def silu(i, gate_used):
                act.wait_ge(chunk_used, gate_used)
                act.wait_ge(a_ready, i)
                A_(act_g, ps[:, 0, :], ACT.Silu).then_inc(silu_ready, 1)

            def a_hi(i):
                act.wait_ge(a_trans, i + 1)
                A_(aT[:, 0, :, :].rearrange("p k m -> p (k m)"), ps[:, 4, :], ACT.Copy).then_inc(aT_hi, 1)

            def tile(i, gate_used):
                def hi_c(c):
                    act.wait_ge(landed[c], (i + (2, 2, 3, 3, 2, 2)[c] + (13 if c < 4 else 0)) * 16)
                    act.wait_ge(chunk_used, i * 6 + (31 + c))
                    A_(wsplit[:, c, 0, :], raw[:, c, :], ACT.Copy).then_inc(hi_ready, 1)

                hi_c(0)
                hi_c(1)
                silu(i, gate_used)
                hi_c(2)
                hi_c(3)
                rows_hi(i + 1)
                hi_c(4)
                hi_c(5)
                a_hi(i)

            rows_hi(0)
            tile(0, M0 + 2)
            tile(1, 6 + 32)
            act.wait_ge(tiles_ready, 1)
            tiles = act.value_load(expert_of[0:1, 31:32], min_val=0, max_val=7) + E
            with act.Fori(2, tiles - 1) as i:
                tile(i, i * 6 + 32)
            silu(tiles - 1, tiles * 6 + 26)
            for c in range(2):
                act.wait_ge(landed[c], tiles * 16 + 14 * 16)
                act.wait_ge(chunk_used, tiles * 6 + (25 + c))
                A_(wsplit[:, c, 0, :], raw[:, c, :], ACT.Copy).then_inc(hi_ready, 1)
            act.wait_ge(chunk_used, tiles * 6 + 30)
            a_hi(tiles - 1)
            for t in range(NT):
                act.wait_ge(fin_x, t + 1)
                A_(raw[:, t, 0:D], x_tiles[:, t, :], ACT.Square, accum_out=stats[:, 28 + t:29 + t]).then_inc(fin_sq, 1)
                if t == 2:
                    act.wait_ge(fin_rms_ready, 1)
                    act.wait_ge(fin_sq, 2)
                    A_(x_tiles[:, 1, :], x_tiles[:, 1, :], ACT.Copy, scale=fin_rms[:, :]).then_inc(fin_scaled, 1)

        @block.vector
        def _(dve):
            V = nc.vector
            steps = [0]

            def step(ins):
                steps[0] += 1
                ins.then_inc(chain, 1)

            def done():
                dve.wait_ge(chain, steps[0])

            def lo(n, slot):
                V.tensor_tensor(wsplit[:, n, 1, :], raw[:, slot, :], wsplit[:, n, 0, :].bitcast(F32),
                                ALU.subtract).then_inc(lo_ready, 1)

            def lo_n(n, slot):
                dve.wait_ge(hi_ready, n + 1)
                lo(split_slot(n), slot)

            def inv_rms(col, n):
                m, yv, sq = stats[:, col:col + n], nrm[:, 0:n], nrm[:, NT:NT + n]
                yi, mi = nrm[:, 0:n].bitcast(I32), m.bitcast(I32)
                step(V.tensor_scalar(m, m, 1.0 / D, EPS, ALU.mult, ALU.add))
                done()
                step(V.tensor_scalar(yi, mi, 1, None, ALU.logical_shift_right))
                done()
                step(V.tensor_scalar(yi, yi, -1.0, float(0x5F3759DF), ALU.mult, ALU.add))
                done()
                for last in (False, False, True):
                    step(V.tensor_tensor(sq, yv, yv, ALU.mult))
                    done()
                    step(V.scalar_tensor_tensor(out=sq, in0=sq, scalar=-0.5, in1=m, op0=ALU.mult, op1=ALU.mult))
                    done()
                    step(V.scalar_tensor_tensor(out=m if last else yv, in0=sq, scalar=1.5, in1=yv,
                                                op0=ALU.add, op1=ALU.mult))
                    done()

            def inv_rms_1(col):
                m, z = stats[:, col:col + 1], nrm[:, 0:1]
                zi = z.bitcast(I32)
                powers = [nrm[:, NT + j:NT + j + 1] for j in range(3)]
                for j in range(3):
                    f = 4.0 ** (3 - j)
                    step(V.tensor_scalar(powers[j], m, f / D, f * EPS, ALU.mult, ALU.add))
                done()
                step(V.tensor_scalar(zi, powers[2].bitcast(I32), -0.5,
                                     float(0x5F3759DF - (2 << 23) - (1 << 31)), ALU.mult, ALU.add))
                done()
                for j in range(3):
                    step(V.scalar_tensor_tensor(out=nrm[:, 2 * NT:2 * NT + 1], in0=z, scalar=powers[j], in1=z,
                                                op0=ALU.mult, op1=ALU.mult))
                    done()
                    step(V.scalar_tensor_tensor(out=m if j == 2 else z, in0=nrm[:, 2 * NT:2 * NT + 1],
                                                scalar=-3.0, in1=z, op0=ALU.add, op1=ALU.mult))
                    done()

            def ada(acc, slot, a):
                for k in range(ND):
                    ins = V.scalar_tensor_tensor(out=acc, in0=raw[:, slot, k * CC:(k + 1) * CC],
                                                 scalar=c_silu[:, k:k + 1], in1=acc, op0=ALU.mult, op1=ALU.add)
                    if k < ND - 1:
                        ins.then_inc(ada_step, 1)
                        dve.wait_ge(ada_step, a * (ND - 1) + (k + 1))
                    else:
                        ins.then_inc(ada_used, 1)

            dve.wait_ge(cols_t, 1)
            V.tensor_copy(cols[:, :], ps[:, 7, 32:80]).then_inc(cols_ready, 1)
            dve.wait_ge(c_ready, 1)
            for i in range(RAW_ADA // 2):
                r = 2 * i
                dve.wait_ge(landed[r % RING_A], 16 * (r // RING_A + 1))
                step(V.tensor_tensor(ada_prod, raw[:, r % RING_A, :].rearrange("p (k n) -> p k n", k=ND),
                                     c_silu[:, :].unsqueeze(2).broadcast_to([P, ND, CC]), ALU.mult))
                done()
                V.tensor_reduce(macc_a[:, i * CC:(i + 1) * CC], ada_prod.rearrange("p k n -> p n k"), AX_X,
                                ALU.add).then_inc(ada_used, 1)
                dve.wait_ge(ada_used, i + 1)
                if i == 0:
                    dve.wait_ge(squares, NT)
                    inv_rms(0, NT)
                    for t in range(NT):
                        V.tensor_scalar(x_tiles[:, t, :], x_tiles[:, t, :], stats[:, t:t + 1], None,
                                        ALU.mult).then_inc(xhat_ready, 1)
            dve.wait_ge(consts, 2)
            step(V.reciprocal(inv_count[:, :], iota1[:, 0:16]))
            lo_n(0, 0)
            dve.wait_ge(mod_mm, RAW_ADA // 2)
            step(V.tensor_tensor(mod_cols[:, :], ps[:, 7, 0:16], cols[:, 32:48], ALU.add))
            done()
            V.scalar_tensor_tensor(out=gain[:, :], in0=mod_cols[:, 8:16], scalar=1.0, in1=cols[:, 8:16],
                                   op0=ALU.add, op1=ALU.mult).then_inc(gain_ready, 1)
            dve.wait_ge(gain_ready, 1)
            for k in range(ND + 1):
                if k < ND:
                    dve.wait_ge(xT_t, k + 1)
                    V.tensor_scalar(ps[:, k, :], ps[:, k, :], gain[:, k:k + 1], mod_cols[:, k:k + 1],
                                    ALU.mult, ALU.add).then_inc(h_aff, 1)
                if k:
                    dve.wait_ge(h_hi, k)
                    V.tensor_tensor(hT[:, 1, k - 1, :], ps[:, k - 1, :], hT[:, 0, k - 1, :].bitcast(F32),
                                    ALU.subtract).then_inc(h_lo, 1)
                if k == 5:
                    lo_n(1, 1)

            for n in range(V0, G0):
                if n >= 1:
                    lo_n(n + 1, (RAW_V + n + 1) % RING_A)
                if n == U0:
                    dve.wait_ge(v_gelu, 2 * NT)
                    step(V.tensor_tensor(stats[:, 16:20], stats[:, 8:12], stats[:, 12:16], ALU.add))
                    done()
                    step(V.tensor_scalar(stats[:, 16:20], stats[:, 16:20], 1.0 / D, None, ALU.mult))
                    done()
                    for t in range(NT):
                        V.tensor_scalar(v[:, t * D:(t + 1) * D], v[:, t * D:(t + 1) * D], stats[:, 16 + t:17 + t],
                                        None, ALU.subtract).then_inc(v_centred, 1)
                    dve.wait_ge(v_square, NT)
                    inv_rms(20, NT)
                    for t in range(NT):
                        V.tensor_scalar(v[:, t * D:(t + 1) * D], v[:, t * D:(t + 1) * D], stats[:, 20 + t:21 + t],
                                        None, ALU.mult).then_inc(v_ready, 1)
                if n == P0:
                    dve.wait_ge(bsb_in, 16)
                    for h in range(NH):
                        dve.wait_ge(s_mm, h + 1)
                        dve.wait_ge(u_ready, h + 1)
                        s_h = ps[:, h, :].rearrange("p (c i) -> p c i", c=NT)
                        b_h = bsb[:, h * P:(h + 1) * P].unsqueeze(1).broadcast_to([P, NT, P])
                        step(V.scalar_tensor_tensor(out=s_h, in0=s_h, scalar=cols[:, 16 + h:17 + h], in1=b_h,
                                                    op0=ALU.mult, op1=ALU.add))
                        done()
                        V.tensor_tensor(u[:, h, :], ps[:, h, :], u[:, h, :], ALU.mult).then_inc(ya_f, 1)
                    dve.wait_ge(ya_lo, NH)
                    step(V.memset(z[0][:, 0:16], 0.0))
                    step(V.memset(z[1][:, 0:16], 0.0))
                    done()
                if n >= P0:
                    i = n - P0
                    w = WINDOWS[3 - i]
                    if i >= 2:
                        dve.wait_ge(mix_mm, 2 * (i - 1))
                    for j in range(2):
                        dve.wait_ge(z_ready, 2 * i + j + 1)
                        src, d, turn = z[j], 1, 0
                        while d < w:
                            dst = (win_a, win_b)[turn]
                            lo_col = 2 * d - 1
                            step(V.tensor_tensor(dst[:, lo_col:], src[:, lo_col:], src[:, lo_col - d:16 + SEQ - d],
                                                 ALU.add))
                            done()
                            src, d, turn = dst, 2 * d, 1 - turn
                        out_j = pooled[:, i % 2, j, :]
                        step(V.scalar_tensor_tensor(out=out_j, in0=src[:, 16:], scalar=1.0 / w, in1=z[j][:, 16:],
                                                    op0=ALU.mult, op1=ALU.subtract))
                        done()
                        step(V.tensor_tensor(src[:, 16:16 + w - 1], src[:, 16:16 + w - 1], inv_count[:, 0:w - 1],
                                             ALU.mult))
                        done()
                        V.tensor_tensor(out_j[:, 0:w - 1], src[:, 16:16 + w - 1], z[j][:, 16:16 + w - 1],
                                        ALU.subtract).then_inc(pooled_ready, 1)
                        dve.wait_ge(pooled_ready, 2 * i + j + 1)
                if n > P0 + 1:
                    mix_lo(dve, V, n - P0 - 2)
            mix_lo(dve, V, 2)
            mix_lo(dve, V, 3)
            dve.wait_ge(mix_mm, NH)
            dve.wait_ge(bb_in, 16)
            def merged_lo(k):
                dve.wait_ge(m_hi, k + 1)
                V.tensor_tensor(hT[:, 1, k, :], merged[:, k, :], hT[:, 0, k, :].bitcast(F32),
                                ALU.subtract).then_inc(m_lo, 1)

            def gate_round(q, last=False):
                def lo_next(j):
                    dve.wait_ge(hi_ready, q * 4 + (G0 + j + 2))
                    lo((j + 1) % 2, (j + 1) % 4)

                def ada_next(j):
                    dve.wait_ge(landed[j], (q * 2 + (RAW_G // 4 + 2)) * 16)
                    ada(macc_b[:, ds(q * (4 * CC) + j * CC, CC)], j, q * 4 + j)

                lo_next(0)
                ada_next(0)
                lo_next(1)
                dve.wait_ge(chunk_used, q * 4 + (G0 + 2))
                dve.wait_ge(gate_ready, q * 4 + 2)
                for b in range(2):
                    V.tensor_tensor(merged[:, ds(q * 2 + b, 1), :].rearrange("p a n -> p (a n)"), ps[:, 2 + b, :],
                                    sig_a[:, b, :], ALU.mult).then_inc(merge_a, 1)
                ada_next(1)
                lo_next(2)
                ada_next(2)
                ada_next(3)
                lo_next(3)
                if last:
                    for k in range(ND - 2):
                        merged_lo(k)
                dve.wait_ge(chunk_used, q * 4 + (G0 + 4))
                dve.wait_ge(gate_ready, q * 4 + 4)
                for b in range(2):
                    V.tensor_tensor(ps[:, 6 + b, :], ps[:, 6 + b, :], sig_b[:, b, :], ALU.mult).then_inc(merge_t, 1)
                for b in range(2):
                    dve.wait_ge(merge_t, q * 2 + (b + 1))
                    dve.wait_ge(merge_a, q * 2 + 2)
                    m_t = merged[:, ds(q * 2 + b, 1), :].rearrange("p a n -> p (a n)")
                    V.tensor_tensor(m_t, ps[:, 6 + b, :], m_t, ALU.add).then_inc(merge_b, 1)

            with dve.Fori(0, 3) as q:
                gate_round(q)
            gate_round(3, last=True)
            for k in range(ND - 2, ND):
                merged_lo(k)
            dve.wait_ge(lo_ready, O0 + 1)
            for b in range(4):
                dve.wait_ge(row_mm, b + 1)
                dst = gm if b < 2 else shf
                V.tensor_copy(dst[:, (b % 2) * 512:(b % 2) * 512 + 512], ps[:, b, :]).then_inc(row_ready, 1)
            lo_n(O0 + 1, 1)
            dve.wait_ge(gff_in, 16)
            for b in range(4):
                dve.wait_ge(row_mm, b + 5)
                c = slice((b % 2) * 512, (b % 2) * 512 + 512)
                if b < 2:
                    ins = V.scalar_tensor_tensor(out=gff[:, c], in0=ps[:, b, :], scalar=1.0, in1=gff[:, c],
                                                 op0=ALU.add, op1=ALU.mult)
                else:
                    ins = V.tensor_copy(gf[:, c], ps[:, b, :])
                ins.then_inc(row_ready, 1)
            lo_n(O0 + 2, 2)
            dve.wait_ge(x_again, 16)
            dve.wait_ge(row_ready, 8)

            def residual(t, half):
                b = 4 - 4 * half + t
                step(V.tensor_tensor(ps[:, b, :], ps[:, b, :], gm[:, half * 512:half * 512 + 512], ALU.mult))
                done()
                x_h = x_tiles[:, t, half * 512:half * 512 + 512]
                V.tensor_tensor(x_h, ps[:, b, :], x_h, ALU.add).then_inc(x2_half, 1)

            def normed(t):
                dve.wait_ge(sq2, t + 1)
                inv_rms_1(24 + t)
                V.scalar_tensor_tensor(out=hf[:, t, :], in0=x_tiles[:, t, :], scalar=stats[:, 24 + t:25 + t],
                                       in1=gff, op0=ALU.mult, op1=ALU.mult).then_inc(hf_scaled, 1)

            lo_n(O0 + 3, 3)
            def mixed(t, half):
                if t < NT - 1:
                    dve.wait_ge(o_tile, 2 * t + half + 1)
                else:
                    dve.wait_ge(chunk_used, M0 - 1 + half)
                residual(t, half)

            mixed(0, 0)
            mixed(0, 1)
            normed(0)
            mixed(1, 0)
            for t in range(1, NT):
                mixed(t, 1)
                if t < NT - 1:
                    mixed(t + 1, 0)
                normed(t)
            dve.wait_ge(hf_scaled, NT)
            dve.wait_ge(hf_ready, NT - 1)
            V.tensor_tensor(hf[:, NT - 1, :], hf[:, NT - 1, :], shf, ALU.add).then_inc(hf_ready, 1)
            dve.wait_ge(consts, 2)
            step(V.tensor_scalar(r_4c, tok_f[:, :], 2.0, 1.0 - SKIP, ALU.mult, ALU.add))
            step(V.tensor_scalar(info[:, :, :, 0], tok_f[:, :].unsqueeze(2).broadcast_to([P, NT, E]), float(-SKIP), None,
                                 ALU.add))
            step(V.memset(r_m_all[:, NT * E:], 0.0))

            lg = ps[:, 4, 0:NT * E].rearrange("p (t e) -> p t e", t=NT)
            te = [P, NT, E]
            dve.wait_ge(logits_mm, NT)
            step(V.tensor_reduce(r_4, lg, AX_X, ALU.max))
            done()
            V.tensor_tensor(r_d3, lg, r_4.unsqueeze(2).broadcast_to(te), ALU.subtract).then_inc(sub_ready, 1)
            dve.wait_ge(expd, 1)
            step(V.tensor_reduce(r_4, r_p3, AX_X, ALU.add))
            done()
            step(V.reciprocal(r_4, r_4))
            done()
            step(V.tensor_tensor(r_p3, r_p3, r_4.unsqueeze(2).broadcast_to(te), ALU.mult))
            done()
            dve.wait_ge(bias_in, 16)
            step(V.tensor_tensor(r_sel3, r_p3, bias_row[:, :].unsqueeze(1).broadcast_to(te), ALU.add))
            done()

            def rank(values, n, result):
                pair = [P, n, EG, EG]
                mine = values.unsqueeze(3).broadcast_to(pair)
                other = values.unsqueeze(2).broadcast_to(pair)
                step(V.tensor_tensor(r_ge[:, 0:n], other, mine, ALU.is_ge))
                step(V.tensor_tensor(r_gt[:, 0:n], other, mine, ALU.is_gt))
                done()
                step(V.tensor_tensor(r_ge[:, 0:n], r_ge[:, 0:n],
                                     order[:, 0, :, :].unsqueeze(1).broadcast_to(pair), ALU.mult))
                step(V.tensor_tensor(r_gt[:, 0:n], r_gt[:, 0:n],
                                     order[:, 1, :, :].unsqueeze(1).broadcast_to(pair), ALU.mult))
                done()
                step(V.tensor_tensor(r_ge[:, 0:n], r_ge[:, 0:n], r_gt[:, 0:n], ALU.add))
                done()
                step(V.tensor_reduce(result, r_ge[:, 0:n], AX_X, ALU.add))
                done()

            ge3 = [P, NT * EG, EG]
            sel_g = r_sel.rearrange("p (g e) -> p g e", e=EG)
            top_g = r_top.rearrange("p (g e) -> p g e", e=EG)
            rank(sel_g, NT * EG, top_g)
            step(V.tensor_scalar(r_top, r_top, 2.0, None, ALU.is_lt))
            done()
            step(V.tensor_tensor(r_m, r_sel, r_top, ALU.mult))
            done()
            step(V.tensor_reduce(r_gs, r_m.rearrange("p (g e) -> p g e", e=EG), AX_X, ALU.add))
            done()
            rank(r_gs.rearrange("p (t g) -> p t g", t=NT), NT, r_gr.rearrange("p (t g) -> p t g", t=NT))
            step(V.tensor_scalar(r_gr, r_gr, 1.0, None, ALU.is_lt))
            done()
            V.tensor_tensor(r_m.rearrange("p (g e) -> p g e", e=EG), top_g,
                            r_gr.unsqueeze(2).broadcast_to(ge3), ALU.mult).then_inc(mask_ready, 1)
            dve.wait_ge(mask_ready, 1)
            step(V.tensor_tensor(r_p, r_p, r_m, ALU.mult))
            step(V.tensor_tensor(r_d3, r_m3, iota1[:, 0:E].unsqueeze(1).broadcast_to(te), ALU.mult))
            done()
            step(V.tensor_reduce(r_4, r_p3, AX_X, ALU.add))
            step(V.tensor_reduce(r_4b, r_d3, AX_X, ALU.max))
            done()
            step(V.reciprocal(r_4, r_4))
            step(V.tensor_tensor(r_d3, r_d3, r_4b.unsqueeze(2).broadcast_to(te), ALU.is_equal))
            done()
            step(V.tensor_tensor(info[:, :, :, 1], r_p3, r_4.unsqueeze(2).broadcast_to(te), ALU.mult))
            step(V.tensor_tensor(info[:, :, :, 2], r_d3, r_4c.unsqueeze(2).broadcast_to(te), ALU.add))
            dve.wait_ge(pos_mm, 1)
            step(V.scalar_tensor_tensor(out=pos1[:, :, :], in0=ps[:, 2, 0:NT * E].rearrange("p (t e) -> p t e", t=NT),
                                        scalar=1.0, in1=r_m3, op0=ALU.add, op1=ALU.mult))
            step(V.tensor_copy(r_cnt, ps[:, 2, NT * E:NT * E + E]))
            done()

            def select(j, e):
                dve.wait_ge(idx_mm, j)
                for t in range(NT):
                    ins = V.tensor_scalar(sel[:, t, :], iota1[:, :], base[:, ds(j, 1)], pos1[:, t, ds(e, 1)],
                                          ALU.add, ALU.is_equal)
                ins.then_inc(sel_ready, 1)

            def indices(j):
                dve.wait_ge(idx_mm, j + 1)
                dve.wait_ge(gathered, j * 16)
                V.tensor_scalar(tok_idx[:, :], ps[:, 7, 0:1], float(SKIP), None, ALU.add)
                V.tensor_copy(row_w[:, ds(j, 1)], ps[:, 7, 1:2])
                V.tensor_scalar(row_dest[:, ds(j, 1)], ps[:, 7, 2:3], float(SKIP), None,
                                ALU.add).then_inc(idx_ready, 1)

            def rows_lo(j):
                dve.wait_ge(hg_hi, j + 1)
                V.tensor_tensor(hgT[:, 1, :, :].rearrange("p k m -> p (k m)"),
                                ps[:, 2:4, :].rearrange("p b n -> p (b n)"),
                                hgT[:, 0, :, :].rearrange("p k m -> p (k m)").bitcast(F32),
                                ALU.subtract).then_inc(hg_lo, 1)

            select(0, 0)
            step(V.tensor_scalar(r_x, r_cnt, float(P), None, ALU.is_gt))
            step(V.tensor_scalar(r_x2, r_cnt, float(2 * P), None, ALU.is_gt))
            step(V.tensor_scalar(r_x3, r_cnt, float(3 * P), None, ALU.is_gt))
            done()
            indices(0)
            select(1, 1)
            step(V.tensor_tensor(r_x, r_x, r_x2, ALU.add))
            step(V.tensor_scalar(r_x3, r_x3, 1.0, None, ALU.add))
            done()
            step(V.tensor_tensor(r_x2, r_x, r_x3, ALU.add))
            done()
            step(V.tensor_scalar(r_extra, r_x2[:, 0:1], -1.0 - E, None, ALU.add))
            done()
            step(V.memset(r_x2[:, 0:1], 1.0))
            done()
            step(V.tensor_tensor_scan(r_cum, ones[:, 0:E], r_x2, 0.0, ALU.mult, ALU.add))
            done()
            ie = [P, TILES_MAX, E]
            lo_n(M0 + 2, 4)
            step(V.tensor_tensor(r_le, iota1[:, 0:TILES_MAX].unsqueeze(2).broadcast_to(ie),
                                 r_cum.unsqueeze(1).broadcast_to(ie), ALU.is_gt))
            done()
            step(V.tensor_reduce(r_n, r_le, AX_X, ALU.add))
            done()
            step(V.tensor_tensor(r_le, r_le, r_cum.unsqueeze(1).broadcast_to(ie), ALU.mult))
            done()
            indices(1)
            rows_lo(0)
            step(V.tensor_reduce(r_first, r_le, AX_X, ALU.max))
            step(V.tensor_scalar(r_wrap, r_n, float(E), None, ALU.is_ge))
            step(V.tensor_scalar(r_i, iota1[:, 0:TILES_MAX], -1.0, None, ALU.add))
            step(V.tensor_tensor(r_extra, r_extra, r_cum[:, E - 1:E], ALU.add))
            done()
            step(V.tensor_tensor(r_i, r_i, r_wrap, ALU.add))
            step(V.scalar_tensor_tensor(out=r_n, in0=r_wrap, scalar=-float(E), in1=r_n, op0=ALU.mult, op1=ALU.add))
            done()
            step(V.tensor_tensor(r_i, r_i, r_first, ALU.subtract))
            step(V.tensor_copy(expert_of[:, 0:TILES_MAX], r_n))
            step(V.tensor_tensor(weights_of[:, 1, 1:TILES_MAX], r_n[:, 1:TILES_MAX], r_n[:, 0:TILES_MAX - 1],
                                 ALU.is_equal))
            step(V.tensor_tensor(weights_of[:, 0, 1:TILES_MAX], r_n[:, 1:TILES_MAX], r_n[:, 0:TILES_MAX - 1],
                                 ALU.not_equal))
            done()
            step(V.tensor_scalar(base[:, 2:TILES_MAX], r_i[:, 2:TILES_MAX], float(P), None, ALU.mult))
            V.tensor_copy(expert_of[:, 31:32], r_extra).then_inc(tiles_ready, 1)
            dve.wait_ge(tiles_ready, 1)
            lo_n(M0 + 3, 5)

            def hidden(i, up_used):
                dve.wait_ge(silu_ready, i + 1)
                dve.wait_ge(chunk_used, up_used)
                dve.wait_ge(a_trans, i)
                V.tensor_tensor(a_t, ps[:, 1, :], act_g, ALU.mult).then_inc(a_ready, 1)

            def a_lo(i):
                dve.wait_ge(aT_hi, i + 1)
                V.tensor_tensor(aT[:, 1, :, :].rearrange("p k m -> p (k m)"), ps[:, 4, :],
                                aT[:, 0, :, :].rearrange("p k m -> p (k m)").bitcast(F32),
                                ALU.subtract).then_inc(aT_lo, 1)

            def destination(j):
                dve.wait_ge(idx_ready, j + 1)
                dve.wait_ge(scattered, j * 16)
                V.tensor_copy(dest_now[:, :], row_dest[:, ds(j, 1)]).then_inc(dest_ready, 1)

            def results(j, used, bank=5):
                dve.wait_ge(chunk_used, used)
                dve.wait_ge(idx_ready, j + 1)
                dve.wait_ge(scattered, j * 16)
                V.scalar_tensor_tensor(out=y, in0=ps[:, bank:bank + 2, :].rearrange("p b n -> p (b n)"),
                                       scalar=row_w[:, ds(j, 1)], in1=gf, op0=ALU.mult,
                                       op1=ALU.mult).then_inc(y_ready, 1)

            def tile(i, e2, up_used, prev, down_used=None):
                def lo_c(c):
                    dve.wait_ge(hi_ready, i * 6 + (37 + c))
                    lo(c, c)

                select(i + 2, e2)
                lo_c(0)
                lo_c(1)
                lo_c(2)
                hidden(i, up_used)
                indices(i + 2)
                lo_c(3)
                rows_lo(i + 1)
                lo_c(4)
                lo_c(5)
                if prev:
                    destination(i - 1)
                a_lo(i)
                if prev:
                    results(i - 1, down_used)

            def expert_ahead(i):
                return dve.value_load(expert_of[0:1, ds(i + 2, 1)], min_val=0, max_val=E - 1)

            tile(0, expert_ahead(0), M0 + 4, False)
            tile(1, expert_ahead(1), 6 + 34, True, 6 + 36)
            tiles = dve.value_load(expert_of[0:1, 31:32], min_val=0, max_val=7) + E
            with dve.Fori(2, tiles - 1) as i:
                tile(i, expert_ahead(i), i * 6 + 34, True, i * 6 + 36)
            hidden(tiles - 1, tiles * 6 + 28)
            for c in range(2):
                dve.wait_ge(hi_ready, tiles * 6 + (31 + c))
                lo(c, c)
            destination(tiles - 2)
            a_lo(tiles - 1)
            results(tiles - 2, tiles * 6 + 30)
            destination(tiles - 1)
            results(tiles - 1, tiles * 6 + 32, LAST_BANK)
            for t in range(NT):
                if t == 0:
                    dve.wait_ge(y_in[0], 16)
                    step(V.tensor_tensor(raw[:, 0, 0:D], raw[:, 0, 0:D], raw[:, 0, D:2 * D], ALU.add))
                    done()
                else:
                    dve.wait_ge(y_sum, t)
                V.tensor_tensor(x_tiles[:, t, :], x_tiles[:, t, :], raw[:, t, 0:D], ALU.add).then_inc(fin_x, 1)
                if t == 2:
                    dve.wait_ge(fin_sq, 2)
                    inv_rms_1(29)
                    V.tensor_copy(fin_rms[:, :], stats[:, 29:30]).then_inc(fin_rms_ready, 1)
                elif t:
                    final(dve, V, inv_rms_1, t - 1)
            final(dve, V, inv_rms_1, NT - 1)

        @block.tensor
        def _(pe):
            def three(out, w_hi, w_lo, m_hi_, m_lo_, first, last):
                nc.tensor.matmul(out, w_hi, m_hi_, start=first, stop=False)
                nc.tensor.matmul(out, w_hi, m_lo_, start=False, stop=False)
                return nc.tensor.matmul(out, w_lo, m_hi_, start=False, stop=last)

            pe.wait_ge(consts, 1)
            pe.wait_ge(rows_in, 80)
            nc.tensor.transpose(ps[:, 7, 32:80], rows_c, ident[0:48, 0:48]).then_inc(cols_t, 1)

            def mod_row_products(i):
                r = 2 * i + 1
                pe.wait_ge(landed[r % RING_A], 16 * (r // RING_A + 1))
                if i == 0:
                    pe.wait_ge(c_ready, 1)
                    pe.wait_ge(cols_ready, 1)
                else:
                    pe.wait_ge(mod_row_ready, i)
                for k in range(ND):
                    mm = nc.tensor.matmul(ps[0:1, 7, CC:2 * CC], c_silu[:, k:k + 1],
                                          raw[:, r % RING_A, k * CC:(k + 1) * CC], start=(k == 0), stop=(k == ND - 1))
                mm.then_inc(mod_used, 1)

            def mod_columns(i):
                pe.wait_ge(ada_used, i + 1)
                pe.wait_ge(mod_row_ready, i + 1)
                for m in range(2):
                    nc.tensor.matmul(ps[:, 7, 4 * i + m:4 * i + m + 1],
                                     macc_a[:, i * CC + m * P:i * CC + (m + 1) * P], ones[:, 0:1],
                                     start=True, stop=True)
                for m in range(2):
                    mm = nc.tensor.matmul(ps[:, 7, 4 * i + 2 + m:4 * i + 3 + m], mod_row[:, m * P:(m + 1) * P],
                                          ones[0:1, 0:1], start=True, stop=True)
                mm.then_inc(mod_mm, 1)

            def x_turn(k):
                for t in range(NT):
                    mm = nc.tensor.transpose(ps[:, k, t * P:(t + 1) * P], x_tiles[:, t, k * P:(k + 1) * P],
                                             ident[:, :])
                mm.then_inc(xT_t, 1)

            mod_row_products(0)
            mod_columns(0)
            mod_row_products(1)
            pe.wait_ge(causal, 1)
            for h in range(NH):
                mm = nc.tensor.transpose(ps[:, 5 + h // 4, (h % 4) * P:(h % 4 + 1) * P], wnat[:, h * P:(h + 1) * P],
                                         ident[:, :])
            mm.then_inc(ws_t, 1)
            pe.wait_ge(xhat_ready, NT)
            for k in range(5):
                x_turn(k)
            mod_columns(1)
            mod_row_products(2)
            pe.wait_ge(ws_ready, 1)
            x_turn(5)
            x_turn(6)
            mod_columns(2)
            mod_row_products(3)
            mod_columns(3)
            pe.wait_ge(gain_ready, 1)
            x_turn(7)

            def wblock(s, part, k, width):
                return wsplit[:, s, part, k * width:(k + 1) * width]

            def by_token(n, stationary, bank):
                s, kh = split_slot(n), n % 2
                for t in range(NT):
                    for k in range(4):
                        kk = 4 * kh + k
                        if n == V0 and t == 0:
                            pe.wait_ge(h_lo, k + 1)
                        mm = three(ps[:, bank + t, :],
                                   stationary[:, 0, kk, t * P:(t + 1) * P], stationary[:, 1, kk, t * P:(t + 1) * P],
                                   wblock(s, 0, k, 512), wblock(s, 1, k, 512), kk == 0, kk == ND - 1)
                mm.then_inc(chunk_used, 1)

            def by_feature(s, moving, bank):
                for m in range(2):
                    for k in range(ND):
                        col = k * CC + m * P
                        w_hi, w_lo = wsplit[:, s, 0, col:col + P], wsplit[:, s, 1, col:col + P]
                        mm = three(ps[:, bank + m, :], w_hi, w_lo, moving[:, 0, k, :], moving[:, 1, k, :],
                                   k == 0, k == ND - 1)
                mm.then_inc(chunk_used, 1)

            for n in range(V0, U0):
                pe.wait_ge(lo_ready, n + 1)
                if n:
                    pe.wait_ge(h_lo, ND)
                by_token(n, hT, 4 * (n // 2))
            for n in range(U0, P0):
                pe.wait_ge(lo_ready, n + 1)
                if n < U0 + 2:
                    pe.wait_ge(v_gelu, NT)
                else:
                    pe.wait_ge(v_gelu, 2 * NT)
                by_feature(n % 2, hT, 2 * (n - U0))
            pe.wait_ge(v_ready, NT)
            pe.wait_ge(ws_ready, 1)
            for h in range(NH):
                pe.wait_ge(u_ready, h + 1)
                for c in range(NT):
                    mm = nc.tensor.matmul(ps[:, h, c * P:(c + 1) * P], v[:, c * D + h * P:c * D + (h + 1) * P],
                                          wsT[:, h * P:(h + 1) * P], start=True, stop=True)
                mm.then_inc(s_mm, 1)

            def mix(i):
                g = 3 - i
                pe.wait_ge(pooled_ready, 2 * i + 2)
                pe.wait_ge(wpool_in, 16)
                for dj in range(2):
                    for k in range(2):
                        col = (2 * g + k) * 256 + dj * P
                        mm = nc.tensor.matmul(ps[:, 2 * i + dj, :], raw[:, 4, col:col + P], pooled[:, i % 2, k, :],
                                              start=(k == 0), stop=(k == 1))
                    mm.then_inc(mix_mm, 1)

            for n in range(P0, G0):
                pe.wait_ge(lo_ready, n + 1)
                pe.wait_ge(ya_f, 2 * (n - P0) + 2)
                s = n % 2
                by_feature(s, hT, 2 * (n - P0))
                if n > P0:
                    mix(n - P0 - 1)
            mix(3)
            pe.wait_ge(ya_lo, NH)
            with pe.Fori(0, 4) as q:
                for j in range(4):
                    pe.wait_ge(lo_ready, q * 4 + (G0 + j + 1))
                    pe.wait_ge(yb_lo, 2 * j + 2)
                    by_feature(j % 2, (hT, ya, hT, yb)[j], 2 * j)

            def row(b, bank):
                nc.tensor.matmul(ps[:, bank, :], ones[:, :], macc_b[:, b * 512:(b + 1) * 512],
                                 start=True, stop=True).then_inc(row_mm, 1)

            def out_tile(n, t):
                s, half, kh = split_slot(n), (n - O0) % 2, (n - O0) // 2
                for k in range(4):
                    kk = 4 * kh + k
                    mm = three(ps[:, 4 - 4 * half + t, :], hT[:, 0, kk, t * P:(t + 1) * P], hT[:, 1, kk, t * P:(t + 1) * P],
                               wblock(s, 0, k, 512), wblock(s, 1, k, 512), kk == 0, kk == ND - 1)
                return mm

            pe.wait_ge(ada_used, RAW_ADA // 2 + 16)
            pe.wait_ge(merge_a, ND)
            for b in range(4):
                row(b, b)
            pe.wait_ge(lo_ready, O0 + 1)
            pe.wait_ge(m_lo, 4)
            pe.wait_ge(merge_b, ND)
            for t in range(NT):
                if t == 2:
                    pe.wait_ge(row_ready, 4)
                    for b in range(4):
                        row(4 + b, b)
                mm = out_tile(O0, t)
            mm.then_inc(chunk_used, 1)
            pe.wait_ge(lo_ready, O0 + 2)
            pe.wait_ge(row_ready, 8)
            for t in range(NT):
                mm = out_tile(O0 + 1, t)
            mm.then_inc(chunk_used, 1)
            pe.wait_ge(lo_ready, O0 + 3)
            pe.wait_ge(m_lo, ND)
            for t in range(NT):
                mm = out_tile(O0 + 2, t)
                mm.then_inc(o_tile if t < NT - 1 else chunk_used, 1)
                if t == 0:
                    pe.wait_ge(lo_ready, O0 + 4)
                mm = out_tile(O0 + 3, t)
                mm.then_inc(o_tile if t < NT - 1 else chunk_used, 1)
            pe.wait_ge(router_in, 16)

            def logits(t):
                for k in range(ND):
                    if k % 4 == 0:
                        pe.wait_ge(hfT_ready, 2 * t + k // 4 + 1)
                    mm = nc.tensor.matmul(ps[:, 4, t * E:(t + 1) * E], hfT[:, t % 2, k, :], router[:, k, :],
                                          start=(k == 0), stop=(k == ND - 1))
                mm.then_inc(logits_mm, 1)

            def turn_normed(t):
                pe.wait_ge(hf_ready, t + 1)
                if t < 2:
                    pe.wait_ge(x2_half, 2 * t + 4)
                else:
                    pe.wait_ge(hfT_ready, 2 * t - 2)
                for k in range(ND):
                    mm = nc.tensor.transpose(ps[:, 5 * (t % 2) + k // 4, (k % 4) * P:(k % 4 + 1) * P],
                                             hf[:, t, k * P:(k + 1) * P], ident[:, :])
                    if k % 4 == 3:
                        mm.then_inc(hf_t, 1)

            turn_normed(0)
            turn_normed(1)
            logits(0)
            logits(1)
            for t in range(2, NT):
                turn_normed(t)
                logits(t)
            pe.wait_ge(mask_ready, 1)
            nc.tensor.matmul(ps[:, 2, 0:(NT + 1) * E], before[:, :], r_m_all, start=True, stop=False)
            for t in range(1, NT + 1):
                mm = nc.tensor.matmul(ps[:, 2, t * E:(NT + 1) * E], ones[:, :], r_m_all[:, 0:(NT + 1 - t) * E],
                                      start=False, stop=(t == NT))
            mm.then_inc(pos_mm, 1)

            def index(j, e):
                pe.wait_ge(sel_ready, j + 1)
                pe.wait_ge(idx_ready, j)
                for t in range(NT):
                    mm = nc.tensor.matmul(ps[:, 7, 0:3], sel[:, t, :],
                                          info[:, t, ds(e, 1), :].rearrange("p a n -> p (a n)"),
                                          start=(t == 0), stop=(t == NT - 1))
                mm.then_inc(idx_mm, 1)

            def turn(j):
                pe.wait_ge(gathered, j * 16 + 16)
                pe.wait_ge(hg_lo, j)
                for k in range(ND):
                    mm = nc.tensor.transpose(ps[:, 2 + k // 4, (k % 4) * P:(k % 4 + 1) * P],
                                             hg[:, k * P:(k + 1) * P], ident[:, :])
                mm.then_inc(hg_t, 1)

            def gate_up(i, first_chunk, slot0):
                pe.wait_ge(hg_lo, i + 1)
                for c in range(4):
                    pe.wait_ge(lo_ready, first_chunk + (c + 1))
                    for k in range(4):
                        kk = 4 * (c % 2) + k
                        mm = three(ps[:, c // 2, :], hgT[:, 0, kk, :], hgT[:, 1, kk, :],
                                   wblock(slot0 + c, 0, k, 512), wblock(slot0 + c, 1, k, 512), kk == 0, kk == ND - 1)
                    mm.then_inc(chunk_used, 1)

            def down(i, first_chunk, slot0=4, bank=5, between=None):
                pe.wait_ge(aT_lo, i + 1)
                if bank == 5:
                    pe.wait_ge(y_ready, i)
                for c in range(2):
                    pe.wait_ge(lo_ready, first_chunk + (c + 1))
                    for k in range(2):
                        for half in range(2):
                            w = 2 * k + half
                            mm = three(ps[:, bank + half, :], aT[:, 0, 2 * c + k, :], aT[:, 1, 2 * c + k, :],
                                       wblock(slot0 + c, 0, w, 512), wblock(slot0 + c, 1, w, 512),
                                       c == 0 and k == 0, c == 1 and k == 1)
                    mm.then_inc(chunk_used, 1)
                    if c == 0 and between:
                        between()

            def turn_hidden(i):
                pe.wait_ge(a_ready, i + 1)
                pe.wait_ge(aT_lo, i)
                for k in range(NF):
                    mm = nc.tensor.transpose(ps[:, 4, k * P:(k + 1) * P], a_t[:, k * P:(k + 1) * P], ident[:, :])
                mm.then_inc(a_trans, 1)

            def expert_ahead(i):
                return pe.value_load(expert_of[0:1, ds(i + 2, 1)], min_val=0, max_val=E - 1)

            index(0, 0)
            index(1, 1)
            turn(0)
            gate_up(0, M0, 2)
            pe.wait_ge(tiles_ready, 1)
            index(2, expert_ahead(0))
            turn(1)
            turn_hidden(0)

            def tile(i, e2):
                gate_up(i, i * 6 + 30, 0)
                index(i + 2, e2)
                turn(i + 1)
                down(i - 1, i * 6 + 34)
                turn_hidden(i)

            tile(1, expert_ahead(1))
            tiles = pe.value_load(expert_of[0:1, 31:32], min_val=0, max_val=7) + E
            with pe.Fori(2, tiles - 1) as i:
                tile(i, expert_ahead(i))
            gate_up(tiles - 1, tiles * 6 + 24, 0)
            down(tiles - 2, tiles * 6 + 28, between=lambda: turn_hidden(tiles - 1))
            down(tiles - 1, tiles * 6 + 30, 0, LAST_BANK)


_INS = ["x", "c", "w_ada", "b_ada", "norm_mix_g", "w_in", "v_norm_g", "sgu_w", "sgu_b", "pool_w", "pool_scale",
        "w_branch_a", "w_branch_b", "w_out", "norm_ffn_g", "router_w", "router_bias",
        "w_exp_gate", "w_exp_up", "w_exp_down", "final_norm_g"]


def kernel(**inputs):
    import numpy as _np
    import concourse.bacc as _bacc
    from concourse import mybir as _mybir
    from concourse.bass_utils import run_bass_kernel_spmd as _run

    nc = _bacc.Bacc("TRN2", target_bir_lowering=False, num_devices=1)
    arrays, aps = {}, {}
    for name in _INS:
        a = _np.ascontiguousarray(inputs[name])
        arrays[f"in_{name}"] = a
        aps[name] = nc.dram_tensor(f"in_{name}", a.shape, _mybir.dt.from_np(a.dtype), kind="ExternalInput").ap()
    out = nc.dram_tensor("out_0", (1, SEQ, D), F32, kind="ExternalOutput").ap()
    tokens_moe_kernel(nc, aps, out)
    r = _run(nc, [arrays], core_ids=[0])
    return r.results[0]["out_0"]
```
